# Optimizing a Trainium2 kernel written in Bass

```python
import jax, jax.numpy as jnp
from jax import lax
import numpy as np

D_MODEL = 2048
BATCH = 1
SEQ = 512
DEPTH = 2

N_META = 16
N_MIXERS = 2
EPS = 1e-6

A_INNER = 2 * D_MODEL
A_HEADS = 8
A_HEAD_IN = A_INNER // A_HEADS
A_DV = A_HEAD_IN
A_DQK = A_HEAD_IN // 2
A_CONV = 4
A_CHUNK = 64

B_HEAD_DIM = 128
B_HEADS = D_MODEL // B_HEAD_DIM
B_INNER = B_HEADS * B_HEAD_DIM
B_QBLOCK = 128

N_A = (DEPTH + 1) // 2
N_B = DEPTH // 2

kernel_name = 'hybrid_mlstm_fox_meta'

def _rmsnorm(x, g):
    xf = x.astype(jnp.float32)
    y = xf * lax.rsqrt(jnp.mean(xf * xf, axis=-1, keepdims=True) + EPS)
    return (y * g.astype(jnp.float32)).astype(x.dtype)

def _causal_conv(x, w, b):
    y = lax.conv_general_dilated(x, w[:, None, :].astype(x.dtype), window_strides=(1,),
                                 padding=[(A_CONV - 1, 0)],
                                 dimension_numbers=('NWC', 'WIO', 'NWC'),
                                 feature_group_count=x.shape[-1])
    return y + b.astype(x.dtype)

def _mlstm_chunk(carry, inp):
    C, n, m = carry
    q, k, v, ig, lf = inp
    L = q.shape[-2]
    b = jnp.cumsum(lf, axis=-1)
    causal = jnp.tril(jnp.ones((L, L), dtype=bool))
    dmat = jnp.where(causal, b[..., :, None] - b[..., None, :] + ig[..., None, :], -jnp.inf)
    m_state = b + m[..., None]
    m_t = jnp.maximum(m_state, jnp.max(dmat, axis=-1))
    s_state = jnp.exp(m_state - m_t)
    w = jnp.exp(dmat - m_t[..., None]) * jnp.einsum('bhtd,bhsd->bhts', q, k)
    num = s_state[..., None] * jnp.einsum('bhtd,bhde->bhte', q, C) + jnp.einsum('bhts,bhse->bhte', w, v)
    den = s_state * jnp.einsum('bhtd,bhd->bht', q, n) + jnp.sum(w, axis=-1)
    h = num / jnp.maximum(jnp.abs(den), jnp.exp(-m_t))[..., None]
    g_end = b[..., -1]
    decay = g_end[..., None] - b + ig
    m_new = jnp.maximum(g_end + m, jnp.max(decay, axis=-1))
    s_old = jnp.exp(g_end + m - m_new)
    w_end = jnp.exp(decay - m_new[..., None])
    C_new = s_old[..., None, None] * C + jnp.einsum('bhs,bhsd,bhse->bhde', w_end, k, v)
    n_new = s_old[..., None] * n + jnp.einsum('bhs,bhsd->bhd', w_end, k)
    return (C_new, n_new, m_new), h

def _mlstm_mixer(xn, w_in, conv_w, conv_b, w_q, w_k, w_v, w_gate, b_gate, head_norm, skip, w_out):
    Bsz, T, _ = xn.shape
    proj = xn @ w_in
    x_m, o_pre, z = jnp.split(proj, 3, axis=-1)
    x_c = jax.nn.silu(_causal_conv(x_m, conv_w, conv_b))
    xc_h = x_c.reshape(Bsz, T, A_HEADS, A_HEAD_IN)
    xm_h = x_m.reshape(Bsz, T, A_HEADS, A_HEAD_IN)
    q = jnp.einsum('bthe,hed->bhtd', xc_h, w_q)
    k = jnp.einsum('bthe,hed->bhtd', xc_h, w_k)
    v = jnp.einsum('bthe,hed->bhtd', xm_h, w_v)
    nqk = A_HEADS * A_DQK
    gw_q = w_gate[:nqk].reshape(A_HEADS, A_DQK, 2 * A_HEADS)
    gw_k = w_gate[nqk:2 * nqk].reshape(A_HEADS, A_DQK, 2 * A_HEADS)
    gw_v = w_gate[2 * nqk:].reshape(A_HEADS, A_DV, 2 * A_HEADS)
    gates = (jnp.einsum('bhtd,hdg->btg', q, gw_q) + jnp.einsum('bhtd,hdg->btg', k, gw_k)
             + jnp.einsum('bhtd,hdg->btg', v, gw_v) + b_gate).astype(jnp.float32)
    ig = jnp.transpose(gates[..., :A_HEADS], (0, 2, 1))
    lf = jnp.transpose(jax.nn.log_sigmoid(gates[..., A_HEADS:]), (0, 2, 1))
    qf = q.astype(jnp.float32) * (A_DQK ** -0.5)
    kf = k.astype(jnp.float32)
    vf = v.astype(jnp.float32)
    carry0 = (jnp.zeros((Bsz, A_HEADS, A_DQK, A_DV), jnp.float32),
              jnp.zeros((Bsz, A_HEADS, A_DQK), jnp.float32),
              jnp.zeros((Bsz, A_HEADS), jnp.float32))
    carry, h_meta = _mlstm_chunk(carry0, (qf[:, :, :N_META], kf[:, :, :N_META], vf[:, :, :N_META],
                                          ig[:, :, :N_META], lf[:, :, :N_META]))
    nc = (T - N_META) // A_CHUNK

    def to_chunks(a):
        r = a[:, :, N_META:]
        r = r.reshape(a.shape[0], a.shape[1], nc, A_CHUNK, *a.shape[3:])
        return jnp.moveaxis(r, 2, 0)

    xs = (to_chunks(qf), to_chunks(kf), to_chunks(vf), to_chunks(ig), to_chunks(lf))
    _, h_real = lax.scan(_mlstm_chunk, carry, xs)
    h_real = jnp.moveaxis(h_real, 0, 2).reshape(Bsz, A_HEADS, T - N_META, A_DV)
    h = jnp.concatenate([h_meta, h_real], axis=2)
    h = jnp.transpose(h, (0, 2, 1, 3)) * jax.nn.sigmoid(o_pre.astype(jnp.float32)).reshape(Bsz, T, A_HEADS, A_DV)
    h = h * lax.rsqrt(jnp.mean(h * h, axis=-1, keepdims=True) + EPS)
    h = h.reshape(Bsz, T, A_INNER) * head_norm.astype(jnp.float32)
    y = (h + skip.astype(jnp.float32) * x_c.astype(jnp.float32)) * jax.nn.silu(z.astype(jnp.float32))
    return y.astype(xn.dtype) @ w_out

def _fox_block(qb, cq, qpos, k, v, ck, kpos):
    s = jnp.einsum('bhqd,bhkd->bhqk', qb, k).astype(jnp.float32) * (B_HEAD_DIM ** -0.5)
    s = s + (cq[..., :, None] - ck[..., None, :])
    s = jnp.where(kpos[None, :] <= qpos[:, None], s, -jnp.inf)
    p = jax.nn.softmax(s, axis=-1)
    return jnp.einsum('bhqk,bhkd->bhqd', p.astype(v.dtype), v)

def _fox_mixer(xn, w_in, b_f, q_norm, k_norm, w_out):
    Bsz, T, _ = xn.shape
    proj = xn @ w_in
    q, k, v, f_pre, z = jnp.split(proj, [B_INNER, 2 * B_INNER, 3 * B_INNER, 3 * B_INNER + B_HEADS], axis=-1)

    def heads(a):
        return jnp.transpose(a.reshape(Bsz, T, B_HEADS, B_HEAD_DIM), (0, 2, 1, 3))

    q = _rmsnorm(heads(q), q_norm)
    k = _rmsnorm(heads(k), k_norm)
    v = heads(v)
    logf = jnp.transpose(jax.nn.log_sigmoid((f_pre + b_f).astype(jnp.float32)), (0, 2, 1))
    c = jnp.cumsum(logf, axis=-1)
    kpos = jnp.arange(T)
    meta_pos = jnp.arange(N_META)
    o_meta = _fox_block(q[:, :, :N_META], c[:, :, :N_META], meta_pos,
                        k[:, :, :N_META], v[:, :, :N_META], c[:, :, :N_META], meta_pos)
    nb = (T - N_META) // B_QBLOCK
    q_r = jnp.moveaxis(q[:, :, N_META:].reshape(Bsz, B_HEADS, nb, B_QBLOCK, B_HEAD_DIM), 2, 0)
    c_r = jnp.moveaxis(c[:, :, N_META:].reshape(Bsz, B_HEADS, nb, B_QBLOCK), 2, 0)
    pos_r = (N_META + jnp.arange(T - N_META)).reshape(nb, B_QBLOCK)
    o_r = lax.map(lambda blk: _fox_block(blk[0], blk[1], blk[2], k, v, c, kpos), (q_r, c_r, pos_r))
    o_r = jnp.moveaxis(o_r, 0, 2).reshape(Bsz, B_HEADS, T - N_META, B_HEAD_DIM)
    o = jnp.concatenate([o_meta, o_r], axis=2)
    o = jnp.transpose(o, (0, 2, 1, 3)).reshape(Bsz, T, B_INNER)
    y = o.astype(jnp.float32) * jax.nn.silu(z.astype(jnp.float32))
    return y.astype(xn.dtype) @ w_out

def setup_inputs(seed: int = 0) -> dict:
    key = jax.random.key(seed)
    ks = jax.random.split(key, 24)
    nrm = jax.random.normal
    f32 = jnp.float32
    x = nrm(ks[0], (BATCH, SEQ, D_MODEL), f32)
    meta_tokens = nrm(ks[1], (N_META, D_MODEL), f32)
    a_norm = 1.0 + 0.02 * nrm(ks[2], (N_A, D_MODEL), f32)
    a_w_in = nrm(ks[3], (N_A, D_MODEL, 3 * A_INNER), f32) * D_MODEL ** -0.5
    a_conv_w = nrm(ks[4], (N_A, A_CONV, A_INNER), f32) * A_CONV ** -0.5
    a_conv_b = 0.02 * nrm(ks[5], (N_A, A_INNER), f32)
    a_w_q = nrm(ks[6], (N_A, A_HEADS, A_HEAD_IN, A_DQK), f32) * A_HEAD_IN ** -0.5
    a_w_k = nrm(ks[7], (N_A, A_HEADS, A_HEAD_IN, A_DQK), f32) * A_HEAD_IN ** -0.5
    a_w_v = nrm(ks[8], (N_A, A_HEADS, A_HEAD_IN, A_DV), f32) * A_HEAD_IN ** -0.5
    gate_in = 2 * A_HEADS * A_DQK + A_HEADS * A_DV
    a_w_gate = nrm(ks[9], (N_A, gate_in, 2 * A_HEADS), f32) * gate_in ** -0.5
    b_in = 0.1 * nrm(ks[10], (N_A, A_HEADS), f32)
    b_fg = jnp.linspace(3.0, 6.0, A_HEADS, dtype=f32)[None, :] + 0.1 * nrm(ks[11], (N_A, A_HEADS), f32)
    a_b_gate = jnp.concatenate([b_in, b_fg], axis=-1)
    a_head_norm = 1.0 + 0.02 * nrm(ks[12], (N_A, A_INNER), f32)
    a_skip = 1.0 + 0.02 * nrm(ks[13], (N_A, A_INNER), f32)
    a_w_out = nrm(ks[14], (N_A, A_INNER, D_MODEL), f32) * A_INNER ** -0.5
    b_norm = 1.0 + 0.02 * nrm(ks[15], (N_B, D_MODEL), f32)
    b_w_in = nrm(ks[16], (N_B, D_MODEL, 4 * B_INNER + B_HEADS), f32) * D_MODEL ** -0.5
    b_b_f = 3.0 + 0.5 * nrm(ks[17], (N_B, B_HEADS), f32)
    b_q_norm = 1.0 + 0.02 * nrm(ks[18], (N_B, B_HEAD_DIM), f32)
    b_k_norm = 1.0 + 0.02 * nrm(ks[19], (N_B, B_HEAD_DIM), f32)
    b_w_out = nrm(ks[20], (N_B, B_INNER, D_MODEL), f32) * B_INNER ** -0.5
    final_norm = 1.0 + 0.02 * nrm(ks[21], (D_MODEL,), f32)
    return {'x': x, 'meta_tokens': meta_tokens,
            'a_norm': a_norm, 'a_w_in': a_w_in, 'a_conv_w': a_conv_w, 'a_conv_b': a_conv_b,
            'a_w_q': a_w_q, 'a_w_k': a_w_k, 'a_w_v': a_w_v, 'a_w_gate': a_w_gate, 'a_b_gate': a_b_gate,
            'a_head_norm': a_head_norm, 'a_skip': a_skip, 'a_w_out': a_w_out,
            'b_norm': b_norm, 'b_w_in': b_w_in, 'b_b_f': b_b_f, 'b_q_norm': b_q_norm,
            'b_k_norm': b_k_norm, 'b_w_out': b_w_out, 'final_norm': final_norm}

def reference(x, meta_tokens, a_norm, a_w_in, a_conv_w, a_conv_b, a_w_q, a_w_k, a_w_v, a_w_gate,
              a_b_gate, a_head_norm, a_skip, a_w_out, b_norm, b_w_in, b_b_f, b_q_norm, b_k_norm,
              b_w_out, final_norm):
    Bsz = x.shape[0]
    meta = jnp.broadcast_to(meta_tokens[None].astype(x.dtype), (Bsz, N_META, D_MODEL))
    h = jnp.concatenate([meta, x], axis=1)
    for i in range(DEPTH):
        j = i // N_MIXERS
        if i % N_MIXERS == 0:
            h = h + _mlstm_mixer(_rmsnorm(h, a_norm[j]), a_w_in[j], a_conv_w[j], a_conv_b[j],
                                 a_w_q[j], a_w_k[j], a_w_v[j], a_w_gate[j], a_b_gate[j],
                                 a_head_norm[j], a_skip[j], a_w_out[j])
        else:
            h = h + _fox_mixer(_rmsnorm(h, b_norm[j]), b_w_in[j], b_b_f[j], b_q_norm[j],
                               b_k_norm[j], b_w_out[j])
    return _rmsnorm(h, final_norm)[:, N_META:]


_drawn_inputs = setup_inputs


def setup_inputs(seed=0):
    import zlib

    import numpy as np

    out = dict(_drawn_inputs(seed))
    spreads = {}
    factors = {'a_conv_b': 3.274,
     'a_head_norm': 5.773,
     'a_skip': 8.0,
     'b_norm': 8.0,
     'b_q_norm': 8.0,
     'b_k_norm': 8.0,
     'final_norm': 2.764}
    for name, (base, spread) in spreads.items():
        noise = np.random.default_rng([zlib.crc32(name.encode()), seed]).standard_normal(out[name].shape)
        drawn = base * np.exp(spread * noise) if base else spread * noise
        out[name] = __import__('jax').numpy.asarray(drawn.astype(out[name].dtype))
    for name, factor in factors.items():
        out[name] = (out[name] * factor).astype(out[name].dtype)
    return out
```

```python
from contextlib import ExitStack

import concourse.bass as bass
from concourse import mybir

F32 = mybir.dt.float32
F32R = mybir.dt.float32r
ALU = mybir.AluOpType
ACT = mybir.ActivationFunctionType
AX_X = mybir.AxisListType.X
ds = bass.ds

P = 128
BANK = 512


def hybrid_trunk(nc, x, meta_tokens, a_norm, a_w_in, a_conv_w, a_conv_b, a_w_q, a_w_k, a_w_v,
                 a_w_gate, a_b_gate, a_head_norm, a_skip, a_w_out, b_norm, b_w_in, b_b_f,
                 b_q_norm, b_k_norm, b_w_out, final_norm, out):
    _, SEQ, D = x.shape
    META = meta_tokens.shape[0]
    T = META + SEQ
    HT = T // 2
    HS = SEQ // 2
    KT = D // P
    AI = a_w_in.shape[2] // 3
    AH, DV, DQK = a_w_q.shape[1], a_w_q.shape[2], a_w_q.shape[3]
    CT = DV // P
    QT = DQK // P
    NG = a_w_gate.shape[2]
    BH, BD = b_b_f.shape[1], b_q_norm.shape[1]
    TAPS = a_conv_w.shape[1]
    EPS = 1e-6
    S_TILES = [(0, META)] + [(META + P * i, P) for i in range(SEQ // P)]
    NS = len(S_TILES)
    NT = SEQ // P
    E_OFF = [sum(T - s for s, _ in S_TILES[:j]) for j in range(NS + 1)]
    assert (T, KT, CT, QT, BD, NG) == (528, 16, 4, 2, P, 2 * AH) and AI == AH * DV

    A1_PER, A2_PER, B1_PER = CT + 2, 2 * CT, 4
    A2_0 = AH * A1_PER
    A3_0 = A2_0 + AH * A2_PER
    B1_0 = A3_0 + 2 * KT
    B2_0 = B1_0 + 1 + BH * B1_PER
    BLOCKS = B2_0 + KT

    def xm_block(h, c):
        if isinstance(h, int) and h == 0:
            return c
        return CT + A1_PER * (h - 1) + (0 if c == 0 else 2 + c)

    def qkv_block(h):
        return A2_0 - 2 if isinstance(h, int) and h == AH - 1 else CT + A1_PER * h + 1

    FT = AI // P
    C_CW, C_CB = 0, TAPS * FT
    C_HN, C_SK = C_CB + FT, C_CB + 2 * FT
    C_AN = C_SK + FT
    C_BN = C_AN + KT
    C_FN = C_BN + KT
    C_QN, C_KN = C_FN + KT, C_FN + KT + 1
    NPAR = C_KN + 1

    with ExitStack() as ctx:
        def sb(name, shape, dt=F32, scope=ctx):
            return scope.enter_context(nc.sbuf_tensor(name, shape, dt))

        def sem(name):
            return ctx.enter_context(nc.semaphore(name))

        def dram(name, shape):
            return nc.dram_tensor(name, shape, F32).ap()

        h_d = dram("h_scratch", [P, KT * T])
        qk_d = dram("qk_scratch", [AH, P, 2 * QT * T])
        v_d = dram("v_scratch", [AH, P, NS * DV])
        xc_d = dram("xc_scratch", [P, FT * T])
        y_d = dram("y_scratch", [P, FT * T])
        negm_d = dram("negm_scratch", [AH, T])
        floor_d = dram("floor_scratch", [AH, T])
        negc_d = dram("negc_scratch", [BH, T])

        XH = sb("xh", [P, KT, T], F32R)
        XL = sb("xl", [P, KT, T], F32R)
        w_raw = [sb(f"w_raw{i}", [P, KT * P]) for i in range(2)]
        w_hi = [sb(f"w_hi{i}", [P, KT * P], F32R) for i in range(2)]
        w_lo = [sb(f"w_lo{i}", [P, KT * P], F32R) for i in range(2)]
        ident = sb("ident", [P, P])
        ones = sb("ones", [P, P])
        causal01 = sb("causal01", [P, P])
        par = sb("par", [P, NPAR])
        rstd = sb("rstd", [P, T])
        rtmp = sb("rtmp", [P, T])
        eps_t = sb("eps", [P, 1])
        sq = [sb(f"sq{i}", [P, T]) for i in range(2)]
        causal_add = sb("causal_add", [P, P])
        bf = sb("bf", [BH, 1])

        s0 = ExitStack()
        hT0 = sb("h0", [P, KT, T], scope=s0)
        x_nat = sb("x_nat", [P, NT, D], scope=s0)
        meta_nat = sb("meta_nat", [META, D], scope=s0)
        par_rows = sb("par_rows", [P, 3, P], scope=s0)
        xt0 = [sb(f"xt0{i}", [P, T], scope=s0) for i in range(2)]
        s0.close()
        s1 = ExitStack()
        xmh = sb("xmh", [P, CT, T], F32R, s1)
        xml = sb("xml", [P, CT, T], F32R, s1)
        xch = sb("xch", [P, CT, T], F32R, s1)
        xcl = sb("xcl", [P, CT, T], F32R, s1)
        qkv = sb("qkv", [P, 2 * QT + CT, T], scope=s1)
        vn1 = sb("vn1", [P, NS, DV], scope=s1)
        xm_pad = [sb(f"xm_pad{i}", [P, TAPS - 1 + T], scope=s1) for i in range(2)]
        conv = [sb(f"conv{i}", [P, T], scope=s1) for i in range(2)]
        xc2 = [sb(f"xc2{i}", [P, T], scope=s1) for i in range(2)]
        th1 = sb("th1", [P, T], scope=s1)
        wg = sb("wg", [P, 2 * QT + CT, NG], scope=s1)
        gacc = sb("gacc", [NG, T], scope=s1)
        bg = sb("bg", [NG, 1], scope=s1)
        s1.close()
        s2 = ExitStack()
        qk2 = sb("qk2", [P, 2 * QT, T], scope=s2)
        v2 = sb("v2", [P, NS, DV], scope=s2)
        EW = sb("ew", [P, E_OFF[NS]], scope=s2)
        negm_b = sb("negm_b", [P, T], scope=s2)
        floor_b = sb("floor_b", [P, T], scope=s2)
        OT = sb("ot", [P, CT, T], scope=s2)
        xcl2 = sb("xc_load", [P, CT, T], scope=s2)
        G = sb("g", [P, CT, T], scope=s2)
        dn = sb("dn", [P, T], scope=s2)
        rd = sb("rd", [P, T], scope=s2)
        th2 = [sb(f"th2{i}", [P, T], scope=s2) for i in range(2)]
        mix = sb("mix", [P, T], scope=s2)
        gate2 = sb("gate2", [P, T], scope=s2)
        yb = [sb(f"yb{i}", [P, T], scope=s2) for i in range(2)]
        aT = sb("aT", [P, NS, AH], scope=s2)
        s2.close()
        s2g = ExitStack()
        gr = {n: sb(f"gr_{n}", [AH, T], scope=s2g)
              for n in ("ig", "f", "abs", "e", "lf", "B", "a", "M", "negm", "m", "floor", "one")}
        s2g.close()
        s3 = ExitStack()
        y_in = sb("y_in", [P, KT, T], scope=s3)
        hT3 = sb("h3", [P, KT, T], scope=s3)
        xt3 = [sb(f"xt3{i}", [P, T], scope=s3) for i in range(2)]
        s3.close()
        s4 = ExitStack()
        Y = sb("y", [P, BH, SEQ], scope=s4)
        QR = sb("q_raw", [P, SEQ], scope=s4)
        KR = sb("k_raw", [P, T], scope=s4)
        VT = sb("v_t", [P, T], scope=s4)
        rq = sb("rq", [P, SEQ], scope=s4)
        QH = sb("q_hat", [P, SEQ], scope=s4)
        KH = sb("k_hat", [P, T], scope=s4)
        vn4 = sb("vn4", [P, NT, BD], scope=s4)
        vm4 = sb("vm4", [META, BD], scope=s4)
        SS = [sb(f"scores{i}", [P, T], scope=s4) for i in range(2)]
        PR = sb("probs", [P, NT, T], scope=s4)
        PTr = sb("probs_t", [P, NT, SEQ], scope=s4)
        PTm = sb("probs_t_meta", [META, SEQ], scope=s4)
        negc_b = sb("negc_b", [P, T], scope=s4)
        th4 = sb("th4", [P, SEQ], scope=s4)
        s_max, s_neg, s_sum, s_inv = (sb(f"s_{n}", [P, NT], scope=s4) for n in ("max", "neg", "sum", "inv"))
        s4.close()
        s4g = ExitStack()
        fg = {n: sb(f"fg_{n}", [BH, T], scope=s4g) for n in ("f", "abs", "e", "l1", "lf", "c", "negc", "one")}
        s4g.close()
        s5 = ExitStack()
        sb("y_kept", [P, BH * SEQ], scope=s5)
        hT5 = sb("h5", [P, KT, T], scope=s5)
        o_nat = [sb(f"o_nat{i}", [P, BANK], scope=s5) for i in range(2)]
        s5.close()

        mm = [ctx.enter_context(nc.psum_tensor(f"mm{i}", [P, 2 * BANK], F32)) for i in range(2)]
        ax = [ctx.enter_context(nc.psum_tensor(f"ax{i}", [P, 2 * BANK], F32)) for i in range(2)]

        def halves(ps, n=HT, rows=P):
            return ps[0:rows, :].rearrange("p (a n) -> p a n", a=2)[:, :, 0:n]

        def two(ap):
            return ap.rearrange("p (a n) -> p a n", a=2)

        X0 = BANK - META
        SCORES_AT = ((ax[0], X0), (ax[1], 0), (ax[1], BANK), (ax[0], 0), (ax[0], BANK))

        w_raw_ready = [sem(f"w_raw_ready{i}") for i in range(2)]
        wk_raw_ready = sem("wk_raw_ready")
        w_hi_ready, w_lo_ready, blk_done = sem("w_hi_ready"), sem("w_lo_ready"), sem("blk_done")
        (x_loaded, par_loaded, const_ready, ident0, par_tr, par_ready, x_tr, h_copied, h_stored, h_loaded,
         sq_ready, sumsq_done, ln_ready, rstd_ready, xt_ready, xh_ready, xl_ready) = (sem(n) for n in (
            "x_loaded", "par_loaded", "const_ready", "ident0", "par_tr", "par_ready", "x_tr", "h_copied",
            "h_stored", "h_loaded", "sq_ready", "sumsq_done", "ln_ready", "rstd_ready", "xt_ready",
            "xh_ready", "xl_ready"))
        (pad_zero, xm_raw, xm_hi, cv_aff, xm_lo, taps, th1_ready, xc2_ready, xc_hi, xc_lo, qkv_mm, qkv_ev,
         gate_mm, gacc_ready, wg_loaded, v_tr, vn1_ev, qk_stored, v_stored) = (sem(n) for n in (
            "pad_zero", "xm_raw", "xm_hi", "cv_aff", "xm_lo", "taps", "th1_ready", "xc2_ready", "xc_hi",
            "xc_lo", "qkv_mm", "qkv_ev", "gate_mm", "gacc_ready", "wg_loaded", "v_tr", "vn1_ev",
            "qk_stored", "v_stored"))
        xc_stored = [sem(f"xc_stored{i}") for i in range(2)]
        (gb_ready, gsel_done, grow, gexp, a_tr, aT_ready, grow_stored, qk_loaded, v_loaded, negm_loaded,
         floor_loaded, xc_loaded, e_arg, e_ready, e_diag, sc_done, w_ready, ot_ready, pv_done, dn_ready,
         rd_ready, g_ready, sqg_ready, sumg_done, th2_ready, mix_ready, gate2_ready, y_ready) = (
            sem(n) for n in (
            "gb_ready", "gsel_done", "grow", "gexp", "a_tr", "aT_ready", "grow_stored", "qk_loaded",
            "v_loaded", "negm_loaded", "floor_loaded", "xc_loaded", "e_arg", "e_ready", "e_diag", "sc_done",
            "w_ready", "ot_ready", "pv_done", "dn_ready", "rd_ready", "g_ready", "sqg_ready", "sumg_done",
            "th2_ready", "mix_ready", "gate2_ready", "y_ready"))
        y_stored = [sem(f"y_stored{i}") for i in range(2)]
        y_loaded, h_acc, h_stored2, h_loaded2 = (sem(n) for n in ("y_loaded", "h_acc", "h_stored2", "h_loaded2"))
        (f_row, fexp, negc_stored, negc_loaded, qkv4_ev, sq4_ready, sum4_done, ln4_ready, r4_ready, hat_ready,
         vtr4, vn4_ev, s4_done, sadd, smask, smax, sneg, pexp, sinv, pscaled, ptr_done, pt_ev, pv4_done,
         th4_ready, gate4_ready, y4_ready) = (sem(n) for n in (
            "f_row", "fexp", "negc_stored", "negc_loaded", "qkv4_ev", "sq4_ready", "sum4_done", "ln4_ready",
            "r4_ready", "hat_ready", "vtr4", "vn4_ev", "s4_done", "sadd", "smask", "smax", "sneg", "pexp",
            "sinv", "pscaled", "ptr_done", "pt_ev", "pv4_done", "th4_ready", "gate4_ready", "y4_ready"))
        hn_ready, out_tr, o_ready = sem("hn_ready"), sem("out_tr"), sem("o_ready")
        out_stored = [sem(f"out_stored{i}") for i in range(2)]

        w_in_a = a_w_in[0].rearrange("(k p) m -> p k m", p=P)
        w_in_b = b_w_in[0].rearrange("(k p) m -> p k m", p=P)
        w_out_a = a_w_out[0].rearrange("(f k p) m -> f p k m", p=P, k=KT)
        w_out_b = b_w_out[0].rearrange("(k p) m -> p k m", p=P)
        w_q = a_w_q[0].rearrange("h (k p) m -> p (h k) m", p=P)
        w_k = a_w_k[0].rearrange("h (k p) m -> p (h k) m", p=P)
        w_v = a_w_v[0].rearrange("h (k p) m -> p (h k) m", p=P)
        w_g = a_w_gate[0].rearrange("(r p) g -> p r g", p=P)
        Z_B = 3 * BH * BD + BH

        def wait(eng, semaphore, value):
            if not (isinstance(value, int) and value <= 0):
                eng.wait_ge(semaphore, value)

        def flat(t):
            return t.rearrange("p a b -> p (a b)")

        block = ctx.enter_context(nc.Block())

        @block.sync
        def _(sp):
            def load(b, par_, src, cols=P, tiles=KT, at=0, done=None):
                if not (isinstance(b, int) and b < 2):
                    sp.wait_ge(w_lo_ready, b - 1)
                full = w_raw[par_][:, :].rearrange("p (k m) -> p k m", k=tiles)
                sp.dma_start(full[:, :, at:at + cols], src).then_inc(done or w_raw_ready[par_], 16)

            def load_xm(h, c):
                load(xm_block(h, c), c % 2, w_in_a[:, :, ds(h * DV + c * P, P)])

            def load_qkv(h, par_):
                b = qkv_block(h)
                load(b, par_, w_k[:, ds(h * CT, CT), :], DQK, CT, DQK, wk_raw_ready)
                sp.wait_ge(wk_raw_ready, h * 16 + 16)
                load(b, par_, w_q[:, ds(h * CT, CT), :], DQK, CT)
                load(b + 1, 1 - par_, w_v[:, ds(h * CT, CT), :], DV, CT)
                if not (isinstance(h, int) and h == 0):
                    sp.wait_ge(gate_mm, h)
                for r, n, at in ((0, QT, 0), (AH * QT, QT, QT), (2 * AH * QT, CT, 2 * QT)):
                    sp.dma_start(wg[:, at:at + n, :], w_g[:, ds(h * n + r, n), :]).then_inc(wg_loaded, 16)

            sp.dma_start(meta_nat[:, :], meta_tokens).then_inc(x_loaded, 16)
            for i in range(NT):
                sp.dma_start(x_nat[:, i, :], x[0, i * P:(i + 1) * P, :]).then_inc(x_loaded, 16)
            for c in range(CT):
                load_xm(0, c)
            sp.wait_ge(xl_ready, KT)
            sp.wait_ge(h_stored, 16)
            with sp.Fori(1, AH) as h:
                load_xm(h, 0)
                load_qkv(h - 1, 1)
                for c in range(1, CT):
                    load_xm(h, c)
            load_qkv(AH - 1, 0)
            with sp.Fori(0, AH) as h:
                for k in range(A2_PER):
                    part = (1 + k // CT) * AI + k % CT * P
                    load(h * A2_PER + (A2_0 + k), k % 2, w_in_a[:, :, ds(h * DV + part, P)])
            for f in range(2):
                with sp.Fori(0, KT // 2) as i:
                    for k in range(2):
                        load(i * 2 + (A3_0 + f * KT + k), k, w_out_a[f][:, :, ds(i * (2 * P) + k * P, P)])
            load(B1_0, B1_0 % 2, w_in_b[:, :, 3 * BH * BD:3 * BH * BD + P])
            with sp.Fori(0, BH) as h:
                for k in range(B1_PER):
                    part = (0, BH * BD, 2 * BH * BD, Z_B)[k]
                    load(h * B1_PER + (B1_0 + 1 + k), (B1_0 + 1 + k) % 2, w_in_b[:, :, ds(h * BD + part, P)])
            with sp.Fori(0, KT // 2) as i:
                for k in range(2):
                    load(i * 2 + (B2_0 + k), (B2_0 + k) % 2, w_out_b[:, :, ds(i * (2 * P) + k * P, P)])
            for i in range(2):
                sp.wait_ge(out_stored[i], 16 * NT * (KT // CT) // 2)

        @block.gpsimd
        def _(pool):
            pool.memset(ident[:, :], 0.0).then_inc(ident0, 1)
            pool.memset(ones[:, :], 1.0).then_inc(ident0, 1)
            pool.memset(causal01[:, :], 1.0).then_inc(ident0, 1)
            pool.memset(causal_add[:, :], 0.0).then_inc(ident0, 1)
            pool.memset(eps_t[:, :], EPS).then_inc(ident0, 1)
            pool.wait_ge(ident0, 5)
            pool.affine_select(out=ident[:, :], in_=ident[:, :], compare_op=ALU.not_equal, fill=1.0, base=0,
                               pattern=[[-1, P]], channel_multiplier=1).then_inc(const_ready, 1)
            pool.affine_select(out=causal01[:, :], in_=causal01[:, :], compare_op=ALU.is_ge, fill=0.0, base=0,
                               pattern=[[1, P]], channel_multiplier=-1).then_inc(const_ready, 1)
            pool.affine_select(out=causal_add[:, :], in_=causal_add[:, :], compare_op=ALU.is_ge, fill=-1e30,
                               base=0, pattern=[[-1, P]], channel_multiplier=1).then_inc(const_ready, 1)
            pool.wait_ge(h_copied, KT)
            pool.dma_start(h_d, flat(hT0[:, :, :])).then_inc(h_stored, 16)

            def store_xc(h, c):
                pool.wait_ge(xc2_ready, h * CT + (c + 1))
                pool.dma_start(xc_d[:, ds(h * (CT * T) + c * T, T)], xc2[c % 2][:, :]).then_inc(xc_stored[c % 2], 16)

            def store_qkv(h):
                pool.wait_ge(qkv_ev, h * (2 * QT + CT) + 2 * QT)
                pool.dma_start(qk_d[ds(h, 1)].rearrange("a p n -> (a p) n"),
                               flat(qkv[:, 0:2 * QT, :])).then_inc(qk_stored, 16)
                pool.wait_ge(vn1_ev, h * NS + NS)
                dst = v_d[ds(h, 1)].rearrange("a p n -> (a p) n")
                pool.dma_start(dst[0:META, 0:DV], vn1[0:META, 0, :]).then_inc(v_stored, 16)
                pool.dma_start(dst[:, DV:NS * DV], flat(vn1[:, 1:NS, :])).then_inc(v_stored, 16)

            for c in range(CT):
                store_xc(0, c)
            with pool.Fori(1, AH) as h:
                store_qkv(h - 1)
                for c in range(CT):
                    store_xc(h, c)
            store_qkv(AH - 1)

            pool.wait_ge(qk_stored, 16 * AH)
            pool.wait_ge(v_stored, 32 * AH)
            for i in range(2):
                pool.wait_ge(xc_stored[i], 16 * AH * CT // 2)
            pool.wait_ge(gate_mm, AH)
            pool.wait_ge(grow, 12)
            pool.wait_ge(gexp, 3)
            pool.dma_start(negm_d, gr["negm"][:, :]).then_inc(grow_stored, 16)
            pool.dma_start(floor_d, gr["floor"][:, :]).then_inc(grow_stored, 16)
            pool.wait_ge(grow_stored, 32)

            def load_negm(h):
                pool.dma_start(negm_b[:, :], negm_d[ds(h, 1), :].broadcast_to([P, T])).then_inc(negm_loaded, 16)

            def load_qk(h):
                pool.dma_start(flat(qk2[:, :, :]), qk_d[ds(h, 1)].rearrange("a p n -> (a p) n")).then_inc(qk_loaded, 16)

            def load_v_floor(h):
                src = v_d[ds(h, 1)].rearrange("a p n -> (a p) n")
                pool.dma_start(v2[0:META, 0, :], src[0:META, 0:DV]).then_inc(v_loaded, 16)
                pool.dma_start(flat(v2[:, 1:NS, :]), src[:, DV:NS * DV]).then_inc(v_loaded, 16)
                pool.dma_start(floor_b[:, :], floor_d[ds(h, 1), :].broadcast_to([P, T])).then_inc(floor_loaded, 16)

            def load_xc(h):
                pool.dma_start(flat(xcl2[:, :, :]), xc_d[:, ds(h * (CT * T), CT * T)]).then_inc(xc_loaded, 16)

            def store_y(h):
                for c in range(CT):
                    pool.wait_ge(y_ready, h * CT + (c + 1))
                    pool.dma_start(y_d[:, ds(h * (CT * T) + c * T, T)], yb[c % 2][:, :]).then_inc(y_stored[c % 2], 16)

            load_negm(0)
            load_qk(0)
            load_v_floor(0)
            load_xc(0)
            with pool.Fori(0, AH - 1) as h:
                pool.wait_ge(e_arg, h * NS + NS)
                load_negm(h + 1)
                pool.wait_ge(sc_done, h * NS + NS)
                load_qk(h + 1)
                pool.wait_ge(pv_done, h * (1 + CT) + (1 + CT))
                load_v_floor(h + 1)
                store_y(h)
                load_xc(h + 1)
            for i in range(2):
                pool.wait_ge(y_stored[i], 16 * AH * CT // 4)
            pool.wait_ge(g_ready, 2 * CT * AH)
            pool.dma_start(flat(y_in[:, :, :]), y_d[:, 0:KT * T]).then_inc(y_loaded, 16)
            store_y(AH - 1)
            for i in range(2):
                pool.wait_ge(y_stored[i], 16 * AH * CT // 2)
            pool.dma_start(flat(hT3[:, :, :]), h_d).then_inc(h_loaded, 16)
            pool.wait_ge(xl_ready, 2 * KT)
            pool.dma_start(flat(y_in[:, :, :]), y_d[:, KT * T:2 * KT * T]).then_inc(y_loaded, 16)
            pool.wait_ge(h_acc, 2 * KT)
            pool.dma_start(h_d, flat(hT3[:, :, :])).then_inc(h_stored2, 16)

            pool.wait_ge(f_row, 6)
            pool.dma_start(negc_d, fg["negc"][:, :]).then_inc(negc_stored, 16)
            pool.wait_ge(negc_stored, 16)
            pool.dma_start(negc_b[:, :], negc_d[0:1, :].broadcast_to([P, T])).then_inc(negc_loaded, 16)
            with pool.Fori(1, BH) as h:
                pool.wait_ge(sadd, h * NT)
                pool.dma_start(negc_b[:, :], negc_d[ds(h, 1), :].broadcast_to([P, T])).then_inc(negc_loaded, 16)
            pool.wait_ge(y4_ready, BH)
            pool.dma_start(flat(hT5[:, :, :]), h_d).then_inc(h_loaded2, 16)

        @block.scalar
        def _(act):
            def round_w(b, par_):
                if isinstance(b, int) and b >= BLOCKS:
                    return
                act.wait_ge(w_raw_ready[par_], b * 8 + (16 - 8 * par_))
                if not (isinstance(b, int) and b < 2):
                    act.wait_ge(blk_done, b - 1)
                act.activation(w_hi[par_][:, :], w_raw[par_][:, :], ACT.Copy).then_inc(w_hi_ready, 1)

            def inv_sqrt(src, dst, scale, tmp, n, view, ln, done):
                act.activation(view(tmp), src, ACT.Ln, bias=eps_t[:, 0:1], scale=scale).then_inc(ln, 1)
                act.wait_ge(ln, n)
                act.activation(dst, tmp, ACT.Exp, scale=-0.5).then_inc(done, 1)

            cw = a_conv_w[0].rearrange("c (j p) -> (c j) p", p=P)
            act.dma_start(par_rows[:, 0, :], cw).then_inc(par_loaded, 16)
            rows = [(a_conv_b[0], FT, 1, 0), (a_head_norm[0], FT, 1, FT), (a_skip[0], FT, 1, 2 * FT),
                    (a_norm[0], KT, 1, 3 * FT), (b_norm[0], KT, 1, 3 * FT + KT), (final_norm, KT, 2, 0),
                    (b_q_norm[0], 1, 2, KT), (b_k_norm[0], 1, 2, KT + 1)]
            for src, n, t, at in rows:
                act.dma_start(par_rows[at:at + n, t, :],
                              src.rearrange("(j p) -> j p", p=P)).then_inc(par_loaded, 16)
            act.dma_start(bf[:, :], b_b_f[0].rearrange("(g a) -> g a", a=1)).then_inc(par_loaded, 16)
            round_w(0, 0)
            round_w(1, 1)
            act.wait_ge(ident0, 5)
            for j in range(KT):
                act.wait_ge(h_copied, j + 1)
                if j >= 2:
                    act.wait_ge(sumsq_done, j - 1)
                act.activation(sq[j % 2][:, :], hT0[:, j, :], ACT.Square).then_inc(sq_ready, 1)
            act.wait_ge(sumsq_done, KT)
            inv_sqrt(halves(mm[1]), rstd[:, :], 1.0 / D, rtmp[:, :], 1, two, ln_ready, rstd_ready)
            for j in range(KT):
                act.wait_ge(xt_ready, j + 1)
                act.activation(XH[:, j, :], xt0[j % 2][:, :], ACT.Copy).then_inc(xh_ready, 1)

            act.wait_ge(xl_ready, KT)
            act.wait_ge(h_stored, 16)
            act.dma_start(bg[:, :], a_b_gate[0].rearrange("(g a) -> g a", a=1)).then_inc(par_loaded, 16)

            def conv_tile(h, c, n, npar):
                b = xm_block(h, c)
                e = h * CT + c
                p = c % 2
                src = halves(mm[p])
                act.wait_ge(blk_done, b + 1)
                if not (isinstance(h, int) and h == 0 and c < 2):
                    act.wait_ge(taps, e * 3 - 3)
                act.activation(two(xm_pad[p][:, TAPS - 1:]), src, ACT.Copy).then_inc(xm_raw, 1)
                act.activation(two(xmh[:, c, :]), src, ACT.Copy).then_inc(xm_hi, 1)
                if not (isinstance(h, int) and h == 0 and c < 2):
                    act.wait_ge(xc2_ready, e - 1)
                act.activation(two(conv[p][:, :]), src, ACT.Identity,
                               bias=par[:, ds(h * CT + (C_CB + c), 1)],
                               scale=par[:, ds(h * CT + (C_CW + (TAPS - 1) * FT + c), 1)]).then_inc(cv_aff, 1)
                round_w(n, npar)
                act.wait_ge(taps, e * 3 + 3)
                act.activation(th1[:, :], conv[p][:, :], ACT.Tanh, scale=0.5).then_inc(th1_ready, 1)
                act.wait_ge(xc2_ready, e + 1)
                act.activation(xch[:, c, :], xc2[p][:, :], ACT.Copy, scale=0.5).then_inc(xc_hi, 1)

            def evacuate_qkv(h, b, par_, n0):
                if not (isinstance(h, int) and h == 0):
                    act.wait_ge(qk_stored, h * 16)
                for j in range(2 * QT + CT):
                    if j == 2 * QT and not (isinstance(h, int) and h == 0):
                        act.wait_ge(v_tr, h * NS)
                        act.wait_ge(gate_mm, h)
                    act.wait_ge(qkv_mm, h * 8 + (j + 1))
                    act.activation(two(qkv[:, j, :]), halves(ax[j % 2]), ACT.Copy).then_inc(qkv_ev, 1)
                    if j == 2 * QT - 1 and n0 is not None:
                        round_w(b + 2, par_)

            for c in range(CT):
                conv_tile(0, c, c + 2, c % 2)
            act.wait_ge(par_loaded, 16 * 11)
            with act.Fori(1, AH) as h:
                b0 = xm_block(h, 0)
                round_w(b0 + 2, 0)
                evacuate_qkv(h - 1, b0 + 1, 1, True)
                conv_tile(h, 0, b0 + 4, 0)
                conv_tile(h, 1, b0 + 5, 1)
                conv_tile(h, 2, b0 + 6, 0)
                conv_tile(h, 3, b0 + 7, 1)
            evacuate_qkv(AH - 1, qkv_block(AH - 1), 0, True)
            round_w(A2_0 + 1, 1)

            act.wait_ge(grow, 3)
            act.activation(gr["e"][:, :], gr["abs"][:, :], ACT.Exp, scale=-1.0).then_inc(gexp, 1)
            act.wait_ge(gexp, 1)
            act.activation(gr["e"][:, :], gr["e"][:, :], ACT.Ln, bias=1.0).then_inc(gexp, 1)
            act.wait_ge(grow, 9)
            act.activation(gr["floor"][:, :], gr["m"][:, :], ACT.Exp, scale=-1.0).then_inc(gexp, 1)

            act.wait_ge(v_stored, 32 * AH)
            for i in range(2):
                act.wait_ge(xc_stored[i], 16 * AH * CT // 2)
            def head_a2(h):
                b = h * A2_PER + A2_0
                for c in range(CT):
                    act.wait_ge(blk_done, b + (c + 1))
                    wait(act, g_ready, h * (2 * CT))
                    act.activation(two(OT[:, c, :]), halves(mm[c % 2]), ACT.Tanh, scale=0.5).then_inc(ot_ready, 1)
                    round_w(b + (c + 2), c % 2)
                    if c == 0:
                        act.wait_ge(e_arg, h * NS + NS)
                        act.activation(EW[0:META, 0:T], EW[0:META, 0:T], ACT.Exp).then_inc(e_ready, 1)
                        act.activation(EW[:, T:], EW[:, T:], ACT.Exp).then_inc(e_ready, 1)
                for c in range(CT):
                    act.wait_ge(g_ready, h * (2 * CT) + (CT + c + 1))
                    if c >= 2:
                        act.wait_ge(sumg_done, h * CT + (c - 1))
                    act.activation(sq[c % 2][:, :], G[:, c, :], ACT.Square).then_inc(sqg_ready, 1)
                for c in range(CT):
                    k = CT + c
                    if c == 0:
                        round_w(b + (k + 2), 0)
                        act.wait_ge(sumg_done, h * CT + CT)
                        wait(act, y_ready, h * CT)
                        inv_sqrt(halves(ax[0]), rstd[:, :], 0.25 / DV, rtmp[:, :], h + 2, two, ln_ready, rstd_ready)
                    act.wait_ge(blk_done, b + (k + 1))
                    if c < 2:
                        wait(act, gate2_ready, h * CT)
                    else:
                        act.wait_ge(gate2_ready, h * CT + (c - 1))
                    act.activation(two(th2[c % 2][:, :]), halves(mm[k % 2]), ACT.Tanh, scale=0.5).then_inc(th2_ready, 1)
                    if c > 0:
                        round_w(b + (k + 2), c % 2)

            head_a2(0)
            with act.Fori(1, AH) as h:
                head_a2(h)

            def round_x(src, use, n=T):
                for j in range(KT):
                    act.activation(XH[:, j, 0:n], src[:, j, :], ACT.Copy).then_inc(xh_ready, 1)

            for f in range(2):
                act.wait_ge(y_loaded, 16 * (f + 1))
                act.wait_ge(blk_done, A3_0 + f * KT)
                round_x(y_in, 1 + f)
                with act.Fori(0, KT // 2) as i:
                    for k in range(2):
                        round_w(i * 2 + (A3_0 + f * KT + 2 + k), k)
                        if f:
                            act.wait_ge(h_acc, i * 2 + (KT + k + 1))
                            act.wait_ge(sumsq_done, i * 2 + (KT + k - 1))
                            row = hT3[:, ds(i * 2 + k, 1), :].rearrange("p a n -> p (a n)")
                            act.activation(sq[k][:, :], row, ACT.Square).then_inc(sq_ready, 1)
            act.wait_ge(sumsq_done, 2 * KT)
            inv_sqrt(halves(ax[0]), rstd[:, :], 1.0 / D, rtmp[:, :], AH + 2, two, ln_ready, rstd_ready)
            for j in range(KT):
                act.wait_ge(xt_ready, KT + j + 1)
                act.activation(XH[:, j, :], xt3[j % 2][:, :], ACT.Copy).then_inc(xh_ready, 1)

            act.wait_ge(f_row, 2)
            act.activation(fg["e"][:, :], fg["abs"][:, :], ACT.Exp, scale=-1.0).then_inc(fexp, 1)
            act.wait_ge(fexp, 1)
            act.activation(fg["l1"][:, :], fg["e"][:, :], ACT.Ln, bias=1.0).then_inc(fexp, 1)
            round_w(B1_0 + 2, B1_0 % 2)
            act.wait_ge(h_stored2, 16)

            def softmax_exp(p_, i):
                act.wait_ge(sneg, p_ * NT + (i + 1))
                w = S_TILES[i + 1][0] + P
                act.activation(PR[:, i, 0:w], SS[i % 2][:, 0:w], ACT.Exp, bias=s_neg[:, i:i + 1],
                               accum_out=s_sum[:, i:i + 1]).then_inc(pexp, 1)

            def head_b1(h, first, attend):
                b = h * B1_PER + (B1_0 + 1)
                q0 = B1_0 + 1
                act.wait_ge(blk_done, b + 1)
                if not first:
                    act.wait_ge(hat_ready, h * 2)
                act.activation(QR[:, :], mm[0][:, 0:SEQ], ACT.Copy).then_inc(qkv4_ev, 1)
                act.activation(sq[0][:, 0:SEQ], mm[0][:, 0:SEQ], ACT.Square).then_inc(sq4_ready, 1)
                round_w(b + 2, q0 % 2)
                if attend:
                    for i in range(3):
                        softmax_exp(h - 1, i)
                act.wait_ge(blk_done, b + 2)
                act.activation(two(KR[:, :]), halves(mm[1]), ACT.Copy).then_inc(qkv4_ev, 1)
                act.activation(two(sq[1][:, :]), halves(mm[1]), ACT.Square).then_inc(sq4_ready, 1)
                round_w(b + 3, (q0 + 1) % 2)
                if attend:
                    softmax_exp(h - 1, 3)
                act.wait_ge(blk_done, b + 3)
                if not first:
                    act.wait_ge(vtr4, h * 2)
                act.activation(two(VT[:, :]), halves(mm[0]), ACT.Copy).then_inc(qkv4_ev, 1)
                round_w(b + 4, q0 % 2)
                act.wait_ge(blk_done, b + 4)
                if not first:
                    act.wait_ge(gate4_ready, h)
                act.activation(th4[:, :], mm[1][:, 0:SEQ], ACT.Tanh, scale=0.5).then_inc(th4_ready, 1)
                act.wait_ge(sum4_done, h * 2 + 1)
                inv_sqrt(halves(mm[0]), rstd[:, :], 1.0 / BD, rtmp[:, :], h * 2 + 1, two, ln4_ready, r4_ready)
                act.wait_ge(sum4_done, h * 2 + 2)
                act.wait_ge(r4_ready, h * 2 + 1)
                inv_sqrt(ax[0][:, 0:SEQ], rq[:, :], 1.0 / BD, rtmp[:, 0:SEQ], h * 2 + 2, lambda t: t, ln4_ready, r4_ready)
                round_w(b + 5, (q0 + 1) % 2)

            head_b1(0, True, False)
            with act.Fori(1, BH) as h:
                head_b1(h, False, True)
            for i in range(NT):
                softmax_exp(BH - 1, i)

            act.wait_ge(y4_ready, BH)
            round_x(Y, 4, SEQ)

            def tile_b2(i, k, more=True):
                if more:
                    round_w(i * 2 + (B2_0 + 2 + k), (B2_0 + k) % 2)
                act.wait_ge(h_acc, i * 2 + (2 * KT + k + 1))
                act.wait_ge(sumsq_done, i * 2 + (2 * KT + k - 1))
                row = hT5[:, ds(i * 2 + k, 1), META:T].rearrange("p a n -> p (a n)")
                act.activation(sq[k][:, 0:SEQ], row, ACT.Square).then_inc(sq_ready, 1)

            with act.Fori(0, KT // 2 - 1) as i:
                for k in range(2):
                    tile_b2(i, k)
            for k in range(2):
                tile_b2(KT // 2 - 1, k, False)
            act.wait_ge(sumsq_done, 3 * KT)
            inv_sqrt(ax[0][:, 0:SEQ], rstd[:, 0:SEQ], 1.0 / D, rtmp[:, 0:SEQ], AH + 3, lambda t: t, ln_ready, rstd_ready)
            for n in range(NT * KT // CT):
                act.wait_ge(out_tr, n + 1)
                if n >= 2:
                    act.wait_ge(out_stored[n % 2], 16 * (n // 2))
                act.activation(o_nat[n % 2][:, :], ax[n % 2][:, 0:BANK], ACT.Copy).then_inc(o_ready, 1)
                act.wait_ge(o_ready, n + 1)
                i, jg = n % NT, n // NT
                act.dma_start(out[0, i * P:(i + 1) * P, jg * BANK:(jg + 1) * BANK], o_nat[n % 2][:, :])\
                    .then_inc(out_stored[n % 2], 16)

        @block.vector
        def _(dve):
            def low_w(b, par_):
                if isinstance(b, int) and b >= BLOCKS:
                    return
                dve.wait_ge(w_hi_ready, b + 1)
                dve.tensor_tensor(w_lo[par_][:, :], w_raw[par_][:, :], w_hi[par_][:, :].bitcast(F32),
                                  ALU.subtract).then_inc(w_lo_ready, 1)

            low_w(0, 0)
            low_w(1, 1)
            dve.wait_ge(par_tr, 3)
            dve.tensor_copy(par[:, :], mm[0][:, 0:NPAR]).then_inc(par_ready, 1)
            dve.wait_ge(par_ready, 1)
            dve.tensor_scalar(par[:, C_HN:C_AN], par[:, C_HN:C_AN], 0.25, None, ALU.mult).then_inc(par_ready, 1)
            dve.wait_ge(par_ready, 2)

            def norm_tile(src, j, gain, xt, base):
                if j >= 2:
                    dve.wait_ge(xl_ready, xl_base + j - 1)
                dve.scalar_tensor_tensor(out=xt[j % 2][:, :], in0=src, scalar=gain, in1=rstd[:, :],
                                         op0=ALU.mult, op1=ALU.mult).then_inc(xt_ready, 1)

            def low_x(src, j, n=T):
                dve.wait_ge(xh_ready, xl_base + j + 1)
                dve.tensor_tensor(XL[:, j, 0:n], src, XH[:, j, 0:n].bitcast(F32), ALU.subtract).then_inc(xl_ready, 1)

            xl_base = 0
            for j in range(KT):
                dve.wait_ge(x_tr, j + 1)
                dve.tensor_copy(hT0[:, j, :], ax[j % 2][:, X0:2 * BANK]).then_inc(h_copied, 1)
            dve.wait_ge(rstd_ready, 1)
            dve.wait_ge(h_copied, KT)
            for j in range(KT + 1):
                if j < KT:
                    norm_tile(hT0[:, j, :], j, par[:, C_AN + j:C_AN + j + 1], xt0, 0)
                if j > 0:
                    if j == 1:
                        pass
                    dve.wait_ge(xt_ready, j)
                    low_x(xt0[(j - 1) % 2][:, :], j - 1)

            dve.wait_ge(xl_ready, KT)
            dve.wait_ge(h_stored, 16)
            for i in range(2):
                dve.memset(xm_pad[i][:, 0:TAPS - 1], 0.0).then_inc(pad_zero, 1)
            dve.memset(gacc[:, :], 0.0).then_inc(gacc_ready, 1)
            dve.wait_ge(pad_zero, 2)

            def conv_tile(h, c, n, npar):
                e = h * CT + c
                p = c % 2
                dve.wait_ge(xm_hi, e + 1)
                dve.tensor_tensor(xml[:, c, :], xm_pad[p][:, TAPS - 1:], xmh[:, c, :].bitcast(F32),
                                  ALU.subtract).then_inc(xm_lo, 1)
                dve.wait_ge(cv_aff, e + 1)
                for k in range(TAPS - 1):
                    tap = TAPS - 2 - k
                    if k:
                        dve.wait_ge(taps, e * 3 + k)
                    dve.scalar_tensor_tensor(out=conv[p][:, :], in0=xm_pad[p][:, tap:tap + T],
                                             scalar=par[:, ds(h * CT + (C_CW + tap * FT + c), 1)],
                                             in1=conv[p][:, :], op0=ALU.mult, op1=ALU.add).then_inc(taps, 1)
                low_w(n, npar)
                dve.wait_ge(th1_ready, e + 1)
                if not (isinstance(h, int) and h == 0 and c < 2):
                    dve.wait_ge(xc_stored[p], h * (8 * CT) + (c // 2) * 16)
                    dve.wait_ge(xc_lo, e - 1)
                dve.scalar_tensor_tensor(out=xc2[p][:, :], in0=th1[:, :], scalar=1.0, in1=conv[p][:, :],
                                         op0=ALU.add, op1=ALU.mult).then_inc(xc2_ready, 1)
                dve.wait_ge(xc_hi, e + 1)
                dve.scalar_tensor_tensor(out=xcl[:, c, :], in0=xc2[p][:, :], scalar=0.5,
                                         in1=xch[:, c, :].bitcast(F32), op0=ALU.mult,
                                         op1=ALU.subtract).then_inc(xc_lo, 1)

            def finish_qkv(h):
                dve.wait_ge(gate_mm, h + 1)
                dve.wait_ge(gacc_ready, h + 1)
                dve.tensor_tensor(two(gacc[:, :]), two(gacc[:, :]), halves(mm[1], HT, NG), ALU.add).then_inc(gacc_ready, 1)
                if not (isinstance(h, int) and h == 0):
                    dve.wait_ge(v_stored, h * 32)
                for i, (_, n) in enumerate(S_TILES):
                    dve.wait_ge(v_tr, h * NS + (i + 1))
                    dve.tensor_copy(vn1[0:n, i, :], ax[i % 2][0:n, 0:BANK]).then_inc(vn1_ev, 1)

            for c in range(CT):
                conv_tile(0, c, c + 2, c % 2)
            with dve.Fori(1, AH) as h:
                b0 = xm_block(h, 0)
                low_w(b0 + 2, 0)
                low_w(b0 + 3, 1)
                finish_qkv(h - 1)
                for c in range(CT):
                    conv_tile(h, c, b0 + (4 + c), c % 2)
            low_w(A2_0, 0)
            finish_qkv(AH - 1)
            low_w(A2_0 + 1, 1)

            dve.wait_ge(gacc_ready, AH + 1)
            dve.wait_ge(par_loaded, 16 * 11)
            dve.tensor_scalar(gacc[:, :], gacc[:, :], bg[:, 0:1], None, ALU.add).then_inc(gb_ready, 1)
            dve.wait_ge(gsel_done, 2)
            dve.wait_ge(qk_stored, 16 * AH)
            dve.wait_ge(v_stored, 32 * AH)
            for i in range(2):
                dve.wait_ge(xc_stored[i], 16 * AH * CT // 2)
            dve.tensor_copy(two(gr["ig"][:, :]), halves(ax[0], HT, AH)).then_inc(grow, 1)
            dve.tensor_copy(two(gr["f"][:, :]), halves(ax[1], HT, AH)).then_inc(grow, 1)
            dve.wait_ge(grow, 2)
            dve.scalar_tensor_tensor(out=gr["abs"][:, :], in0=gr["f"][:, :], scalar=-1.0, in1=gr["f"][:, :],
                                     op0=ALU.mult, op1=ALU.max).then_inc(grow, 1)
            dve.memset(gr["one"][:, :], 1.0).then_inc(grow, 1)
            dve.wait_ge(gexp, 2)
            dve.scalar_tensor_tensor(out=gr["lf"][:, :], in0=gr["f"][:, :], scalar=0.0, in1=gr["e"][:, :],
                                     op0=ALU.min, op1=ALU.subtract).then_inc(grow, 1)
            dve.wait_ge(grow, 5)
            dve.tensor_tensor_scan(gr["B"][:, :], gr["one"][:, :], gr["lf"][:, :], 0.0, ALU.mult, ALU.add).then_inc(grow, 1)
            dve.wait_ge(grow, 6)
            dve.tensor_tensor(gr["a"][:, :], gr["ig"][:, :], gr["B"][:, :], ALU.subtract).then_inc(grow, 1)
            dve.wait_ge(grow, 7)
            dve.tensor_tensor_scan(gr["M"][:, :], gr["one"][:, :], gr["a"][:, :], 0.0, ALU.mult, ALU.max).then_inc(grow, 1)
            dve.wait_ge(grow, 8)
            dve.tensor_tensor(gr["m"][:, :], gr["B"][:, :], gr["M"][:, :], ALU.add).then_inc(grow, 1)
            dve.tensor_scalar(gr["negm"][:, :], gr["M"][:, :], -1.0, None, ALU.mult).then_inc(grow, 1)
            dve.wait_ge(a_tr, 1)
            dve.tensor_copy(aT[0:META, 0, :], ax[0][0:META, 0:AH]).then_inc(grow, 1)
            dve.tensor_copy(flat(aT[:, 1:NS, :]), ax[0][:, AH:NS * AH]).then_inc(grow, 1)
            dve.wait_ge(grow, 12)

            def head_a2(h):
                b = h * A2_PER + A2_0
                dve.wait_ge(negm_loaded, h * 16 + 16)
                wait(dve, pv_done, h * (1 + CT))
                for j, (s, n) in enumerate(S_TILES):
                    dve.tensor_scalar(EW[0:n, E_OFF[j]:E_OFF[j + 1]], negm_b[0:n, s:T],
                                      aT[0:n, j, ds(h, 1)], 0.0, ALU.add, ALU.min).then_inc(e_arg, 1)
                low_w(b + 2, 0)
                dve.wait_ge(e_ready, h * 2 + 2)
                for j, (s, n) in enumerate(S_TILES):
                    dg = EW[0:n, E_OFF[j]:E_OFF[j] + n]
                    dve.tensor_tensor(dg, dg, causal01[0:n, 0:n], ALU.mult).then_inc(e_diag, 1)
                for j, (s, n) in enumerate(S_TILES):
                    if j == 3:
                        low_w(b + 3, 1)
                    dve.wait_ge(sc_done, h * NS + (j + 1))
                    if j == 0:
                        dve.wait_ge(e_diag, h * NS + NS)
                    ps, at = SCORES_AT[j]
                    row = EW[0:n, E_OFF[j]:E_OFF[j + 1]]
                    dve.scalar_tensor_tensor(out=row, in0=ps[0:n, at:at + T - s], scalar=float(DQK) ** -0.5, in1=row,
                                             op0=ALU.mult, op1=ALU.mult).then_inc(w_ready, 1)
                low_w(b + 4, 0)
                dve.wait_ge(floor_loaded, h * 16 + 16)
                dve.wait_ge(pv_done, h * (1 + CT) + 1)
                dve.scalar_tensor_tensor(out=two(dn[:, :]), in0=halves(ax[1]), scalar=-1.0, in1=two(floor_b[:, :]),
                                         op0=ALU.mult, op1=ALU.max).then_inc(dn_ready, 1)
                dve.wait_ge(dn_ready, h * 2 + 1)
                dve.tensor_tensor(two(dn[:, :]), halves(ax[1]), two(dn[:, :]), ALU.max).then_inc(dn_ready, 1)
                dve.wait_ge(dn_ready, h * 2 + 2)
                dve.reciprocal(rd[:, :], dn[:, :]).then_inc(rd_ready, 1)
                low_w(b + 5, 1)
                dve.wait_ge(rd_ready, h + 1)
                for c in range(CT):
                    dve.wait_ge(pv_done, h * (1 + CT) + (c + 2))
                    dve.tensor_tensor(two(G[:, c, :]), halves(ax[c % 2]), two(rd[:, :]), ALU.mult).then_inc(g_ready, 1)
                dve.wait_ge(ot_ready, h * CT + CT)
                dve.wait_ge(g_ready, h * (2 * CT) + CT)
                for c in range(CT):
                    dve.scalar_tensor_tensor(out=G[:, c, :], in0=OT[:, c, :], scalar=1.0, in1=G[:, c, :],
                                             op0=ALU.add, op1=ALU.mult).then_inc(g_ready, 1)
                low_w(b + 6, 0)
                dve.wait_ge(rstd_ready, h + 2)
                dve.wait_ge(xc_loaded, h * 16 + 16)
                for c in range(CT):
                    k = CT + c
                    if c:
                        dve.wait_ge(y_ready, h * CT + c)
                    dve.scalar_tensor_tensor(out=mix[:, :], in0=G[:, c, :],
                                             scalar=par[:, ds(h * CT + (C_HN + c), 1)], in1=rstd[:, :],
                                             op0=ALU.mult, op1=ALU.mult).then_inc(mix_ready, 1)
                    dve.wait_ge(mix_ready, h * (2 * CT) + (2 * c + 1))
                    dve.scalar_tensor_tensor(out=mix[:, :], in0=xcl2[:, c, :],
                                             scalar=par[:, ds(h * CT + (C_SK + c), 1)], in1=mix[:, :],
                                             op0=ALU.mult, op1=ALU.add).then_inc(mix_ready, 1)
                    dve.wait_ge(th2_ready, h * CT + (c + 1))
                    dve.scalar_tensor_tensor(out=two(gate2[:, :]), in0=two(th2[c % 2][:, :]), scalar=1.0,
                                             in1=halves(mm[k % 2]), op0=ALU.add, op1=ALU.mult).then_inc(gate2_ready, 1)
                    dve.wait_ge(gate2_ready, h * CT + (c + 1))
                    dve.wait_ge(mix_ready, h * (2 * CT) + (2 * c + 2))
                    wait(dve, y_stored[c % 2], h * (8 * CT) + (c // 2) * 16)
                    dve.tensor_tensor(yb[c % 2][:, :], mix[:, :], gate2[:, :], ALU.mult).then_inc(y_ready, 1)
                    if c < CT - 1:
                        low_w(b + (k + 3), (k + 3) % 2)

            head_a2(0)
            with dve.Fori(1, AH) as h:
                head_a2(h)

            for f in range(2):
                xl_base = KT * (1 + f)
                dve.wait_ge(y_loaded, 16 * (f + 1))
                for j in range(KT):
                    low_x(y_in[:, j, :], j)
                dve.wait_ge(h_loaded, 16)
                with dve.Fori(0, KT // 2) as i:
                    for k in range(2):
                        b = i * 2 + (A3_0 + f * KT + k)
                        dve.wait_ge(blk_done, b + 1)
                        if f:
                            dve.wait_ge(h_acc, i * 2 + (k + 1))
                        row = hT3[:, ds(i * 2 + k, 1), :].rearrange("p a (b n) -> p (a b) n", b=2)
                        dve.tensor_tensor(row, row, halves(mm[k]), ALU.add).then_inc(h_acc, 1)
                        low_w(b + 2, k)
            xl_base = 3 * KT
            dve.wait_ge(rstd_ready, AH + 2)
            for j in range(KT + 1):
                if j < KT:
                    norm_tile(hT3[:, j, :], j, par[:, C_BN + j:C_BN + j + 1], xt3, 0)
                if j > 0:
                    dve.wait_ge(xt_ready, KT + j)
                    low_x(xt3[(j - 1) % 2][:, :], j - 1)

            dve.wait_ge(h_stored2, 16)
            dve.wait_ge(xl_ready, 4 * KT)
            dve.wait_ge(blk_done, B1_0 + 1)
            dve.tensor_scalar(two(fg["f"][:, :]), halves(mm[1], HT, BH), bf[:, 0:1], None, ALU.add).then_inc(f_row, 1)
            dve.wait_ge(f_row, 1)
            dve.scalar_tensor_tensor(out=fg["abs"][:, :], in0=fg["f"][:, :], scalar=-1.0, in1=fg["f"][:, :],
                                     op0=ALU.mult, op1=ALU.max).then_inc(f_row, 1)
            dve.memset(fg["one"][:, :], 1.0).then_inc(f_row, 1)
            dve.wait_ge(fexp, 2)
            dve.scalar_tensor_tensor(out=fg["lf"][:, :], in0=fg["f"][:, :], scalar=0.0, in1=fg["l1"][:, :],
                                     op0=ALU.min, op1=ALU.subtract).then_inc(f_row, 1)
            dve.wait_ge(f_row, 4)
            dve.tensor_tensor_scan(fg["c"][:, :], fg["one"][:, :], fg["lf"][:, :], 0.0, ALU.mult, ALU.add).then_inc(f_row, 1)
            dve.wait_ge(f_row, 5)
            dve.tensor_scalar(fg["negc"][:, :], fg["c"][:, :], -1.0, None, ALU.mult).then_inc(f_row, 1)
            low_w(B1_0 + 2, B1_0 % 2)
            dve.wait_ge(negc_stored, 16)

            def softmax_in(p_, i):
                w = S_TILES[i + 1][0] + P
                ps, at = ((ax[0], 0), (ax[0], BANK), (ax[1], 0), (ax[0], X0))[i]
                src = ps[:, at:at + w]
                s_ = SS[i % 2]
                dve.wait_ge(s4_done, p_ * NT + (i + 1))
                if i == 0:
                    dve.wait_ge(negc_loaded, p_ * 16 + 16)
                if i >= 2:
                    dve.wait_ge(pexp, p_ * NT + (i - 1))
                dve.scalar_tensor_tensor(out=s_[:, 0:w], in0=src, scalar=float(BD) ** -0.5, in1=negc_b[:, 0:w],
                                         op0=ALU.mult, op1=ALU.add).then_inc(sadd, 1)
                dve.wait_ge(sadd, p_ * NT + (i + 1))
                dve.tensor_tensor(s_[:, w - P:w], s_[:, w - P:w], causal_add[:, :], ALU.add).then_inc(smask, 1)
                dve.wait_ge(smask, p_ * NT + (i + 1))
                dve.reduce_max(s_max[:, i:i + 1], s_[:, 0:w], AX_X).then_inc(smax, 1)
                dve.wait_ge(smax, p_ * NT + (i + 1))
                dve.tensor_scalar(s_neg[:, i:i + 1], s_max[:, i:i + 1], -1.0, None, ALU.mult).then_inc(sneg, 1)

            def softmax_out(p_, i):
                w = S_TILES[i + 1][0] + P
                dve.wait_ge(pexp, p_ * NT + (i + 1))
                dve.reciprocal(s_inv[:, i:i + 1], s_sum[:, i:i + 1]).then_inc(sinv, 1)
                dve.wait_ge(sinv, p_ * NT + (i + 1))
                dve.tensor_scalar(PR[:, i, 0:w], PR[:, i, 0:w], s_inv[:, i:i + 1], None, ALU.mult).then_inc(pscaled, 1)

            def take_pt(p_, i):
                dve.wait_ge(ptr_done, p_ * (NT + 1) + (i + 1))
                if i < NT:
                    w = (i + 1) * P
                    src = ax[1][:, 0:w] if i % 2 else ax[1][:, BANK:BANK + w]
                    dve.tensor_copy(PTr[:, i, 0:w], src).then_inc(pt_ev, 1)
                else:
                    dve.tensor_copy(PTm[:, :], ax[0][0:META, 0:SEQ]).then_inc(pt_ev, 1)

            def head_b1(h, proj, attend, p_):
                b = h * B1_PER + (B1_0 + 1)
                q0 = B1_0 + 1
                if attend:
                    for i in range(3):
                        softmax_in(p_, i)
                if proj:
                    low_w(b + 2, q0 % 2)
                if attend:
                    for i in range(3):
                        softmax_out(p_, i)
                    softmax_in(p_, 3)
                    take_pt(p_, 0)
                if proj:
                    low_w(b + 3, (q0 + 1) % 2)
                if attend:
                    softmax_out(p_, 3)
                    for i in range(1, NT + 1):
                        take_pt(p_, i)
                if proj:
                    low_w(b + 4, q0 % 2)
                if attend:
                    dve.wait_ge(pv4_done, p_ + 1)
                    row = Y[:, ds(p_, 1), :].rearrange("p a n -> p (a n)")
                    dve.scalar_tensor_tensor(out=row, in0=ax[1][:, BANK:BANK + SEQ], scalar=0.5, in1=row,
                                             op0=ALU.mult, op1=ALU.mult).then_inc(y4_ready, 1)
                if proj:
                    dve.wait_ge(th4_ready, h + 1)
                    row = Y[:, ds(h, 1), :].rearrange("p a n -> p (a n)")
                    dve.scalar_tensor_tensor(out=row, in0=th4[:, :], scalar=1.0, in1=mm[1][:, 0:SEQ],
                                             op0=ALU.add, op1=ALU.mult).then_inc(gate4_ready, 1)
                    dve.wait_ge(vtr4, h * 2 + 2)
                    dve.tensor_copy(flat(vn4[:, :, :]), ax[1][:, 0:NT * BD]).then_inc(vn4_ev, 1)
                    dve.tensor_copy(vm4[:, :], ax[0][0:META, BANK:BANK + BD]).then_inc(vn4_ev, 1)
                    dve.wait_ge(r4_ready, h * 2 + 1)
                    dve.scalar_tensor_tensor(out=KH[:, :], in0=KR[:, :], scalar=par[:, C_KN:C_KN + 1], in1=rstd[:, :],
                                             op0=ALU.mult, op1=ALU.mult).then_inc(hat_ready, 1)
                    dve.wait_ge(r4_ready, h * 2 + 2)
                    dve.scalar_tensor_tensor(out=QH[:, :], in0=QR[:, :], scalar=par[:, C_QN:C_QN + 1], in1=rq[:, :],
                                             op0=ALU.mult, op1=ALU.mult).then_inc(hat_ready, 1)
                    low_w(b + 5, (q0 + 1) % 2)

            head_b1(0, True, False, 0)
            with dve.Fori(1, BH) as h:
                head_b1(h, True, True, h - 1)
            head_b1(BH, False, True, BH - 1)

            xl_base = 4 * KT
            dve.wait_ge(y4_ready, BH)
            for j in range(KT):
                low_x(Y[:, j, :], j, SEQ)
            dve.wait_ge(h_loaded2, 16)

            def add_b2(i, k, more=True):
                b = i * 2 + (B2_0 + k)
                dve.wait_ge(blk_done, b + 1)
                row = hT5[:, ds(i * 2 + k, 1), META:T].rearrange("p a n -> p (a n)")
                dve.tensor_tensor(row, row, mm[k][:, 0:SEQ], ALU.add).then_inc(h_acc, 1)
                if more:
                    low_w(b + 2, (B2_0 + k) % 2)

            with dve.Fori(0, KT // 2 - 1) as i:
                for k in range(2):
                    add_b2(i, k)
            for k in range(2):
                add_b2(KT // 2 - 1, k, False)
            dve.wait_ge(rstd_ready, AH + 3)
            dve.wait_ge(h_acc, 3 * KT)
            for j in range(KT):
                dve.scalar_tensor_tensor(out=hT5[:, j, META:T], in0=hT5[:, j, META:T],
                                         scalar=par[:, C_FN + j:C_FN + j + 1], in1=rstd[:, 0:SEQ],
                                         op0=ALU.mult, op1=ALU.mult).then_inc(hn_ready, 1)

        @block.tensor
        def _(pe):
            ALL = ((0, 0, HT), (BANK, HT, HT))
            REAL = ((0, META, SEQ),)
            PACKED = ((0, 0, SEQ),)

            def three(ps, wh, wl, xh, xl, spans, first, last):
                for k, (w, v) in enumerate(((wh, xh), (wh, xl), (wl, xh))):
                    for at, t0, n in spans:
                        i = pe.matmul(ps[:, at:at + n], w, v[:, t0:t0 + n],
                                      start=first and k == 0, stop=last and k == 2)
                return i

            def blockmm(b, par_, ps, spans=ALL, fresh=None):
                pe.wait_ge(w_lo_ready, b + 1)
                for k in range(KT):
                    if fresh is not None:
                        pe.wait_ge(xl_ready, fresh + k + 1)
                    i = three(ps, w_hi[par_][:, k * P:(k + 1) * P], w_lo[par_][:, k * P:(k + 1) * P],
                              XH[:, k, :], XL[:, k, :], spans, k == 0, k == KT - 1)
                i.then_inc(blk_done, 1)

            def full_sum(ps, src, n, first=True, last=True):
                for a in range(2):
                    i = pe.matmul(ps[:, a * BANK:a * BANK + n], ones[:, :], src[:, a * n:(a + 1) * n],
                                  start=first, stop=last)
                return i

            def sum_squares(n, buf, spans, first, last):
                pe.wait_ge(sq_ready, n + 1)
                for at, t0, w in spans:
                    i = pe.matmul(ax[0][:, at:at + w], ones[:, :], sq[buf][:, t0:t0 + w], start=first, stop=last)
                i.then_inc(sumsq_done, 1)

            pe.wait_ge(const_ready, 3)
            pe.wait_ge(par_loaded, 16 * 10)
            for t, n in enumerate((P, P, NPAR - 2 * P)):
                pe.transpose(mm[0][:, t * P:t * P + n], par_rows[0:n, t, :], ident[0:n, 0:n]).then_inc(par_tr, 1)
            pe.wait_ge(x_loaded, 16 * (NT + 1))
            for j in range(KT + 1):
                if j < KT:
                    if j >= 2:
                        pe.wait_ge(h_copied, j - 1)
                    ps = ax[j % 2]
                    pe.transpose(ps[:, X0:BANK], meta_nat[:, j * P:(j + 1) * P], ident[0:META, 0:META])
                    for i in range(NT):
                        t = pe.transpose(ps[:, BANK + i * P:BANK + (i + 1) * P], x_nat[:, i, j * P:(j + 1) * P], ident[:, :])
                    t.then_inc(x_tr, 1)
                if j > 0:
                    pe.wait_ge(sq_ready, j)
                    full_sum(mm[1], sq[(j - 1) % 2], HT, j == 1, j == KT).then_inc(sumsq_done, 1)

            def xm_tile(h, c, par_):
                if isinstance(h, int) and h == 0:
                    if c == 0:
                        pe.wait_ge(par_ready, 1)
                    if c == 1:
                        pe.wait_ge(rstd_ready, 1)
                    if c >= 2:
                        pe.wait_ge(cv_aff, c - 1)
                else:
                    pe.wait_ge(cv_aff, h * CT + (c - 1))
                    if c == 1:
                        pe.wait_ge(gacc_ready, h + 1)
                blockmm(xm_block(h, c), par_, mm[c % 2], fresh=0 if isinstance(h, int) and h == 0 and c == 0 else None)

            def qkv_tiles(h, par_):
                b = qkv_block(h)
                pe.wait_ge(w_lo_ready, b + 1)
                pe.wait_ge(xc_lo, h * CT + CT)
                first = isinstance(h, int) and h == 0
                NJ = 2 * QT + CT

                def gate(j):
                    pe.wait_ge(qkv_ev, h * NJ + (j + 1))
                    for a in range(2):
                        i = pe.matmul(mm[1][0:NG, a * BANK:a * BANK + HT], wg[:, j, :], qkv[:, j, a * HT:(a + 1) * HT],
                                      start=j == 0, stop=j == NJ - 1)
                    return i

                for j in range(NJ):
                    if j == 2 * QT:
                        pe.wait_ge(w_lo_ready, b + 2)
                    if j < 2:
                        if not first:
                            pe.wait_ge(vn1_ev, h * NS)
                    else:
                        pe.wait_ge(qkv_ev, h * NJ + (j - 1))
                    p_ = par_ if j < 2 * QT else 1 - par_
                    col = j % (2 * QT) * P
                    xh, xl = (xch, xcl) if j < 2 * QT else (xmh, xml)
                    for k in range(CT):
                        at = k * CT * P + col
                        i = three(ax[j % 2], w_hi[p_][:, at:at + P], w_lo[p_][:, at:at + P],
                                  xh[:, k, :], xl[:, k, :], ALL, k == 0, k == CT - 1)
                    if j % (2 * QT) == 2 * QT - 1:
                        i.then_inc(qkv_mm, 1)
                        pe.wait_ge(qkv_mm, h * NJ + (j + 1))
                        pe.sem_inc(blk_done, 1)
                    else:
                        i.then_inc(qkv_mm, 1)
                    if j == 1:
                        pe.wait_ge(wg_loaded, h * 48 + 48)
                    if j >= 1:
                        gate(j - 1)
                gate(NJ - 1).then_inc(gate_mm, 1)
                for i, (s, n) in enumerate(S_TILES):
                    if i >= 2:
                        pe.wait_ge(vn1_ev, h * NS + (i - 1))
                    for c in range(CT):
                        t = pe.transpose(ax[i % 2][0:n, c * P:(c + 1) * P], qkv[:, 2 * QT + c, s:s + n], ident[:, :])
                    t.then_inc(v_tr, 1)

            for c in range(CT):
                xm_tile(0, c, c % 2)
            with pe.Fori(1, AH) as h:
                xm_tile(h, 0, 0)
                qkv_tiles(h - 1, 1)
                for c in range(1, CT):
                    xm_tile(h, c, c % 2)
            qkv_tiles(AH - 1, 0)

            pe.wait_ge(gb_ready, 1)
            pe.wait_ge(vn1_ev, AH * NS)
            for g in range(2):
                for a in range(2):
                    i = pe.matmul(ax[g][0:AH, a * BANK:a * BANK + HT], ident[0:NG, g * AH:(g + 1) * AH],
                                  gacc[:, a * HT:(a + 1) * HT], start=True, stop=True)
                i.then_inc(gsel_done, 1)
            pe.wait_ge(grow, 7)
            for i, (s, n) in enumerate(S_TILES):
                t = pe.transpose(ax[0][0:n, i * AH:(i + 1) * AH], gr["a"][:, s:s + n], ident[0:AH, 0:AH])
            t.then_inc(a_tr, 1)

            pe.wait_ge(grow, 12)
            pe.wait_ge(gacc_ready, AH + 1)
            def scores_a2(h, j):
                s, n = S_TILES[j]
                ps, at0 = SCORES_AT[j]
                if j == 0:
                    pe.wait_ge(qk_loaded, h * 16 + 16)
                    wait(pe, ln_ready, h + 1)
                    wait(pe, g_ready, h * (2 * CT))
                if j == 3:
                    pe.wait_ge(w_ready, h * NS + 1)
                for at, t0, w in ([(X0, 0, META), (BANK, META, SEQ)] if j == 0 else [(at0, s, T - s)]):
                    for k in range(QT):
                        i = pe.matmul(ps[0:n, at:at + w], qk2[:, QT + k, s:s + n],
                                      qk2[:, k, t0:t0 + w], start=k == 0, stop=k == QT - 1)
                i.then_inc(sc_done, 1)

            def over_s(ps, stationary):
                for j, (s, n) in enumerate(S_TILES):
                    for a in range(2):
                        lo, hi = max(s, a * HT), (a + 1) * HT
                        if lo >= hi:
                            continue
                        last = not any(max(s2, a * HT) < hi for s2, _ in S_TILES[j + 1:])
                        i = pe.matmul(ps[:, a * BANK + lo - a * HT:a * BANK + HT], stationary(j, n),
                                      EW[0:n, E_OFF[j] + lo - s:E_OFF[j] + hi - s], start=j == 0, stop=last)
                i.then_inc(pv_done, 1)

            def head_a2(h):
                b = h * A2_PER + A2_0
                for c in range(CT):
                    if c < 2:
                        wait(pe, gate2_ready, h * CT + (c - 1))
                    else:
                        pe.wait_ge(ot_ready, h * CT + (c - 1))
                    blockmm(b + c, c % 2, mm[c % 2])
                    if c == 0:
                        for j in range(3):
                            scores_a2(h, j)
                    if c == 1:
                        for j in range(3, NS):
                            scores_a2(h, j)
                    if c == 2:
                        pe.wait_ge(w_ready, h * NS + NS)
                        over_s(ax[1], lambda j, n: ones[0:n, :])
                pe.wait_ge(v_loaded, h * 32 + 32)
                for c in range(CT):
                    if c == 1:
                        pe.wait_ge(dn_ready, h * 2 + 2)
                    if c > 1:
                        pe.wait_ge(g_ready, h * (2 * CT) + (c - 1))
                    over_s(ax[c % 2], lambda j, n: v2[0:n, j, c * P:(c + 1) * P])
                for c in range(CT):
                    k = CT + c
                    if c < 2:
                        pe.wait_ge(ot_ready, h * CT + (c + 3))
                    else:
                        pe.wait_ge(gate2_ready, h * CT + (c - 1))
                    blockmm(b + k, k % 2, mm[k % 2])
                    if c == 0:
                        pe.wait_ge(g_ready, h * (2 * CT) + CT)
                        for c2 in range(CT):
                            pe.wait_ge(sqg_ready, h * CT + (c2 + 1))
                            full_sum(ax[0], sq[c2 % 2], HT, c2 == 0, c2 == CT - 1).then_inc(sumg_done, 1)

            head_a2(0)
            with pe.Fori(1, AH) as h:
                head_a2(h)

            def out_blocks(b0, acc0, spans, fresh, sq0=None):
                for k in range(2):
                    blockmm(b0 + k, (b0 + k) % 2, mm[k], spans, fresh if k == 0 else None)
                if sq0 is not None:
                    sum_squares(sq0, 0, spans, True, False)
                with pe.Fori(1, KT // 2) as i:
                    for k in range(2):
                        pe.wait_ge(h_acc, i * 2 + (acc0 + k - 1))
                        blockmm(i * 2 + (b0 + k), (b0 + k) % 2, mm[k], spans)
                        if sq0 is not None:
                            sum_squares(i * 2 + (sq0 + k - 1), 1 - k, spans, False, False)
                if sq0 is not None:
                    sum_squares(sq0 + KT - 1, 1, spans, False, True)

            pe.wait_ge(gate2_ready, AH * CT)
            out_blocks(A3_0, 0, ALL, KT)
            pe.wait_ge(h_acc, KT)
            out_blocks(A3_0 + KT, KT, ALL, 2 * KT, KT)

            pe.wait_ge(rstd_ready, AH + 2)
            blockmm(B1_0, B1_0 % 2, mm[1], fresh=3 * KT)

            def scores(p_, i):
                w = S_TILES[i + 1][0] + P
                q = QH[:, i * P:(i + 1) * P]
                if i < 3:
                    at = (ax[0][:, 0:w], ax[0][:, BANK:BANK + w], ax[1][:, 0:w])[i]
                    m = pe.matmul(at, q, KH[:, 0:w], start=True, stop=True)
                else:
                    pe.matmul(ax[0][:, X0:BANK], q, KH[:, 0:META], start=True, stop=True)
                    m = pe.matmul(ax[0][:, BANK:2 * BANK], q, KH[:, META:T], start=True, stop=True)
                m.then_inc(s4_done, 1)

            def transpose_p(p_, i):
                pe.wait_ge(pscaled, p_ * NT + (min(i, NT - 1) + 1))
                if i < NT:
                    base = 0 if i % 2 else BANK
                    for j in range(i + 1):
                        s = S_TILES[j + 1][0]
                        t = pe.transpose(ax[1][:, base + j * P:base + (j + 1) * P], PR[:, i, s:s + P], ident[:, :])
                else:
                    for j in range(NT):
                        t = pe.transpose(ax[0][0:META, j * P:(j + 1) * P], PR[:, j, 0:META], ident[:, :])
                t.then_inc(ptr_done, 1)

            def head_b1(h, proj, attend, p_, first=False):
                b = h * B1_PER + (B1_0 + 1)
                q0 = B1_0 + 1
                if proj:
                    if not first:
                        pe.wait_ge(ln4_ready, h * 2 - 1)
                    blockmm(b, q0 % 2, mm[0], REAL)
                if attend:
                    pe.wait_ge(hat_ready, p_ * 2 + 2)
                    pe.wait_ge(vn4_ev, p_ * 2 + 2)
                    pe.wait_ge(ln4_ready, p_ * 2 + 2)
                    for i in range(3):
                        scores(p_, i)
                if proj:
                    if first:
                        pe.wait_ge(f_row, 1)
                    else:
                        pe.wait_ge(gate4_ready, h)
                    blockmm(b + 1, (q0 + 1) % 2, mm[1])
                if attend:
                    pe.wait_ge(sadd, p_ * NT + 2)
                    scores(p_, 3)
                    transpose_p(p_, 0)
                if proj:
                    pe.wait_ge(sq4_ready, h * 2 + 1)
                    blockmm(b + 2, q0 % 2, mm[0])
                if attend:
                    pe.wait_ge(sadd, p_ * NT + 4)
                    transpose_p(p_, 1)
                    pe.wait_ge(pt_ev, p_ * (NT + 1) + 1)
                    transpose_p(p_, 2)
                    pe.wait_ge(pt_ev, p_ * (NT + 1) + 2)
                    transpose_p(p_, 3)
                    transpose_p(p_, NT)
                if proj:
                    pe.wait_ge(sq4_ready, h * 2 + 2)
                    blockmm(b + 3, (q0 + 1) % 2, mm[1], REAL)
                    pe.wait_ge(qkv4_ev, h * 3 + 3)
                    full_sum(mm[0], sq[1], HT).then_inc(sum4_done, 1)
                    if attend:
                        pe.wait_ge(pt_ev, p_ * (NT + 1) + (NT + 1))
                    pe.matmul(ax[0][:, 0:SEQ], ones[:, :], sq[0][:, 0:SEQ], start=True, stop=True).then_inc(sum4_done, 1)
                if attend:
                    pe.wait_ge(pt_ev, p_ * (NT + 1) + (NT + 1))
                    o = ax[1][:, BANK:BANK + SEQ]
                    pe.matmul(o, vm4[:, :], PTm[:, :], start=True, stop=False)
                    for i in range(NT):
                        for j in range(i + 1):
                            m = pe.matmul(o[:, i * P:(i + 1) * P], vn4[:, j, :], PTr[:, i, j * P:(j + 1) * P],
                                          start=False, stop=i == j == NT - 1)
                    m.then_inc(pv4_done, 1)
                if proj:
                    for j in range(NT):
                        s = S_TILES[j + 1][0]
                        t = pe.transpose(ax[1][:, j * P:(j + 1) * P], VT[:, s:s + P], ident[:, :])
                    t.then_inc(vtr4, 1)
                    pe.transpose(ax[0][0:META, BANK:BANK + P], VT[:, 0:META], ident[:, :]).then_inc(vtr4, 1)

            head_b1(0, True, False, 0, True)
            with pe.Fori(1, BH) as h:
                head_b1(h, True, True, h - 1)
            head_b1(BH, False, True, BH - 1)

            pe.wait_ge(y4_ready, BH)
            out_blocks(B2_0, 2 * KT, PACKED, 4 * KT, 2 * KT)
            pe.wait_ge(ln_ready, AH + 3)
            for n in range(NT * KT // CT):
                i, jg = n % NT, n // NT
                pe.wait_ge(hn_ready, (jg + 1) * CT)
                if n >= 2:
                    pe.wait_ge(o_ready, n - 1)
                for c in range(CT):
                    t = pe.transpose(ax[n % 2][:, c * P:(c + 1) * P],
                                     hT5[:, jg * CT + c, META + i * P:META + (i + 1) * P], ident[:, :])
                t.then_inc(out_tr, 1)


_INS = ['x', 'meta_tokens', 'a_norm', 'a_w_in', 'a_conv_w', 'a_conv_b', 'a_w_q', 'a_w_k', 'a_w_v', 'a_w_gate',
        'a_b_gate', 'a_head_norm', 'a_skip', 'a_w_out', 'b_norm', 'b_w_in', 'b_b_f', 'b_q_norm', 'b_k_norm',
        'b_w_out', 'final_norm']


def kernel(**inputs):
    import numpy as _np
    import concourse.bacc as _bacc
    from concourse import mybir as _mybir
    from concourse.bass_utils import run_bass_kernel_spmd as _run

    nc = _bacc.Bacc("TRN2", target_bir_lowering=False, num_devices=1)
    arrays, args = {}, []
    for name in _INS:
        a = _np.ascontiguousarray(inputs[name])
        arrays[f"in_{name}_dram"] = a
        args.append(nc.dram_tensor(f"in_{name}_dram", a.shape, _mybir.dt.from_np(a.dtype), kind="ExternalInput").ap())
    shape = tuple(inputs["x"].shape)
    args.append(nc.dram_tensor("out_0_dram", shape, _mybir.dt.from_np(_np.dtype("float32")), kind="ExternalOutput").ap())
    hybrid_trunk(nc, *args)
    r = _run(nc, [arrays], core_ids=[0])
    return r.results[0]["out_0_dram"]
```

```python
from contextlib import ExitStack

import concourse.bass as bass
from concourse import mybir

F32 = mybir.dt.float32
F32R = mybir.dt.float32r
ALU = mybir.AluOpType
ACT = mybir.ActivationFunctionType
AX_X = mybir.AxisListType.X
ds = bass.ds

P = 128
BANK = 512


def hybrid_trunk(nc, x, meta_tokens, a_norm, a_w_in, a_conv_w, a_conv_b, a_w_q, a_w_k, a_w_v,
                 a_w_gate, a_b_gate, a_head_norm, a_skip, a_w_out, b_norm, b_w_in, b_b_f,
                 b_q_norm, b_k_norm, b_w_out, final_norm, out):
    _, SEQ, D = x.shape
    META = meta_tokens.shape[0]
    T = META + SEQ
    HT = T // 2
    HS = SEQ // 2
    KT = D // P
    AI = a_w_in.shape[2] // 3
    AH, DV, DQK = a_w_q.shape[1], a_w_q.shape[2], a_w_q.shape[3]
    CT = DV // P
    QT = DQK // P
    NG = a_w_gate.shape[2]
    BH, BD = b_b_f.shape[1], b_q_norm.shape[1]
    TAPS = a_conv_w.shape[1]
    H_PARTS = 4
    EPS = 1e-6
    S_TILES = [(0, META)] + [(META + P * i, P) for i in range(SEQ // P)]
    NS = len(S_TILES)
    NT = SEQ // P
    E_OFF = [sum(T - s for s, _ in S_TILES[:j]) for j in range(NS + 1)]
    assert (T, KT, CT, QT, BD, NG) == (528, 16, 4, 2, P, 2 * AH) and AI == AH * DV

    A1_PER, A2_PER, B1_PER = CT + 2, 2 * CT, 4
    A2_0 = AH * A1_PER
    A3_0 = A2_0 + AH * A2_PER
    B1_0 = A3_0 + 2 * KT
    B2_0 = B1_0 + 1 + BH * B1_PER
    BLOCKS = B2_0 + KT

    def xm_block(h, c):
        if isinstance(h, int) and h == 0:
            return c
        return CT + A1_PER * (h - 1) + (0 if c == 0 else 2 + c)

    O0_BLOCK = CT + A1_PER * (AH - 1)

    def qkv_block(h):
        return CT + A1_PER * h + 1

    FT = AI // P
    C_CW, C_CB = 0, TAPS * FT
    C_HN, C_SK = C_CB + FT, C_CB + 2 * FT
    C_AN = C_SK + FT
    C_BN = C_AN + KT
    C_FN = C_BN + KT
    C_QN, C_KN = C_FN + KT, C_FN + KT + 1
    NPAR = C_KN + 1

    with ExitStack() as ctx:
        def sb(name, shape, dt=F32, scope=ctx):
            return scope.enter_context(nc.sbuf_tensor(name, shape, dt))

        def sb_split(name, shape, scope):
            whole = ExitStack()
            raw = sb(name + "_whole", shape, scope=whole)
            whole.close()
            return raw, sb(name + "_low", shape, F32R, scope)

        def sem(name):
            return ctx.enter_context(nc.semaphore(name))

        def dram(name, shape):
            return nc.dram_tensor(name, shape, F32).ap()

        h_d = dram("h_scratch", [P, KT * T])
        qk_d = dram("qk_scratch", [AH, P, 2 * QT * T])
        v_d = dram("v_scratch", [AH, P, NS * DV])
        xc_d = dram("xc_scratch", [P, FT * T])
        y_d = dram("y_scratch", [P, FT * T])
        negm_d = dram("negm_scratch", [AH, T])
        floor_d = dram("floor_scratch", [AH, T])
        negc_d = dram("negc_scratch", [BH, T])

        XH = sb("xh", [P, KT, T], F32R)
        XL = sb("xl", [P, KT, T], F32R)
        w_raw = [sb(f"w_raw{i}", [P, KT * P]) for i in range(2)]
        w_hi = [sb(f"w_hi{i}", [P, KT * P], F32R) for i in range(2)]
        w_lo = [sb(f"w_lo{i}", [P, KT * P], F32R) for i in range(2)]
        ident = sb("ident", [P, P])
        ones = sb("ones", [P, P])
        ones_r = sb("ones_r", [P, P], F32R)
        causal01 = sb("causal01", [P, P])
        par = sb("par", [P, NPAR])
        rstd = sb("rstd", [P, T])
        rtmp = sb("rtmp", [P, T])
        eps_t = sb("eps", [P, 1])
        sq = [sb(f"sq{i}", [P, T]) for i in range(2)]
        causal_add = sb("causal_add", [P, P])
        bf = sb("bf", [BH, 1])

        s0 = ExitStack()
        hT0 = sb("h0", [P, KT, T], scope=s0)
        x_nat = sb("x_nat", [P, NT, D], scope=s0)
        meta_nat = sb("meta_nat", [META, D], scope=s0)
        par_rows = sb("par_rows", [P, 3, P], scope=s0)
        xt0 = [sb(f"xt0{i}", [P, T], scope=s0) for i in range(2)]
        diag0 = sb("diag0", [P, NT + 1, P], scope=s0)
        stat0 = sb("stat0", [P, 3, NT + 1], scope=s0)
        s0.close()
        s1 = ExitStack()
        xmh = sb("xmh", [P, CT, T], F32R, s1)
        xml = sb("xml", [P, CT, T], F32R, s1)
        xch = sb("xch", [P, CT, T], F32R, s1)
        xcl = sb("xcl", [P, CT, T], F32R, s1)
        qkv = sb("qkv", [P, 2 * QT + CT, T], scope=s1)
        vn1 = sb("vn1", [P, NS, DV], scope=s1)
        xm_pad = [sb(f"xm_pad{i}", [P, TAPS - 1 + T], scope=s1) for i in range(2)]
        conv = [sb(f"conv{i}", [P, T], scope=s1) for i in range(2)]
        xc2 = [sb(f"xc2{i}", [P, T], scope=s1) for i in range(2)]
        th1 = sb("th1", [P, T], scope=s1)
        wg = sb("wg", [P, 2 * QT + CT, NG], scope=s1)
        gacc = sb("gacc", [NG, T], scope=s1)
        bg = sb("bg", [NG, 1], scope=s1)
        s1.close()
        s2 = ExitStack()
        qkh = sb("qkh", [P, 2 * QT, T], F32R, s2)
        qk2, qkl = sb_split("qk", [P, 2 * QT, T], s2)
        vh = sb("vh", [P, NS, DV], F32R, s2)
        v2, vl = sb_split("v", [P, NS, DV], s2)
        OT = sb("ot", [P, CT, T], scope=s2)
        aT = sb("aT", [P, NS, AH], scope=s2)
        s2g = ExitStack()
        gr = {n: sb(f"gr_{n}", [AH, T], scope=s2g)
              for n in ("ig", "f", "abs", "e", "lf", "B", "a", "M", "negm", "m", "floor", "one")}
        s2g.close()
        EW, EWl = sb_split("w", [P, E_OFF[NS]], s2)
        EWh = sb("ewh", [P, E_OFF[NS]], F32R, s2)
        xcl2 = sb("xc_load", [P, CT, T], scope=s2)
        yb = [sb(f"yb{i}", [P, T], scope=s2) for i in range(2)]
        th2 = [sb(f"th2{i}", [P, T], scope=s2) for i in range(2)]
        negm_b = sb("negm_b", [P, T], scope=s2)
        floor_b = sb("floor_b", [P, T], scope=s2)
        dn = sb("dn", [P, T], scope=s2)
        s2.close()
        s3 = ExitStack()
        y_in = sb("y_in", [P, KT, T], scope=s3)
        hT3 = sb("h3", [P, KT, T], scope=s3)
        xt3 = [sb(f"xt3{i}", [P, T], scope=s3) for i in range(2)]
        s3.close()
        s4 = ExitStack()
        Y = sb("y", [P, BH, SEQ], scope=s4)
        QR = sb("q_raw", [P, SEQ], scope=s4)
        KR = sb("k_raw", [P, T], scope=s4)
        VT = sb("v_t", [P, T], scope=s4)
        rq = sb("rq", [P, SEQ], scope=s4)
        QH = sb("q_hat", [P, SEQ], scope=s4)
        KH = sb("k_hat", [P, T], scope=s4)
        vn4 = sb("vn4", [P, NT, BD], scope=s4)
        vm4 = sb("vm4", [META, BD], scope=s4)
        SS = [sb(f"scores{i}", [P, T], scope=s4) for i in range(2)]
        PR = sb("probs", [P, NT, T], scope=s4)
        PTr = sb("probs_t", [P, NT, SEQ], scope=s4)
        PTm = sb("probs_t_meta", [META, SEQ], scope=s4)
        negc_b = sb("negc_b", [P, T], scope=s4)
        th4 = sb("th4", [P, SEQ], scope=s4)
        s_max, s_neg, s_sum, s_inv = (sb(f"s_{n}", [P, NT], scope=s4) for n in ("max", "neg", "sum", "inv"))
        s4.close()
        s4g = ExitStack()
        fg = {n: sb(f"fg_{n}", [BH, T], scope=s4g) for n in ("f", "abs", "e", "l1", "lf", "c", "negc", "one")}
        s4g.close()
        s5 = ExitStack()
        sb("y_kept", [P, BH * SEQ], scope=s5)
        hT5 = sb("h5", [P, KT, T], scope=s5)
        hg = [sb(f"hg{i}", [P, SEQ], scope=s5) for i in range(2)]
        stat5 = sb("stat5", [P, 2, NT], scope=s5)
        s5.close()
        o_nat = sb("o_nat", [P, NT, D], scope=s5)
        s5.close()

        mm = [ctx.enter_context(nc.psum_tensor(f"mm{i}", [P, 2 * BANK], F32)) for i in range(2)]
        ax = [ctx.enter_context(nc.psum_tensor(f"ax{i}", [P, 2 * BANK], F32)) for i in range(2)]

        def halves(ps, n=HT, rows=P):
            return ps[0:rows, :].rearrange("p (a n) -> p a n", a=2)[:, :, 0:n]

        def two(ap):
            return ap.rearrange("p (a n) -> p a n", a=2)

        X0 = BANK - META
        SCORES_AT = ((ax[0], X0), (ax[1], 0), (ax[1], BANK), (ax[0], 0), (ax[0], BANK))

        w_raw_ready = [sem(f"w_raw_ready{i}") for i in range(2)]
        wk_raw_ready = sem("wk_raw_ready")
        w_hi_ready, w_lo_ready, blk_done = sem("w_hi_ready"), sem("w_lo_ready"), sem("blk_done")
        meta_loaded = sem("meta_loaded")
        x_loaded = [sem(f"x_loaded{i}") for i in range(NT)]
        ones_ready, stat0_ready, diag0_ready, bcast0_done, rstd0_ready = (sem(n) for n in (
            "ones_ready", "stat0_ready", "diag0_ready", "bcast0_done", "rstd0_ready"))
        qk_hi, qk_lo, v_hi, v_lo, w2_hi, w2_lo, og_ready, ss2_ready, ss_ready = (sem(n) for n in (
            "qk_hi", "qk_lo", "v_hi", "v_lo", "w2_hi", "w2_lo", "og_ready", "ss2_ready", "ss_ready"))
        (par_loaded, const_ready, ident0, par_tr, par_ready, x_tr, h_copied, h_stored, h_loaded,
         sq_ready, sumsq_done, ln_ready, rstd_ready, xt_ready, xh_ready, xl_ready) = (sem(n) for n in (
            "par_loaded", "const_ready", "ident0", "par_tr", "par_ready", "x_tr", "h_copied",
            "h_stored", "h_loaded", "sq_ready", "sumsq_done", "ln_ready", "rstd_ready", "xt_ready",
            "xh_ready", "xl_ready"))
        (pad_zero, xm_raw, xm_hi, cv_aff, xm_lo, taps, th1_ready, xc2_ready, xc_hi, xc_lo, qkv_mm, qkv_ev,
         gate_mm, gacc_ready, wg_loaded, v_tr, vn1_ev, qk_stored, v_stored) = (sem(n) for n in (
            "pad_zero", "xm_raw", "xm_hi", "cv_aff", "xm_lo", "taps", "th1_ready", "xc2_ready", "xc_hi",
            "xc_lo", "qkv_mm", "qkv_ev", "gate_mm", "gacc_ready", "wg_loaded", "v_tr", "vn1_ev",
            "qk_stored", "v_stored"))
        xc_stored = [sem(f"xc_stored{i}") for i in range(2)]
        (gb_ready, gsel_done, grow, gexp, a_tr, aT_ready, grow_stored, qk_loaded, v_loaded, negm_loaded,
         floor_loaded, xc_loaded, e_arg, e_ready, e_diag, sc_done, w_ready, ot_ready, pv_done, dn_ready,
         rd_ready, g_ready, sqg_ready, sumg_done, th2_ready, mix_ready, gate2_ready, y_ready) = (
            sem(n) for n in (
            "gb_ready", "gsel_done", "grow", "gexp", "a_tr", "aT_ready", "grow_stored", "qk_loaded",
            "v_loaded", "negm_loaded", "floor_loaded", "xc_loaded", "e_arg", "e_ready", "e_diag", "sc_done",
            "w_ready", "ot_ready", "pv_done", "dn_ready", "rd_ready", "g_ready", "sqg_ready", "sumg_done",
            "th2_ready", "mix_ready", "gate2_ready", "y_ready"))
        y_stored = [sem(f"y_stored{i}") for i in range(2)]
        y_loaded, h_acc, h_stored2, h_loaded2 = (sem(n) for n in ("y_loaded", "h_acc", "h_stored2", "h_loaded2"))
        (f_row, fexp, negc_stored, negc_loaded, qkv4_ev, sq4_ready, sum4_done, ln4_ready, r4_ready, hat_ready,
         vtr4, vn4_ev, s4_done, sadd, smask, smax, sneg, pexp, sinv, pscaled, ptr_done, pt_ev, pv4_done,
         th4_ready, gate4_ready, y4_ready) = (sem(n) for n in (
            "f_row", "fexp", "negc_stored", "negc_loaded", "qkv4_ev", "sq4_ready", "sum4_done", "ln4_ready",
            "r4_ready", "hat_ready", "vtr4", "vn4_ev", "s4_done", "sadd", "smask", "smax", "sneg", "pexp",
            "sinv", "pscaled", "ptr_done", "pt_ev", "pv4_done", "th4_ready", "gate4_ready", "y4_ready"))
        hg_ready, out_tr, raw_ready, stat5_ready, o_even, o_odd, out_stored = (sem(n) for n in (
            "hg_ready", "out_tr", "raw_ready", "stat5_ready", "o_even", "o_odd", "out_stored"))

        w_in_a = a_w_in[0].rearrange("(k p) m -> p k m", p=P)
        w_in_b = b_w_in[0].rearrange("(k p) m -> p k m", p=P)
        w_out_a = a_w_out[0].rearrange("(f k p) m -> f p k m", p=P, k=KT)
        w_out_b = b_w_out[0].rearrange("(k p) m -> p k m", p=P)
        w_q = a_w_q[0].rearrange("h (k p) m -> p (h k) m", p=P)
        w_k = a_w_k[0].rearrange("h (k p) m -> p (h k) m", p=P)
        w_v = a_w_v[0].rearrange("h (k p) m -> p (h k) m", p=P)
        w_g = a_w_gate[0].rearrange("(r p) g -> p r g", p=P)
        Z_B = 3 * BH * BD + BH

        def wait(eng, semaphore, value):
            if not (isinstance(value, int) and value <= 0):
                eng.wait_ge(semaphore, value)

        def flat(t):
            return t.rearrange("p a b -> p (a b)")

        block = ctx.enter_context(nc.Block())

        @block.sync
        def _(sp):
            def load(b, par_, src, cols=P, tiles=KT, at=0, done=None):
                if not (isinstance(b, int) and b < 2):
                    sp.wait_ge(w_lo_ready, b - 1)
                full = w_raw[par_][:, :].rearrange("p (k m) -> p k m", k=tiles)
                sp.dma_start(full[:, :, at:at + cols], src).then_inc(done or w_raw_ready[par_], 16)

            def load_xm(h, c):
                load(xm_block(h, c), c % 2, w_in_a[:, :, ds(h * DV + c * P, P)])

            def load_qkv(h, par_):
                b = qkv_block(h)
                load(b, par_, w_k[:, ds(h * CT, CT), :], DQK, CT, DQK, wk_raw_ready)
                sp.wait_ge(wk_raw_ready, h * 16 + 16)
                load(b, par_, w_q[:, ds(h * CT, CT), :], DQK, CT)
                load(b + 1, 1 - par_, w_v[:, ds(h * CT, CT), :], DV, CT)
                if not (isinstance(h, int) and h == 0):
                    sp.wait_ge(gate_mm, h)
                for r, n, at in ((0, QT, 0), (AH * QT, QT, QT), (2 * AH * QT, CT, 2 * QT)):
                    sp.dma_start(wg[:, at:at + n, :], w_g[:, ds(h * n + r, n), :]).then_inc(wg_loaded, 16)

            sp.dma_start(meta_nat[:, :], meta_tokens).then_inc(meta_loaded, 16)
            for i in range(NT):
                if i == NT // 2:
                    load_xm(0, 0)
                sp.dma_start(x_nat[:, i, :], x[0, i * P:(i + 1) * P, :]).then_inc(x_loaded[i], 16)
            for c in range(1, CT):
                load_xm(0, c)
            sp.wait_ge(xl_ready, KT)
            sp.wait_ge(h_stored, 16 * H_PARTS)

            def load_head_a1(h):
                load_xm(h, 0)
                load_qkv(h - 1, 1)
                for c in range(1, CT):
                    load_xm(h, c)

            def load_a2(h, k, b):
                part = (1 + k // CT) * AI + k % CT * P
                load(b, k % 2, w_in_a[:, :, ds(h * DV + part, P)])

            load_head_a1(1)
            with sp.Fori(2, AH) as h:
                load_head_a1(h)
            load_a2(0, 0, O0_BLOCK)
            load_qkv(AH - 1, 1)
            for k in range(1, A2_PER):
                load_a2(0, k, A2_0 + k)
            with sp.Fori(1, AH) as h:
                for k in range(A2_PER):
                    load_a2(h, k, h * A2_PER + (A2_0 + k))
            for f in range(2):
                with sp.Fori(0, KT // 2) as i:
                    for k in range(2):
                        load(i * 2 + (A3_0 + f * KT + k), k, w_out_a[f][:, :, ds(i * (2 * P) + k * P, P)])
            load(B1_0, B1_0 % 2, w_in_b[:, :, 3 * BH * BD:3 * BH * BD + P])
            with sp.Fori(0, BH) as h:
                for k in range(B1_PER):
                    part = (0, BH * BD, 2 * BH * BD, Z_B)[k]
                    load(h * B1_PER + (B1_0 + 1 + k), (B1_0 + 1 + k) % 2, w_in_b[:, :, ds(h * BD + part, P)])
            with sp.Fori(0, KT // 2) as i:
                for k in range(2):
                    load(i * 2 + (B2_0 + k), (B2_0 + k) % 2, w_out_b[:, :, ds(i * (2 * P) + k * P, P)])
            for i in range(NT):
                sp.wait_ge((o_even, o_odd)[i % 2], i // 2 + 1)
                sp.dma_start(out[0, i * P:(i + 1) * P, :], o_nat[:, i, :]).then_inc(out_stored, 16)
            sp.wait_ge(out_stored, 16 * NT)

        @block.gpsimd
        def _(pool):
            pool.memset(ident[:, :], 0.0).then_inc(ident0, 1)
            pool.memset(ones[:, :], 1.0).then_inc(ident0, 1)
            pool.memset(causal01[:, :], 1.0).then_inc(ident0, 1)
            pool.memset(causal_add[:, :], 0.0).then_inc(ident0, 1)
            pool.memset(eps_t[:, :], EPS).then_inc(ident0, 1)
            pool.wait_ge(ident0, 5)
            pool.affine_select(out=ident[:, :], in_=ident[:, :], compare_op=ALU.not_equal, fill=1.0, base=0,
                               pattern=[[-1, P]], channel_multiplier=1).then_inc(const_ready, 1)
            pool.affine_select(out=causal01[:, :], in_=causal01[:, :], compare_op=ALU.is_ge, fill=0.0, base=0,
                               pattern=[[1, P]], channel_multiplier=-1).then_inc(const_ready, 1)
            pool.affine_select(out=causal_add[:, :], in_=causal_add[:, :], compare_op=ALU.is_ge, fill=-1e30,
                               base=0, pattern=[[-1, P]], channel_multiplier=1).then_inc(const_ready, 1)
            for i in range(H_PARTS):
                w = KT // H_PARTS
                pool.wait_ge(h_copied, (i + 1) * w)
                pool.dma_start(h_d[:, i * w * T:(i + 1) * w * T],
                               flat(hT0[:, i * w:(i + 1) * w, :])).then_inc(h_stored, 16)

            def store_xc(h, c):
                pool.wait_ge(xc2_ready, h * CT + (c + 1))
                pool.dma_start(xc_d[:, ds(h * (CT * T) + c * T, T)], xc2[c % 2][:, :]).then_inc(xc_stored[c % 2], 16)

            def store_qkv(h):
                pool.wait_ge(qkv_ev, h * (2 * QT + CT) + 2 * QT)
                pool.dma_start(qk_d[ds(h, 1)].rearrange("a p n -> (a p) n"),
                               flat(qkv[:, 0:2 * QT, :])).then_inc(qk_stored, 16)
                pool.wait_ge(vn1_ev, h * NS + NS)
                dst = v_d[ds(h, 1)].rearrange("a p n -> (a p) n")
                pool.dma_start(dst[0:META, 0:DV], vn1[0:META, 0, :]).then_inc(v_stored, 16)
                pool.dma_start(dst[:, DV:NS * DV], flat(vn1[:, 1:NS, :])).then_inc(v_stored, 16)

            for c in range(CT):
                store_xc(0, c)
            store_qkv(0)
            for c in range(CT):
                store_xc(1, c)
            with pool.Fori(2, AH) as h:
                store_qkv(h - 1)
                for c in range(CT):
                    store_xc(h, c)
            store_qkv(AH - 1)

            def load_negm(h):
                pool.dma_start(negm_b[:, :], negm_d[ds(h, 1), :].broadcast_to([P, T])).then_inc(negm_loaded, 16)

            def load_qk(h):
                pool.dma_start(flat(qk2[:, :, :]),
                               qk_d[ds(h, 1)].rearrange("a p n -> (a p) n")).then_inc(qk_loaded, 16)

            def load_v(h):
                src = v_d[ds(h, 1)].rearrange("a p n -> (a p) n")
                pool.dma_start(v2[0:META, 0, :], src[0:META, 0:DV]).then_inc(v_loaded, 16)
                pool.dma_start(flat(v2[:, 1:NS, :]), src[:, DV:NS * DV]).then_inc(v_loaded, 16)

            def load_floor(h):
                pool.dma_start(floor_b[:, :], floor_d[ds(h, 1), :].broadcast_to([P, T])).then_inc(floor_loaded, 16)

            def load_xc(h):
                pool.dma_start(flat(xcl2[:, :, :]), xc_d[:, ds(h * (CT * T), CT * T)]).then_inc(xc_loaded, 16)

            def sum_squares_a2(h):
                for c in range(1, CT):
                    pool.wait_ge(sqg_ready, h * CT + (c + 1))
                    if c > 1:
                        pool.wait_ge(ss2_ready, h * (CT - 1) + (c - 1))
                    pool.tensor_tensor(rtmp[:, :], sq[0][:, :] if c == 1 else rtmp[:, :], sq[c % 2][:, :],
                                       ALU.add).then_inc(ss2_ready, 1)

            def store_y(h):
                for c in range(CT):
                    pool.wait_ge(y_ready, h * CT + (c + 1))
                    pool.dma_start(y_d[:, ds(h * (CT * T) + c * T, T)], yb[c % 2][:, :]).then_inc(y_stored[c % 2], 16)

            def sum_squares(r, w):
                pool.memset(rtmp[:, 0:w], 0.0).then_inc(ss_ready, 2)
                with pool.Fori(0, KT // 2) as i:
                    for k in range(2):
                        pool.wait_ge(sq_ready, i * 2 + (r * KT + k + 1))
                        pool.wait_ge(ss_ready, i * 2 + (r * (KT + 2) + 2 + k))
                        pool.tensor_tensor(rtmp[:, 0:w], rtmp[:, 0:w], sq[k][:, 0:w], ALU.add).then_inc(ss_ready, 1)

            pool.wait_ge(qk_stored, 16 * AH)
            pool.wait_ge(v_stored, 32 * AH)
            for i in range(2):
                pool.wait_ge(xc_stored[i], 16 * AH * CT // 2)
            pool.wait_ge(gate_mm, AH)
            load_qk(0)
            load_v(0)
            pool.wait_ge(grow, 12)
            pool.wait_ge(gexp, 3)
            pool.dma_start(negm_d, gr["negm"][:, :]).then_inc(grow_stored, 16)
            pool.dma_start(floor_d, gr["floor"][:, :]).then_inc(grow_stored, 16)
            pool.wait_ge(grow_stored, 32)
            load_negm(0)
            load_floor(0)
            load_xc(0)
            with pool.Fori(0, AH - 1) as h:
                pool.wait_ge(e_arg, h * NS + NS)
                load_negm(h + 1)
                pool.wait_ge(sc_done, h * NS + NS)
                load_qk(h + 1)
                pool.wait_ge(pv_done, h * (1 + CT) + (1 + CT))
                load_v(h + 1)
                load_floor(h + 1)
                sum_squares_a2(h)
                store_y(h)
                load_xc(h + 1)
            for i in range(2):
                pool.wait_ge(y_stored[i], 16 * AH * CT // 4)
            pool.wait_ge(pv_done, (1 + CT) * AH)
            pool.dma_start(flat(y_in[:, :, :]), y_d[:, 0:KT * T]).then_inc(y_loaded, 16)
            sum_squares_a2(AH - 1)
            store_y(AH - 1)
            for i in range(2):
                pool.wait_ge(y_stored[i], 16 * AH * CT // 2)
            pool.dma_start(flat(hT3[:, :, :]), h_d).then_inc(h_loaded, 16)
            pool.wait_ge(xl_ready, 2 * KT)
            pool.dma_start(flat(y_in[:, :, :]), y_d[:, KT * T:2 * KT * T]).then_inc(y_loaded, 16)
            pool.wait_ge(rstd_ready, AH)
            sum_squares(0, T)
            pool.wait_ge(h_acc, 2 * KT)
            pool.dma_start(h_d, flat(hT3[:, :, :])).then_inc(h_stored2, 16)

            pool.wait_ge(f_row, 6)
            pool.dma_start(negc_d, fg["negc"][:, :]).then_inc(negc_stored, 16)
            pool.wait_ge(negc_stored, 16)
            pool.dma_start(negc_b[:, :], negc_d[0:1, :].broadcast_to([P, T])).then_inc(negc_loaded, 16)
            with pool.Fori(1, BH) as h:
                pool.wait_ge(sadd, h * NT)
                pool.dma_start(negc_b[:, :], negc_d[ds(h, 1), :].broadcast_to([P, T])).then_inc(negc_loaded, 16)
            pool.wait_ge(y4_ready, BH)
            pool.dma_start(flat(hT5[:, :, :]), h_d).then_inc(h_loaded2, 16)
            pool.wait_ge(r4_ready, 2 * BH)
            sum_squares(1, SEQ)

        @block.scalar
        def _(act):
            def round_w(b, par_):
                if isinstance(b, int) and b >= BLOCKS:
                    return
                act.wait_ge(w_raw_ready[par_], b * 8 + (16 - 8 * par_))
                if not (isinstance(b, int) and b < 2):
                    act.wait_ge(blk_done, b - 1)
                act.activation(w_hi[par_][:, :], w_raw[par_][:, :], ACT.Copy).then_inc(w_hi_ready, 1)

            def inv_sqrt(src, dst, scale, tmp, n, view, ln, done):
                act.activation(view(tmp), src, ACT.Ln, bias=eps_t[:, 0:1], scale=scale).then_inc(ln, 1)
                act.wait_ge(ln, n)
                act.activation(dst, tmp, ACT.Exp, scale=-0.5).then_inc(done, 1)

            cw = a_conv_w[0].rearrange("c (j p) -> (c j) p", p=P)
            act.dma_start(par_rows[:, 0, :], cw).then_inc(par_loaded, 16)
            rows = [(a_conv_b[0], FT, 1, 0), (a_head_norm[0], FT, 1, FT), (a_skip[0], FT, 1, 2 * FT),
                    (a_norm[0], KT, 1, 3 * FT), (b_norm[0], KT, 1, 3 * FT + KT), (final_norm, KT, 2, 0),
                    (b_q_norm[0], 1, 2, KT), (b_k_norm[0], 1, 2, KT + 1)]
            for src, n, t, at in rows:
                act.dma_start(par_rows[at:at + n, t, :],
                              src.rearrange("(j p) -> j p", p=P)).then_inc(par_loaded, 16)
            act.dma_start(bf[:, :], b_b_f[0].rearrange("(g a) -> g a", a=1)).then_inc(par_loaded, 16)
            act.wait_ge(ident0, 5)
            act.activation(ones_r[:, :], ones[:, :], ACT.Copy).then_inc(ones_ready, 1)
            act.wait_ge(meta_loaded, 16)
            act.activation(flat(hT0[:, :, :])[0:META, 0:D], meta_nat[:, :], ACT.Square,
                           accum_out=stat0[0:META, 0, NT:NT + 1]).then_inc(stat0_ready, 1)
            act.wait_ge(stat0_ready, 1)
            for i in range(NT):
                if i == NT // 2:
                    round_w(0, 0)
                act.wait_ge(x_loaded[i], 16)
                act.activation(flat(hT0[:, :, :])[:, i * D:(i + 1) * D], x_nat[:, i, :], ACT.Square,
                               accum_out=stat0[:, 0, i:i + 1]).then_inc(stat0_ready, 1)
            act.wait_ge(stat0_ready, NT + 1)
            for r, c0, c1 in ((P, 0, NT), (META, NT, NT + 1)):
                act.activation(stat0[0:r, 1, c0:c1], stat0[0:r, 0, c0:c1], ACT.Ln, bias=eps_t[0:r, 0:1],
                               scale=1.0 / D).then_inc(stat0_ready, 1)
            act.wait_ge(stat0_ready, NT + 3)
            for r, c0, c1 in ((P, 0, NT), (META, NT, NT + 1)):
                act.activation(stat0[0:r, 2, c0:c1], stat0[0:r, 1, c0:c1], ACT.Exp, scale=-0.5).then_inc(stat0_ready, 1)

            def copy_h(j):
                act.wait_ge(x_tr, j + 1)
                act.activation(hT0[:, j, :], ax[j % 2][:, X0:2 * BANK], ACT.Copy).then_inc(h_copied, 1)

            copy_h(0)
            copy_h(1)
            round_w(1, 1)
            for j in range(KT):
                act.wait_ge(xt_ready, j + 1)
                act.activation(XH[:, j, :], xt0[j % 2][:, :], ACT.Copy).then_inc(xh_ready, 1)
                if j + 2 < KT:
                    copy_h(j + 2)

            act.wait_ge(xl_ready, KT)
            act.wait_ge(h_stored, 16 * H_PARTS)
            act.dma_start(bg[:, :], a_b_gate[0].rearrange("(g a) -> g a", a=1)).then_inc(par_loaded, 16)

            def conv_tile(h, c, n, npar):
                b = xm_block(h, c)
                e = h * CT + c
                p = c % 2
                src = halves(mm[p])
                act.wait_ge(blk_done, b + 1)
                if not (isinstance(h, int) and h == 0 and c < 2):
                    act.wait_ge(taps, e * 3 - 3)
                act.activation(two(xm_pad[p][:, TAPS - 1:]), src, ACT.Copy).then_inc(xm_raw, 1)
                act.activation(two(xmh[:, c, :]), src, ACT.Copy).then_inc(xm_hi, 1)
                if not (isinstance(h, int) and h == 0 and c < 2):
                    act.wait_ge(xc2_ready, e - 1)
                act.activation(two(conv[p][:, :]), src, ACT.Identity,
                               bias=par[:, ds(h * CT + (C_CB + c), 1)],
                               scale=par[:, ds(h * CT + (C_CW + (TAPS - 1) * FT + c), 1)]).then_inc(cv_aff, 1)
                round_w(n, npar)
                act.wait_ge(taps, e * 3 + 3)
                act.activation(th1[:, :], conv[p][:, :], ACT.Tanh, scale=0.5).then_inc(th1_ready, 1)
                act.wait_ge(xc2_ready, e + 1)
                act.activation(xch[:, c, :], xc2[p][:, :], ACT.Copy, scale=0.5).then_inc(xc_hi, 1)

            def evacuate_qkv(h, b):
                if not (isinstance(h, int) and h == 0):
                    act.wait_ge(qk_stored, h * 16)
                for j in range(2 * QT + CT):
                    if j == 2 * QT and not (isinstance(h, int) and h == 0):
                        act.wait_ge(v_tr, h * NS)
                        act.wait_ge(gate_mm, h)
                    act.wait_ge(qkv_mm, h * 8 + (j + 1))
                    act.activation(two(qkv[:, j, :]), halves(ax[j % 2]), ACT.Copy).then_inc(qkv_ev, 1)
                    if j == 2 * QT - 1:
                        round_w(b + 2, 1)

            for c in range(CT):
                conv_tile(0, c, c + 2, c % 2)
            act.wait_ge(par_loaded, 16 * 11)

            def head_a1(h):
                b0 = xm_block(h, 0)
                round_w(b0 + 2, 0)
                evacuate_qkv(h - 1, b0 + 1)
                for c in range(CT):
                    conv_tile(h, c, b0 + (4 + c), c % 2)

            head_a1(1)
            with act.Fori(2, AH) as h:
                head_a1(h)
            round_w(O0_BLOCK + 2, 0)
            evacuate_qkv(AH - 1, O0_BLOCK + 1)

            act.wait_ge(v_stored, 32 * AH)
            for i in range(2):
                act.wait_ge(xc_stored[i], 16 * AH * CT // 2)

            def gates():
                act.wait_ge(grow, 3)
                act.activation(gr["e"][:, :], gr["abs"][:, :], ACT.Exp, scale=-1.0).then_inc(gexp, 1)
                act.wait_ge(gexp, 1)
                act.activation(gr["e"][:, :], gr["e"][:, :], ACT.Ln, bias=1.0).then_inc(gexp, 1)
                act.wait_ge(grow, 9)
                act.activation(gr["floor"][:, :], gr["m"][:, :], ACT.Exp, scale=-1.0).then_inc(gexp, 1)

            def round_qk(h):
                act.wait_ge(qk_loaded, h * 16 + 16)
                act.activation(flat(qkh[:, :, :]), flat(qk2[:, :, :]), ACT.Copy).then_inc(qk_hi, 1)

            def round_v(h):
                act.wait_ge(v_loaded, h * 32 + 32)
                act.activation(vh[0:META, 0, :], v2[0:META, 0, :], ACT.Copy).then_inc(v_hi, 1)
                act.activation(flat(vh[:, 1:NS, :]), flat(v2[:, 1:NS, :]), ACT.Copy).then_inc(v_hi, 1)

            def exponentials(h):
                act.wait_ge(e_arg, h * NS + NS)
                for rows, c0, c1 in ((META, 0, T), (P, T, E_OFF[NS])):
                    e = EW[0:rows, c0:c1]
                    act.activation(e, e, ACT.Exp).then_inc(e_ready, 1)

            def round_w2(h, j):
                n = S_TILES[j][1]
                cols = slice(E_OFF[j], E_OFF[j + 1])
                act.wait_ge(w_ready, h * NS + (j + 1))
                act.activation(EWh[0:n, cols], EW[0:n, cols], ACT.Copy).then_inc(w2_hi, 1)

            def o_gate(h, c):
                b = h * A2_PER + A2_0
                act.wait_ge(blk_done, b + (c + 1))
                wait(act, y_ready, h * CT)
                act.activation(two(OT[:, c, :]), halves(mm[c % 2]), ACT.Tanh, scale=0.5).then_inc(ot_ready, 1)
                round_w(b + (c + 2), c % 2)

            def head_a2(h, first=False):
                b = h * A2_PER + A2_0
                if first:
                    o_gate(h, 0)
                    gates()
                    o_gate(h, 1)
                    round_qk(h)
                    round_v(h)
                    exponentials(h)
                else:
                    round_qk(h)
                    o_gate(h, 0)
                    exponentials(h)
                    round_v(h)
                for j in range(3):
                    round_w2(h, j)
                o_gate(h, 2 if first else 1)
                for j in range(3, NS):
                    round_w2(h, j)
                for c in range(3 if first else 2, CT):
                    o_gate(h, c)
                for c in range(CT):
                    act.wait_ge(g_ready, h * CT + (c + 1))
                    if c >= 2:
                        act.wait_ge(ss2_ready, h * (CT - 1) + (c - 1))
                    act.activation(sq[c % 2][:, :], OT[:, c, :], ACT.Square).then_inc(sqg_ready, 1)
                for c in range(CT):
                    k = CT + c
                    if c == 0:
                        round_w(b + (k + 2), 0)
                        act.wait_ge(sumg_done, h + 1)
                        wait(act, y_ready, h * CT)
                        inv_sqrt(halves(ax[0]), rstd[:, :], 0.25 / DV, rtmp[:, :], h + 1, two, ln_ready, rstd_ready)
                    act.wait_ge(blk_done, b + (k + 1))
                    wait(act, y_ready, h * CT + (c - 1))
                    act.activation(two(th2[c % 2][:, :]), halves(mm[k % 2]), ACT.Tanh, scale=0.5).then_inc(th2_ready, 1)
                    if c > 0:
                        round_w(b + (k + 2), c % 2)

            head_a2(0, True)
            with act.Fori(1, AH) as h:
                head_a2(h)

            def round_x(src, use, n=T):
                for j in range(KT):
                    act.activation(XH[:, j, 0:n], src[:, j, :], ACT.Copy).then_inc(xh_ready, 1)

            for f in range(2):
                act.wait_ge(y_loaded, 16 * (f + 1))
                act.wait_ge(blk_done, A3_0 + f * KT)
                round_x(y_in, 1 + f)
                with act.Fori(0, KT // 2) as i:
                    for k in range(2):
                        round_w(i * 2 + (A3_0 + f * KT + 2 + k), k)
                        if f:
                            act.wait_ge(h_acc, i * 2 + (KT + k + 1))
                            act.wait_ge(ss_ready, i * 2 + (k + 1))
                            row = hT3[:, ds(i * 2 + k, 1), :].rearrange("p a n -> p (a n)")
                            act.activation(sq[k][:, :], row, ACT.Square).then_inc(sq_ready, 1)
            act.wait_ge(sumsq_done, 1)
            inv_sqrt(halves(ax[0]), rstd[:, :], 1.0 / D, rtmp[:, :], AH + 1, two, ln_ready, rstd_ready)
            for j in range(KT):
                act.wait_ge(xt_ready, KT + j + 1)
                act.activation(XH[:, j, :], xt3[j % 2][:, :], ACT.Copy).then_inc(xh_ready, 1)

            act.wait_ge(f_row, 2)
            act.activation(fg["e"][:, :], fg["abs"][:, :], ACT.Exp, scale=-1.0).then_inc(fexp, 1)
            act.wait_ge(fexp, 1)
            act.activation(fg["l1"][:, :], fg["e"][:, :], ACT.Ln, bias=1.0).then_inc(fexp, 1)
            round_w(B1_0 + 2, B1_0 % 2)
            act.wait_ge(h_stored2, 16)

            def softmax_exp(p_, i):
                act.wait_ge(sneg, p_ * NT + (i + 1))
                w = S_TILES[i + 1][0] + P
                act.activation(PR[:, i, 0:w], SS[i % 2][:, 0:w], ACT.Exp, bias=s_neg[:, i:i + 1],
                               accum_out=s_sum[:, i:i + 1]).then_inc(pexp, 1)

            def head_b1(h, first, attend):
                b = h * B1_PER + (B1_0 + 1)
                q0 = B1_0 + 1
                act.wait_ge(blk_done, b + 1)
                if not first:
                    act.wait_ge(hat_ready, h * 2)
                act.activation(QR[:, :], mm[0][:, 0:SEQ], ACT.Copy).then_inc(qkv4_ev, 1)
                act.activation(sq[0][:, 0:SEQ], mm[0][:, 0:SEQ], ACT.Square).then_inc(sq4_ready, 1)
                round_w(b + 2, q0 % 2)
                if attend:
                    for i in range(3):
                        softmax_exp(h - 1, i)
                act.wait_ge(blk_done, b + 2)
                act.activation(two(KR[:, :]), halves(mm[1]), ACT.Copy).then_inc(qkv4_ev, 1)
                act.activation(two(sq[1][:, :]), halves(mm[1]), ACT.Square).then_inc(sq4_ready, 1)
                round_w(b + 3, (q0 + 1) % 2)
                if attend:
                    softmax_exp(h - 1, 3)
                act.wait_ge(blk_done, b + 3)
                if not first:
                    act.wait_ge(vtr4, h * 2)
                act.activation(two(VT[:, :]), halves(mm[0]), ACT.Copy).then_inc(qkv4_ev, 1)
                round_w(b + 4, q0 % 2)
                act.wait_ge(blk_done, b + 4)
                if not first:
                    act.wait_ge(gate4_ready, h)
                act.activation(th4[:, :], mm[1][:, 0:SEQ], ACT.Tanh, scale=0.5).then_inc(th4_ready, 1)
                act.wait_ge(sum4_done, h * 2 + 1)
                inv_sqrt(halves(mm[0]), rstd[:, :], 1.0 / BD, rtmp[:, :], h * 2 + 1, two, ln4_ready, r4_ready)
                act.wait_ge(sum4_done, h * 2 + 2)
                act.wait_ge(r4_ready, h * 2 + 1)
                inv_sqrt(ax[0][:, 0:SEQ], rq[:, :], 1.0 / BD, rtmp[:, 0:SEQ], h * 2 + 2, lambda t: t, ln4_ready, r4_ready)
                round_w(b + 5, (q0 + 1) % 2)

            head_b1(0, True, False)
            with act.Fori(1, BH) as h:
                head_b1(h, False, True)
            for i in range(NT):
                softmax_exp(BH - 1, i)

            act.wait_ge(y4_ready, BH)
            round_x(Y, 4, SEQ)

            def tile_b2(i, k, more=True):
                if more:
                    round_w(i * 2 + (B2_0 + 2 + k), (B2_0 + k) % 2)
                act.wait_ge(h_acc, i * 2 + (2 * KT + k + 1))
                act.wait_ge(ss_ready, i * 2 + (KT + 2 + k + 1))
                row = hT5[:, ds(i * 2 + k, 1), META:T].rearrange("p a n -> p (a n)")
                act.activation(sq[k][:, 0:SEQ], row, ACT.Square).then_inc(sq_ready, 1)
                if not (isinstance(i, int) and i == 0):
                    act.wait_ge(out_tr, i * 2 + (k - 1))
                act.activation(hg[k][:, :], row, ACT.Copy, scale=par[:, ds(i * 2 + (C_FN + k), 1)]).then_inc(hg_ready, 1)

            for k in range(2):
                tile_b2(0, k)
            with act.Fori(1, KT // 2 - 1) as i:
                for k in range(2):
                    tile_b2(i, k)
            for k in range(2):
                tile_b2(KT // 2 - 1, k, False)
            act.wait_ge(sumsq_done, 2)
            act.activation(stat5[:, 0, :], ax[0][:, 0:NT], ACT.Ln, bias=eps_t[:, 0:1], scale=1.0 / D).then_inc(stat5_ready, 1)
            act.wait_ge(stat5_ready, 1)
            act.activation(stat5[:, 1, :], stat5[:, 0, :], ACT.Exp, scale=-0.5).then_inc(stat5_ready, 1)
            act.wait_ge(stat5_ready, 2)
            act.wait_ge(raw_ready, KT)
            for i in range(1, NT, 2):
                act.activation(o_nat[:, i, :], o_nat[:, i, :], ACT.Copy, scale=stat5[:, 1, i:i + 1]).then_inc(o_odd, 1)

        @block.vector
        def _(dve):
            def low_w(b, par_):
                if isinstance(b, int) and b >= BLOCKS:
                    return
                dve.wait_ge(w_hi_ready, b + 1)
                dve.tensor_tensor(w_lo[par_][:, :], w_raw[par_][:, :], w_hi[par_][:, :].bitcast(F32),
                                  ALU.subtract).then_inc(w_lo_ready, 1)


            def norm_tile(src, j, gain, xt, base):
                if j >= 2:
                    dve.wait_ge(xl_ready, xl_base + j - 1)
                dve.scalar_tensor_tensor(out=xt[j % 2][:, :], in0=src, scalar=gain, in1=rstd[:, :],
                                         op0=ALU.mult, op1=ALU.mult).then_inc(xt_ready, 1)

            def low_x(src, j, n=T):
                dve.wait_ge(xh_ready, xl_base + j + 1)
                dve.tensor_tensor(XL[:, j, 0:n], src, XH[:, j, 0:n].bitcast(F32), ALU.subtract).then_inc(xl_ready, 1)

            xl_base = 0
            low_w(0, 0)
            dve.wait_ge(const_ready, 3)
            dve.wait_ge(stat0_ready, NT + 5)
            for i in range(NT):
                dve.tensor_scalar(diag0[:, i, :], ident[:, :], stat0[:, 2, i:i + 1], None, ALU.mult).then_inc(diag0_ready, 1)
            dve.tensor_scalar(diag0[0:META, NT, 0:META], ident[0:META, 0:META], stat0[0:META, 2, NT:NT + 1], None,
                              ALU.mult).then_inc(diag0_ready, 1)
            dve.wait_ge(par_tr, 3)
            dve.tensor_copy(par[:, :], mm[0][:, 0:NPAR]).then_inc(par_ready, 1)
            dve.wait_ge(par_ready, 1)
            dve.tensor_scalar(par[:, C_HN:C_AN], par[:, C_HN:C_AN], 0.25, None, ALU.mult).then_inc(par_ready, 1)
            dve.wait_ge(par_ready, 2)
            dve.wait_ge(bcast0_done, 1)
            dve.tensor_copy(rstd[:, :], mm[1][:, X0:2 * BANK]).then_inc(rstd0_ready, 1)
            dve.wait_ge(rstd0_ready, 1)
            for j in range(KT + 1):
                if j < KT:
                    dve.wait_ge(h_copied, j + 1)
                    norm_tile(hT0[:, j, :], j, par[:, C_AN + j:C_AN + j + 1], xt0, 0)
                if j == 2:
                    low_w(1, 1)
                if j > 0:
                    low_x(xt0[(j - 1) % 2][:, :], j - 1)

            dve.wait_ge(xl_ready, KT)
            dve.wait_ge(h_stored, 16 * H_PARTS)
            for i in range(2):
                dve.memset(xm_pad[i][:, 0:TAPS - 1], 0.0).then_inc(pad_zero, 1)
            dve.memset(gacc[:, :], 0.0).then_inc(gacc_ready, 1)
            dve.wait_ge(pad_zero, 2)

            def conv_tile(h, c, n, npar):
                e = h * CT + c
                p = c % 2
                dve.wait_ge(xm_hi, e + 1)
                dve.tensor_tensor(xml[:, c, :], xm_pad[p][:, TAPS - 1:], xmh[:, c, :].bitcast(F32),
                                  ALU.subtract).then_inc(xm_lo, 1)
                dve.wait_ge(cv_aff, e + 1)
                for k in range(TAPS - 1):
                    tap = TAPS - 2 - k
                    if k:
                        dve.wait_ge(taps, e * 3 + k)
                    dve.scalar_tensor_tensor(out=conv[p][:, :], in0=xm_pad[p][:, tap:tap + T],
                                             scalar=par[:, ds(h * CT + (C_CW + tap * FT + c), 1)],
                                             in1=conv[p][:, :], op0=ALU.mult, op1=ALU.add).then_inc(taps, 1)
                low_w(n, npar)
                dve.wait_ge(th1_ready, e + 1)
                if not (isinstance(h, int) and h == 0 and c < 2):
                    dve.wait_ge(xc_stored[p], h * (8 * CT) + (c // 2) * 16)
                    dve.wait_ge(xc_lo, e - 1)
                dve.scalar_tensor_tensor(out=xc2[p][:, :], in0=th1[:, :], scalar=1.0, in1=conv[p][:, :],
                                         op0=ALU.add, op1=ALU.mult).then_inc(xc2_ready, 1)
                dve.wait_ge(xc_hi, e + 1)
                dve.scalar_tensor_tensor(out=xcl[:, c, :], in0=xc2[p][:, :], scalar=0.5,
                                         in1=xch[:, c, :].bitcast(F32), op0=ALU.mult,
                                         op1=ALU.subtract).then_inc(xc_lo, 1)

            def finish_qkv(h):
                dve.wait_ge(gate_mm, h + 1)
                dve.wait_ge(gacc_ready, h + 1)
                dve.tensor_tensor(two(gacc[:, :]), two(gacc[:, :]), halves(mm[1], HT, NG), ALU.add).then_inc(gacc_ready, 1)
                if not (isinstance(h, int) and h == 0):
                    dve.wait_ge(v_stored, h * 32)
                for i, (_, n) in enumerate(S_TILES):
                    dve.wait_ge(v_tr, h * NS + (i + 1))
                    dve.tensor_copy(vn1[0:n, i, :], ax[i % 2][0:n, 0:BANK]).then_inc(vn1_ev, 1)

            for c in range(CT):
                conv_tile(0, c, c + 2, c % 2)

            def head_a1(h):
                b0 = xm_block(h, 0)
                low_w(b0 + 2, 0)
                low_w(b0 + 3, 1)
                finish_qkv(h - 1)
                for c in range(CT):
                    conv_tile(h, c, b0 + (4 + c), c % 2)

            head_a1(1)
            with dve.Fori(2, AH) as h:
                head_a1(h)
            low_w(O0_BLOCK + 2, 0)
            low_w(O0_BLOCK + 3, 1)
            finish_qkv(AH - 1)

            dve.wait_ge(gacc_ready, AH + 1)
            dve.wait_ge(par_loaded, 16 * 11)
            dve.tensor_scalar(gacc[:, :], gacc[:, :], bg[:, 0:1], None, ALU.add).then_inc(gb_ready, 1)
            dve.wait_ge(gsel_done, 2)
            dve.wait_ge(qk_stored, 16 * AH)
            dve.wait_ge(v_stored, 32 * AH)
            for i in range(2):
                dve.wait_ge(xc_stored[i], 16 * AH * CT // 2)
            dve.tensor_copy(two(gr["ig"][:, :]), halves(ax[0], HT, AH)).then_inc(grow, 1)
            dve.tensor_copy(two(gr["f"][:, :]), halves(ax[1], HT, AH)).then_inc(grow, 1)
            dve.wait_ge(grow, 2)
            dve.scalar_tensor_tensor(out=gr["abs"][:, :], in0=gr["f"][:, :], scalar=-1.0, in1=gr["f"][:, :],
                                     op0=ALU.mult, op1=ALU.max).then_inc(grow, 1)
            dve.memset(gr["one"][:, :], 1.0).then_inc(grow, 1)
            low_w(A2_0 + 2, 0)
            dve.wait_ge(gexp, 2)
            dve.scalar_tensor_tensor(out=gr["lf"][:, :], in0=gr["f"][:, :], scalar=0.0, in1=gr["e"][:, :],
                                     op0=ALU.min, op1=ALU.subtract).then_inc(grow, 1)
            dve.wait_ge(grow, 5)
            dve.tensor_tensor_scan(gr["B"][:, :], gr["one"][:, :], gr["lf"][:, :], 0.0, ALU.mult, ALU.add).then_inc(grow, 1)
            dve.wait_ge(grow, 6)
            dve.tensor_tensor(gr["a"][:, :], gr["ig"][:, :], gr["B"][:, :], ALU.subtract).then_inc(grow, 1)
            dve.wait_ge(grow, 7)
            dve.tensor_tensor_scan(gr["M"][:, :], gr["one"][:, :], gr["a"][:, :], 0.0, ALU.mult, ALU.max).then_inc(grow, 1)
            dve.wait_ge(grow, 8)
            dve.tensor_tensor(gr["m"][:, :], gr["B"][:, :], gr["M"][:, :], ALU.add).then_inc(grow, 1)
            dve.tensor_scalar(gr["negm"][:, :], gr["M"][:, :], -1.0, None, ALU.mult).then_inc(grow, 1)
            dve.wait_ge(a_tr, 1)
            dve.tensor_copy(aT[0:META, 0, :], ax[0][0:META, 0:AH]).then_inc(grow, 1)
            dve.tensor_copy(flat(aT[:, 1:NS, :]), ax[0][:, AH:NS * AH]).then_inc(grow, 1)
            dve.wait_ge(grow, 12)

            def low_qk(h):
                dve.wait_ge(qk_hi, h + 1)
                dve.tensor_tensor(flat(qkl[:, :, :]), flat(qk2[:, :, :]), flat(qkh[:, :, :]).bitcast(F32), ALU.subtract).then_inc(qk_lo, 1)

            def low_v(h):
                dve.wait_ge(v_hi, h * 2 + 2)
                dve.tensor_tensor(vl[0:META, 0, :], v2[0:META, 0, :], vh[0:META, 0, :].bitcast(F32),
                                  ALU.subtract).then_inc(v_lo, 1)
                dve.tensor_tensor(flat(vl[:, 1:NS, :]), flat(v2[:, 1:NS, :]), flat(vh[:, 1:NS, :]).bitcast(F32),
                                  ALU.subtract).then_inc(v_lo, 1)

            def exponents(h):
                dve.wait_ge(negm_loaded, h * 16 + 16)
                wait(dve, pv_done, h * (1 + CT))
                for j, (s, n) in enumerate(S_TILES):
                    dve.tensor_scalar(EW[0:n, E_OFF[j]:E_OFF[j + 1]], negm_b[0:n, s:T],
                                      aT[0:n, j, ds(h, 1)], 0.0, ALU.add, ALU.min).then_inc(e_arg, 1)

            def causal_w(h):
                dve.wait_ge(e_ready, h * 2 + 2)
                for j, (s, n) in enumerate(S_TILES):
                    dg = EW[0:n, E_OFF[j]:E_OFF[j] + n]
                    dve.tensor_tensor(dg, dg, causal01[0:n, 0:n], ALU.mult).then_inc(e_diag, 1)
                dve.wait_ge(e_diag, h * NS + NS)

            def w_rows(h, tiles):
                for j in tiles:
                    s, n = S_TILES[j]
                    dve.wait_ge(sc_done, h * NS + (j + 1))
                    ps, at = SCORES_AT[j]
                    row = EW[0:n, E_OFF[j]:E_OFF[j + 1]]
                    dve.scalar_tensor_tensor(out=row, in0=ps[0:n, at:at + T - s], scalar=float(DQK) ** -0.5, in1=row,
                                             op0=ALU.mult, op1=ALU.mult).then_inc(w_ready, 1)
                for j in tiles:
                    n = S_TILES[j][1]
                    cols = slice(E_OFF[j], E_OFF[j + 1])
                    dve.wait_ge(w2_hi, h * NS + (j + 1))
                    dve.tensor_tensor(EWl[0:n, cols], EW[0:n, cols], EWh[0:n, cols].bitcast(F32),
                                      ALU.subtract).then_inc(w2_lo, 1)

            def head_a2(h, first=False):
                b = h * A2_PER + A2_0
                if first:
                    low_w(b + 3, 1)
                low_qk(h)
                exponents(h)
                if not first:
                    low_w(b + 2, 0)
                causal_w(h)
                w_rows(h, range(3))
                if not first:
                    low_w(b + 3, 1)
                low_v(h)
                w_rows(h, range(3, NS))
                low_w(b + 4, 0)
                dve.wait_ge(floor_loaded, h * 16 + 16)
                dve.wait_ge(pv_done, h * (1 + CT) + 1)
                dve.scalar_tensor_tensor(out=two(dn[:, :]), in0=halves(ax[1]), scalar=-1.0, in1=two(floor_b[:, :]),
                                         op0=ALU.mult, op1=ALU.max).then_inc(dn_ready, 1)
                dve.wait_ge(dn_ready, h * 2 + 1)
                dve.tensor_tensor(two(dn[:, :]), halves(ax[1]), two(dn[:, :]), ALU.max).then_inc(dn_ready, 1)
                dve.wait_ge(dn_ready, h * 2 + 2)
                dve.reciprocal(dn[:, :], dn[:, :]).then_inc(rd_ready, 1)
                dve.wait_ge(rd_ready, h + 1)
                for c in range(CT):
                    dve.wait_ge(ot_ready, h * CT + (c + 1))
                    dve.scalar_tensor_tensor(out=OT[:, c, :], in0=OT[:, c, :], scalar=1.0, in1=dn[:, :],
                                             op0=ALU.add, op1=ALU.mult).then_inc(og_ready, 1)
                low_w(b + 5, 1)
                for c in range(CT):
                    dve.wait_ge(pv_done, h * (1 + CT) + (c + 2))
                    dve.wait_ge(og_ready, h * CT + (c + 1))
                    dve.tensor_tensor(two(OT[:, c, :]), halves(ax[c % 2]), two(OT[:, c, :]), ALU.mult).then_inc(g_ready, 1)
                low_w(b + 6, 0)
                dve.wait_ge(rstd_ready, h + 1)
                dve.wait_ge(xc_loaded, h * 16 + 16)
                for c in range(CT):
                    k = CT + c
                    y = yb[c % 2]
                    wait(dve, y_stored[c % 2], h * 32 + (c // 2) * 16)
                    dve.scalar_tensor_tensor(out=y[:, :], in0=OT[:, c, :],
                                             scalar=par[:, ds(h * CT + (C_HN + c), 1)], in1=rstd[:, :],
                                             op0=ALU.mult, op1=ALU.mult).then_inc(mix_ready, 1)
                    dve.wait_ge(mix_ready, h * (2 * CT) + (2 * c + 1))
                    dve.scalar_tensor_tensor(out=y[:, :], in0=xcl2[:, c, :],
                                             scalar=par[:, ds(h * CT + (C_SK + c), 1)], in1=y[:, :],
                                             op0=ALU.mult, op1=ALU.add).then_inc(mix_ready, 1)
                    dve.wait_ge(th2_ready, h * CT + (c + 1))
                    dve.scalar_tensor_tensor(out=two(th2[c % 2][:, :]), in0=two(th2[c % 2][:, :]), scalar=1.0,
                                             in1=halves(mm[k % 2]), op0=ALU.add, op1=ALU.mult).then_inc(gate2_ready, 1)
                    dve.wait_ge(gate2_ready, h * CT + (c + 1))
                    dve.wait_ge(mix_ready, h * (2 * CT) + (2 * c + 2))
                    dve.tensor_tensor(y[:, :], y[:, :], th2[c % 2][:, :], ALU.mult).then_inc(y_ready, 1)
                    if c < CT - 1:
                        low_w(b + (k + 3), (k + 3) % 2)

            head_a2(0, True)
            with dve.Fori(1, AH) as h:
                head_a2(h)

            for f in range(2):
                xl_base = KT * (1 + f)
                dve.wait_ge(y_loaded, 16 * (f + 1))
                for j in range(KT):
                    low_x(y_in[:, j, :], j)
                dve.wait_ge(h_loaded, 16)
                with dve.Fori(0, KT // 2) as i:
                    for k in range(2):
                        b = i * 2 + (A3_0 + f * KT + k)
                        dve.wait_ge(blk_done, b + 1)
                        if f:
                            dve.wait_ge(h_acc, i * 2 + (k + 1))
                        row = hT3[:, ds(i * 2 + k, 1), :].rearrange("p a (b n) -> p (a b) n", b=2)
                        dve.tensor_tensor(row, row, halves(mm[k]), ALU.add).then_inc(h_acc, 1)
                        low_w(b + 2, k)
            xl_base = 3 * KT
            dve.wait_ge(rstd_ready, AH + 1)
            for j in range(KT + 1):
                if j < KT:
                    norm_tile(hT3[:, j, :], j, par[:, C_BN + j:C_BN + j + 1], xt3, 0)
                if j > 0:
                    dve.wait_ge(xt_ready, KT + j)
                    low_x(xt3[(j - 1) % 2][:, :], j - 1)

            dve.wait_ge(h_stored2, 16)
            dve.wait_ge(xl_ready, 4 * KT)
            dve.wait_ge(blk_done, B1_0 + 1)
            dve.tensor_scalar(two(fg["f"][:, :]), halves(mm[1], HT, BH), bf[:, 0:1], None, ALU.add).then_inc(f_row, 1)
            dve.wait_ge(f_row, 1)
            dve.scalar_tensor_tensor(out=fg["abs"][:, :], in0=fg["f"][:, :], scalar=-1.0, in1=fg["f"][:, :],
                                     op0=ALU.mult, op1=ALU.max).then_inc(f_row, 1)
            dve.memset(fg["one"][:, :], 1.0).then_inc(f_row, 1)
            dve.wait_ge(fexp, 2)
            dve.scalar_tensor_tensor(out=fg["lf"][:, :], in0=fg["f"][:, :], scalar=0.0, in1=fg["l1"][:, :],
                                     op0=ALU.min, op1=ALU.subtract).then_inc(f_row, 1)
            dve.wait_ge(f_row, 4)
            dve.tensor_tensor_scan(fg["c"][:, :], fg["one"][:, :], fg["lf"][:, :], 0.0, ALU.mult, ALU.add).then_inc(f_row, 1)
            dve.wait_ge(f_row, 5)
            dve.tensor_scalar(fg["negc"][:, :], fg["c"][:, :], -1.0, None, ALU.mult).then_inc(f_row, 1)
            low_w(B1_0 + 2, B1_0 % 2)
            dve.wait_ge(negc_stored, 16)

            def softmax_in(p_, i):
                w = S_TILES[i + 1][0] + P
                ps, at = ((ax[0], 0), (ax[0], BANK), (ax[1], 0), (ax[0], X0))[i]
                src = ps[:, at:at + w]
                s_ = SS[i % 2]
                dve.wait_ge(s4_done, p_ * NT + (i + 1))
                if i == 0:
                    dve.wait_ge(negc_loaded, p_ * 16 + 16)
                if i >= 2:
                    dve.wait_ge(pexp, p_ * NT + (i - 1))
                dve.scalar_tensor_tensor(out=s_[:, 0:w], in0=src, scalar=float(BD) ** -0.5, in1=negc_b[:, 0:w],
                                         op0=ALU.mult, op1=ALU.add).then_inc(sadd, 1)
                dve.wait_ge(sadd, p_ * NT + (i + 1))
                dve.tensor_tensor(s_[:, w - P:w], s_[:, w - P:w], causal_add[:, :], ALU.add).then_inc(smask, 1)
                dve.wait_ge(smask, p_ * NT + (i + 1))
                dve.reduce_max(s_max[:, i:i + 1], s_[:, 0:w], AX_X).then_inc(smax, 1)
                dve.wait_ge(smax, p_ * NT + (i + 1))
                dve.tensor_scalar(s_neg[:, i:i + 1], s_max[:, i:i + 1], -1.0, None, ALU.mult).then_inc(sneg, 1)

            def softmax_out(p_, i):
                w = S_TILES[i + 1][0] + P
                dve.wait_ge(pexp, p_ * NT + (i + 1))
                dve.reciprocal(s_inv[:, i:i + 1], s_sum[:, i:i + 1]).then_inc(sinv, 1)
                dve.wait_ge(sinv, p_ * NT + (i + 1))
                dve.tensor_scalar(PR[:, i, 0:w], PR[:, i, 0:w], s_inv[:, i:i + 1], None, ALU.mult).then_inc(pscaled, 1)

            def take_pt(p_, i):
                dve.wait_ge(ptr_done, p_ * (NT + 1) + (i + 1))
                if i < NT:
                    w = (i + 1) * P
                    src = ax[1][:, 0:w] if i % 2 else ax[1][:, BANK:BANK + w]
                    dve.tensor_copy(PTr[:, i, 0:w], src).then_inc(pt_ev, 1)
                else:
                    dve.tensor_copy(PTm[:, :], ax[0][0:META, 0:SEQ]).then_inc(pt_ev, 1)

            def head_b1(h, proj, attend, p_):
                b = h * B1_PER + (B1_0 + 1)
                q0 = B1_0 + 1
                if attend:
                    for i in range(3):
                        softmax_in(p_, i)
                if proj:
                    low_w(b + 2, q0 % 2)
                if attend:
                    for i in range(3):
                        softmax_out(p_, i)
                    softmax_in(p_, 3)
                    take_pt(p_, 0)
                if proj:
                    low_w(b + 3, (q0 + 1) % 2)
                if attend:
                    softmax_out(p_, 3)
                    for i in range(1, NT + 1):
                        take_pt(p_, i)
                if proj:
                    low_w(b + 4, q0 % 2)
                if attend:
                    dve.wait_ge(pv4_done, p_ + 1)
                    row = Y[:, ds(p_, 1), :].rearrange("p a n -> p (a n)")
                    dve.scalar_tensor_tensor(out=row, in0=ax[1][:, BANK:BANK + SEQ], scalar=0.5, in1=row,
                                             op0=ALU.mult, op1=ALU.mult).then_inc(y4_ready, 1)
                if proj:
                    dve.wait_ge(th4_ready, h + 1)
                    row = Y[:, ds(h, 1), :].rearrange("p a n -> p (a n)")
                    dve.scalar_tensor_tensor(out=row, in0=th4[:, :], scalar=1.0, in1=mm[1][:, 0:SEQ],
                                             op0=ALU.add, op1=ALU.mult).then_inc(gate4_ready, 1)
                    dve.wait_ge(vtr4, h * 2 + 2)
                    dve.tensor_copy(flat(vn4[:, :, :]), ax[1][:, 0:NT * BD]).then_inc(vn4_ev, 1)
                    dve.tensor_copy(vm4[:, :], ax[0][0:META, BANK:BANK + BD]).then_inc(vn4_ev, 1)
                    dve.wait_ge(r4_ready, h * 2 + 1)
                    dve.scalar_tensor_tensor(out=KH[:, :], in0=KR[:, :], scalar=par[:, C_KN:C_KN + 1], in1=rstd[:, :],
                                             op0=ALU.mult, op1=ALU.mult).then_inc(hat_ready, 1)
                    dve.wait_ge(r4_ready, h * 2 + 2)
                    dve.scalar_tensor_tensor(out=QH[:, :], in0=QR[:, :], scalar=par[:, C_QN:C_QN + 1], in1=rq[:, :],
                                             op0=ALU.mult, op1=ALU.mult).then_inc(hat_ready, 1)
                    low_w(b + 5, (q0 + 1) % 2)

            head_b1(0, True, False, 0)
            with dve.Fori(1, BH) as h:
                head_b1(h, True, True, h - 1)
            head_b1(BH, False, True, BH - 1)

            xl_base = 4 * KT
            dve.wait_ge(y4_ready, BH)
            for j in range(KT):
                low_x(Y[:, j, :], j, SEQ)
            dve.wait_ge(h_loaded2, 16)

            def add_b2(i, k, more=True):
                b = i * 2 + (B2_0 + k)
                dve.wait_ge(blk_done, b + 1)
                row = hT5[:, ds(i * 2 + k, 1), META:T].rearrange("p a n -> p (a n)")
                dve.tensor_tensor(row, row, mm[k][:, 0:SEQ], ALU.add).then_inc(h_acc, 1)
                if more:
                    low_w(b + 2, (B2_0 + k) % 2)

            def take_raw(i, k):
                dve.wait_ge(out_tr, i * 2 + (k + 1))
                dve.tensor_copy(o_nat[:, :, ds(i * (2 * P) + k * P, P)],
                                ax[1][:, k * BANK:(k + 1) * BANK].rearrange("p (a n) -> p a n", a=NT)).then_inc(raw_ready, 1)

            add_b2(0, 0)
            add_b2(0, 1)
            with dve.Fori(1, KT // 2 - 1) as i:
                for k in range(2):
                    add_b2(i, k)
                    take_raw(i - 1, k)
            for k in range(2):
                add_b2(KT // 2 - 1, k, False)
                take_raw(KT // 2 - 2, k)
            for k in range(2):
                take_raw(KT // 2 - 1, k)
            dve.wait_ge(raw_ready, KT)
            dve.wait_ge(stat5_ready, 2)
            for i in range(0, NT, 2):
                dve.tensor_scalar(o_nat[:, i, :], o_nat[:, i, :], stat5[:, 1, i:i + 1], None, ALU.mult).then_inc(o_even, 1)

        @block.tensor
        def _(pe):
            ALL = ((0, 0, HT), (BANK, HT, HT))
            REAL = ((0, META, SEQ),)
            PACKED = ((0, 0, SEQ),)

            def three(ps, wh, wl, xh, xl, spans, first, last):
                for k, (w, v) in enumerate(((wh, xh), (wh, xl), (wl, xh))):
                    for at, t0, n in spans:
                        i = pe.matmul(ps[:, at:at + n], w, v[:, t0:t0 + n],
                                      start=first and k == 0, stop=last and k == 2)
                return i

            def block_tile(par_, ps, spans, k, fresh):
                if fresh is not None:
                    pe.wait_ge(xl_ready, fresh + k + 1)
                i = three(ps, w_hi[par_][:, k * P:(k + 1) * P], w_lo[par_][:, k * P:(k + 1) * P],
                          XH[:, k, :], XL[:, k, :], spans, k == 0, k == KT - 1)
                if k == KT - 1:
                    i.then_inc(blk_done, 1)

            BEHIND = 8

            def two_blocks(b, par_, ps, spans, fresh):
                for k in range(KT + BEHIND):
                    for a, j in enumerate((k, k - BEHIND)):
                        if j == 0:
                            pe.wait_ge(w_lo_ready, b + a + 1)
                        if 0 <= j < KT:
                            block_tile((par_ + a) % 2, ps[a], spans[a], j, fresh)

            def blockmm(b, par_, ps, spans=ALL, fresh=None):
                pe.wait_ge(w_lo_ready, b + 1)
                for k in range(KT):
                    block_tile(par_, ps, spans, k, fresh)

            def full_sum(ps, src, n, first=True, last=True):
                for a in range(2):
                    i = pe.matmul(ps[:, a * BANK:a * BANK + n], ones[:, :], src[:, a * n:(a + 1) * n],
                                  start=first, stop=last)
                return i

            pe.wait_ge(const_ready, 3)
            pe.wait_ge(meta_loaded, 16)
            for i in range(NT):
                pe.wait_ge(x_loaded[i], 16)
            LAG = 3
            for j in range(KT + LAG + BEHIND):
                if j == 2:
                    pe.wait_ge(par_loaded, 16 * 10)
                    for t, n in enumerate((P, P, NPAR - 2 * P)):
                        pe.transpose(mm[0][:, t * P:t * P + n], par_rows[0:n, t, :], ident[0:n, 0:n]).then_inc(par_tr, 1)
                    pe.wait_ge(diag0_ready, NT + 1)
                    pe.matmul(mm[1][:, X0:BANK], ones[0:META, :], diag0[0:META, NT, 0:META], start=True, stop=True)
                    pe.matmul(mm[1][:, BANK:2 * BANK], ones[:, :], flat(diag0[:, 0:NT, :]), start=True,
                              stop=True).then_inc(bcast0_done, 1)
                if j < KT:
                    if j >= 2:
                        pe.wait_ge(h_copied, j - 1)
                    ps = ax[j % 2]
                    pe.transpose(ps[:, X0:BANK], meta_nat[:, j * P:(j + 1) * P], ident[0:META, 0:META])
                    for i in range(NT):
                        t = pe.transpose(ps[:, BANK + i * P:BANK + (i + 1) * P], x_nat[:, i, j * P:(j + 1) * P], ident[:, :])
                    t.then_inc(x_tr, 1)
                if j >= LAG:
                    if j == LAG:
                        pe.wait_ge(par_ready, 1)
                        pe.wait_ge(rstd0_ready, 1)
                        pe.wait_ge(w_lo_ready, 1)
                    if j < KT + LAG:
                        block_tile(0, mm[0], ALL, j - LAG, 0)
                    if j == LAG + BEHIND:
                        pe.wait_ge(w_lo_ready, 2)
                    if j >= LAG + BEHIND:
                        block_tile(1, mm[1], ALL, j - LAG - BEHIND, 0)

            def xm_tile(h, c, par_):
                if isinstance(h, int) and h == 0:
                    pe.wait_ge(cv_aff, c - 1)
                else:
                    pe.wait_ge(cv_aff, h * CT + (c - 1))
                    if c == 1:
                        pe.wait_ge(gacc_ready, h + 1)
                blockmm(xm_block(h, c), par_, mm[c % 2])

            def qkv_tiles(h, par_):
                b = qkv_block(h)
                pe.wait_ge(w_lo_ready, b + 1)
                pe.wait_ge(xc_lo, h * CT + CT)
                first = isinstance(h, int) and h == 0
                NJ = 2 * QT + CT

                def gate(j):
                    pe.wait_ge(qkv_ev, h * NJ + (j + 1))
                    for a in range(2):
                        i = pe.matmul(mm[1][0:NG, a * BANK:a * BANK + HT], wg[:, j, :], qkv[:, j, a * HT:(a + 1) * HT],
                                      start=j == 0, stop=j == NJ - 1)
                    return i

                for j in range(NJ):
                    if j == 2 * QT:
                        pe.wait_ge(w_lo_ready, b + 2)
                    if j < 2:
                        if not first:
                            pe.wait_ge(vn1_ev, h * NS)
                    else:
                        pe.wait_ge(qkv_ev, h * NJ + (j - 1))
                    p_ = par_ if j < 2 * QT else 1 - par_
                    col = j % (2 * QT) * P
                    xh, xl = (xch, xcl) if j < 2 * QT else (xmh, xml)
                    for k in range(CT):
                        at = k * CT * P + col
                        i = three(ax[j % 2], w_hi[p_][:, at:at + P], w_lo[p_][:, at:at + P],
                                  xh[:, k, :], xl[:, k, :], ALL, k == 0, k == CT - 1)
                    if j % (2 * QT) == 2 * QT - 1:
                        i.then_inc(qkv_mm, 1)
                        pe.wait_ge(qkv_mm, h * NJ + (j + 1))
                        pe.sem_inc(blk_done, 1)
                    else:
                        i.then_inc(qkv_mm, 1)
                    if j == 1:
                        pe.wait_ge(wg_loaded, h * 48 + 48)
                    if j >= 1:
                        gate(j - 1)
                gate(NJ - 1).then_inc(gate_mm, 1)
                for i, (s, n) in enumerate(S_TILES):
                    if i >= 2:
                        pe.wait_ge(vn1_ev, h * NS + (i - 1))
                    for c in range(CT):
                        t = pe.transpose(ax[i % 2][0:n, c * P:(c + 1) * P], qkv[:, 2 * QT + c, s:s + n], ident[:, :])
                    t.then_inc(v_tr, 1)

            for c in range(2, CT):
                xm_tile(0, c, c % 2)

            def head_a1(h):
                xm_tile(h, 0, 0)
                qkv_tiles(h - 1, 1)
                for c in range(1, CT):
                    xm_tile(h, c, c % 2)

            head_a1(1)
            with pe.Fori(2, AH) as h:
                head_a1(h)
            pe.wait_ge(cv_aff, AH * CT - 1)
            blockmm(O0_BLOCK, 0, mm[0])
            qkv_tiles(AH - 1, 1)

            def three_f32r(ps, xh, xl, yh, yl, first, last):
                for k, (x_, y_) in enumerate(((xh, yh), (xh, yl), (xl, yh))):
                    i = pe.matmul(ps, x_, y_, start=first and k == 0, stop=last and k == 2)
                return i

            def gates():
                pe.wait_ge(gb_ready, 1)
                pe.wait_ge(vn1_ev, AH * NS)
                for g in range(2):
                    for a in range(2):
                        i = pe.matmul(ax[g][0:AH, a * BANK:a * BANK + HT], ident[0:NG, g * AH:(g + 1) * AH],
                                      gacc[:, a * HT:(a + 1) * HT], start=True, stop=True)
                    i.then_inc(gsel_done, 1)

            def a_columns():
                pe.wait_ge(grow, 7)
                for i, (s, n) in enumerate(S_TILES):
                    t = pe.transpose(ax[0][0:n, i * AH:(i + 1) * AH], gr["a"][:, s:s + n], ident[0:AH, 0:AH])
                t.then_inc(a_tr, 1)

            def scores_a2(h, j):
                s, n = S_TILES[j]
                ps, at0 = SCORES_AT[j]
                if j == 0:
                    pe.wait_ge(qk_lo, h + 1)
                    wait(pe, rstd_ready, h)
                    wait(pe, g_ready, h * CT)
                if j == 3:
                    pe.wait_ge(w_ready, h * NS + 1)
                for at, t0, w in ([(X0, 0, META), (BANK, META, SEQ)] if j == 0 else [(at0, s, T - s)]):
                    for k in range(QT):
                        i = three_f32r(ps[0:n, at:at + w], qkh[:, QT + k, s:s + n], qkl[:, QT + k, s:s + n],
                                       qkh[:, k, t0:t0 + w], qkl[:, k, t0:t0 + w], k == 0, k == QT - 1)
                i.then_inc(sc_done, 1)

            def over_s(ps, high, low):
                for j, (s, n) in enumerate(S_TILES):
                    for a in range(2):
                        lo, hi = max(s, a * HT), (a + 1) * HT
                        if lo >= hi:
                            continue
                        last = not any(max(s2, a * HT) < hi for s2, _ in S_TILES[j + 1:])
                        cols = slice(E_OFF[j] + lo - s, E_OFF[j] + hi - s)
                        passes = [(high(j, n), EWh), (high(j, n), EWl)] + ([(low(j, n), EWh)] if low else [])
                        for k, (v, w) in enumerate(passes):
                            i = pe.matmul(ps[:, a * BANK + lo - a * HT:a * BANK + HT], v, w[0:n, cols],
                                          start=j == 0 and k == 0, stop=last and k == len(passes) - 1)
                i.then_inc(pv_done, 1)

            def head_a2(h, first=False):
                b = h * A2_PER + A2_0
                for c in range(CT):
                    if c < 2:
                        if first:
                            pe.wait_ge(gacc_ready, AH + 1)
                        else:
                            pe.wait_ge(gate2_ready, h * CT + (c - 1))
                    else:
                        pe.wait_ge(ot_ready, h * CT + (c - 1))
                    if not (first and c == 0):
                        blockmm(b + c, c % 2, mm[c % 2])
                    if first and c == 0:
                        gates()
                    if first and c == 1:
                        a_columns()
                    if c == (2 if first else 0):
                        if first:
                            pe.wait_ge(grow, 12)
                        for j in range(3):
                            scores_a2(h, j)
                    if c == (3 if first else 1):
                        for j in range(3, NS):
                            scores_a2(h, j)
                    if c == (3 if first else 2):
                        pe.wait_ge(w2_lo, h * NS + NS)
                        over_s(ax[1], lambda j, n: ones_r[0:n, :], None)
                pe.wait_ge(v_lo, h * 2 + 2)
                for c in range(CT):
                    if c == 1:
                        pe.wait_ge(dn_ready, h * 2 + 2)
                    if c > 1:
                        pe.wait_ge(g_ready, h * CT + (c - 1))
                    cols = slice(c * P, (c + 1) * P)
                    over_s(ax[c % 2], lambda j, n: vh[0:n, j, cols], lambda j, n: vl[0:n, j, cols])
                for c in range(CT):
                    k = CT + c
                    if c < 2:
                        pe.wait_ge(ot_ready, h * CT + (c + 3))
                    else:
                        pe.wait_ge(gate2_ready, h * CT + (c - 1))
                    blockmm(b + k, k % 2, mm[k % 2])
                    if c == 0:
                        pe.wait_ge(g_ready, h * CT + CT)
                        pe.wait_ge(ss2_ready, h * (CT - 1) + (CT - 1))
                        full_sum(ax[0], rtmp, HT).then_inc(sumg_done, 1)

            head_a2(0, True)
            with pe.Fori(1, AH) as h:
                head_a2(h)

            def out_blocks(b0, acc0, spans, fresh):
                for k in range(2):
                    blockmm(b0 + k, (b0 + k) % 2, mm[k], spans, fresh if k == 0 else None)
                with pe.Fori(1, KT // 2) as i:
                    for k in range(2):
                        pe.wait_ge(h_acc, i * 2 + (acc0 + k - 1))
                        blockmm(i * 2 + (b0 + k), (b0 + k) % 2, mm[k], spans)

            pe.wait_ge(gate2_ready, AH * CT)
            out_blocks(A3_0, 0, ALL, KT)
            pe.wait_ge(h_acc, KT)
            out_blocks(A3_0 + KT, KT, ALL, 2 * KT)
            pe.wait_ge(ss_ready, KT + 2)
            full_sum(ax[0], rtmp, HT).then_inc(sumsq_done, 1)

            pe.wait_ge(h_acc, 2 * KT)
            two_blocks(B1_0, B1_0 % 2, (mm[1], mm[0]), (ALL, REAL), 3 * KT)

            def scores(p_, i):
                w = S_TILES[i + 1][0] + P
                q = QH[:, i * P:(i + 1) * P]
                if i < 3:
                    at = (ax[0][:, 0:w], ax[0][:, BANK:BANK + w], ax[1][:, 0:w])[i]
                    m = pe.matmul(at, q, KH[:, 0:w], start=True, stop=True)
                else:
                    pe.matmul(ax[0][:, X0:BANK], q, KH[:, 0:META], start=True, stop=True)
                    m = pe.matmul(ax[0][:, BANK:2 * BANK], q, KH[:, META:T], start=True, stop=True)
                m.then_inc(s4_done, 1)

            def transpose_p(p_, i):
                pe.wait_ge(pscaled, p_ * NT + (min(i, NT - 1) + 1))
                if i < NT:
                    base = 0 if i % 2 else BANK
                    for j in range(i + 1):
                        s = S_TILES[j + 1][0]
                        t = pe.transpose(ax[1][:, base + j * P:base + (j + 1) * P], PR[:, i, s:s + P], ident[:, :])
                else:
                    for j in range(NT):
                        t = pe.transpose(ax[0][0:META, j * P:(j + 1) * P], PR[:, j, 0:META], ident[:, :])
                t.then_inc(ptr_done, 1)

            def head_b1(h, proj, attend, p_, first=False):
                b = h * B1_PER + (B1_0 + 1)
                q0 = B1_0 + 1
                if proj and not first:
                    pe.wait_ge(ln4_ready, h * 2 - 1)
                    blockmm(b, q0 % 2, mm[0], REAL)
                if attend:
                    pe.wait_ge(hat_ready, p_ * 2 + 2)
                    pe.wait_ge(vn4_ev, p_ * 2 + 2)
                    pe.wait_ge(ln4_ready, p_ * 2 + 2)
                    for i in range(3):
                        scores(p_, i)
                if proj:
                    if first:
                        pe.wait_ge(f_row, 1)
                    else:
                        pe.wait_ge(gate4_ready, h)
                    blockmm(b + 1, (q0 + 1) % 2, mm[1])
                if attend:
                    pe.wait_ge(sadd, p_ * NT + 2)
                    scores(p_, 3)
                    transpose_p(p_, 0)
                if proj:
                    pe.wait_ge(sq4_ready, h * 2 + 1)
                    blockmm(b + 2, q0 % 2, mm[0])
                if attend:
                    pe.wait_ge(sadd, p_ * NT + 4)
                    transpose_p(p_, 1)
                    pe.wait_ge(pt_ev, p_ * (NT + 1) + 1)
                    transpose_p(p_, 2)
                    pe.wait_ge(pt_ev, p_ * (NT + 1) + 2)
                    transpose_p(p_, 3)
                    transpose_p(p_, NT)
                if proj:
                    pe.wait_ge(sq4_ready, h * 2 + 2)
                    blockmm(b + 3, (q0 + 1) % 2, mm[1], REAL)
                    pe.wait_ge(qkv4_ev, h * 3 + 3)
                    full_sum(mm[0], sq[1], HT).then_inc(sum4_done, 1)
                    if attend:
                        pe.wait_ge(pt_ev, p_ * (NT + 1) + (NT + 1))
                    pe.matmul(ax[0][:, 0:SEQ], ones[:, :], sq[0][:, 0:SEQ], start=True, stop=True).then_inc(sum4_done, 1)
                if attend:
                    pe.wait_ge(pt_ev, p_ * (NT + 1) + (NT + 1))
                    o = ax[1][:, BANK:BANK + SEQ]
                    pe.matmul(o, vm4[:, :], PTm[:, :], start=True, stop=False)
                    for i in range(NT):
                        for j in range(i + 1):
                            m = pe.matmul(o[:, i * P:(i + 1) * P], vn4[:, j, :], PTr[:, i, j * P:(j + 1) * P],
                                          start=False, stop=i == j == NT - 1)
                    m.then_inc(pv4_done, 1)
                if proj:
                    for j in range(NT):
                        s = S_TILES[j + 1][0]
                        t = pe.transpose(ax[1][:, j * P:(j + 1) * P], VT[:, s:s + P], ident[:, :])
                    t.then_inc(vtr4, 1)
                    pe.transpose(ax[0][0:META, BANK:BANK + P], VT[:, 0:META], ident[:, :]).then_inc(vtr4, 1)

            head_b1(0, True, False, 0, True)
            with pe.Fori(1, BH) as h:
                head_b1(h, True, True, h - 1)
            head_b1(BH, False, True, BH - 1)

            def transpose_h(i, k):
                pe.wait_ge(hg_ready, i * 2 + (k + 1))
                if not (isinstance(i, int) and i == 0):
                    pe.wait_ge(raw_ready, i * 2 + (k - 1))
                for a in range(NT):
                    t = pe.transpose(ax[1][:, k * BANK + a * P:k * BANK + (a + 1) * P], hg[k][:, a * P:(a + 1) * P], ident[:, :])
                t.then_inc(out_tr, 1)

            pe.wait_ge(y4_ready, BH)
            for k in range(2):
                blockmm(B2_0 + k, (B2_0 + k) % 2, mm[k], PACKED, 4 * KT if k == 0 else None)
            pe.wait_ge(h_acc, 2 * KT + 1)
            blockmm(B2_0 + 2, B2_0 % 2, mm[0], PACKED)
            for k in range(2):
                transpose_h(0, k)
            pe.wait_ge(h_acc, 2 * KT + 2)
            blockmm(B2_0 + 3, (B2_0 + 1) % 2, mm[1], PACKED)
            with pe.Fori(2, KT // 2) as i:
                for k in range(2):
                    pe.wait_ge(h_acc, i * 2 + (2 * KT + k - 1))
                    blockmm(i * 2 + (B2_0 + k), (B2_0 + k) % 2, mm[k], PACKED)
                    transpose_h(i - 1, k)
            for k in range(2):
                transpose_h(KT // 2 - 1, k)
            pe.wait_ge(ss_ready, 2 * (KT + 2))
            for a in range(NT):
                i = pe.matmul(ax[0][:, a:a + 1], rtmp[:, a * P:(a + 1) * P], ones[:, 0:1], start=True, stop=True)
            i.then_inc(sumsq_done, 1)


_INS = ['x', 'meta_tokens', 'a_norm', 'a_w_in', 'a_conv_w', 'a_conv_b', 'a_w_q', 'a_w_k', 'a_w_v', 'a_w_gate',
        'a_b_gate', 'a_head_norm', 'a_skip', 'a_w_out', 'b_norm', 'b_w_in', 'b_b_f', 'b_q_norm', 'b_k_norm',
        'b_w_out', 'final_norm']


def kernel(**inputs):
    import numpy as _np
    import concourse.bacc as _bacc
    from concourse import mybir as _mybir
    from concourse.bass_utils import run_bass_kernel_spmd as _run

    nc = _bacc.Bacc("TRN2", target_bir_lowering=False, num_devices=1)
    arrays, args = {}, []
    for name in _INS:
        a = _np.ascontiguousarray(inputs[name])
        arrays[f"in_{name}_dram"] = a
        args.append(nc.dram_tensor(f"in_{name}_dram", a.shape, _mybir.dt.from_np(a.dtype), kind="ExternalInput").ap())
    shape = tuple(inputs["x"].shape)
    args.append(nc.dram_tensor("out_0_dram", shape, _mybir.dt.from_np(_np.dtype("float32")), kind="ExternalOutput").ap())
    hybrid_trunk(nc, *args)
    r = _run(nc, [arrays], core_ids=[0])
    return r.results[0]["out_0_dram"]
```

```python
from contextlib import ExitStack

import concourse.bass as bass
from concourse import mybir

F32 = mybir.dt.float32
F32R = mybir.dt.float32r
ALU = mybir.AluOpType
ACT = mybir.ActivationFunctionType
AX_X = mybir.AxisListType.X
ds = bass.ds

P = 128
BANK = 512


def hybrid_trunk(nc, x, meta_tokens, a_norm, a_w_in, a_conv_w, a_conv_b, a_w_q, a_w_k, a_w_v,
                 a_w_gate, a_b_gate, a_head_norm, a_skip, a_w_out, b_norm, b_w_in, b_b_f,
                 b_q_norm, b_k_norm, b_w_out, final_norm, out):
    _, SEQ, D = x.shape
    META = meta_tokens.shape[0]
    T = META + SEQ
    HT = T // 2
    HS = SEQ // 2
    KT = D // P
    AI = a_w_in.shape[2] // 3
    AH, DV, DQK = a_w_q.shape[1], a_w_q.shape[2], a_w_q.shape[3]
    CT = DV // P
    QT = DQK // P
    NG = a_w_gate.shape[2]
    BH, BD = b_b_f.shape[1], b_q_norm.shape[1]
    TAPS = a_conv_w.shape[1]
    M0, M1, M2 = (slice(32 * i, 32 * i + META) for i in range(3))
    MROWS = 64 + META
    W_AFTER = 5
    H_PARTS = 4
    EPS = 1e-6
    S_TILES = [(0, META)] + [(META + P * i, P) for i in range(SEQ // P)]
    NS = len(S_TILES)
    NT = SEQ // P
    E_OFF = [sum(T - s for s, _ in S_TILES[:j]) for j in range(NS + 1)]
    assert (T, KT, CT, QT, BD, NG) == (528, 16, 4, 2, P, 2 * AH) and AI == AH * DV

    A1_PER, A2_PER, B1_PER = CT + 2, 2 * CT, 4
    A2_0 = AH * A1_PER
    A3_0 = A2_0 + AH * A2_PER
    B1_0 = A3_0 + 2 * KT
    B2_0 = B1_0 + 1 + BH * B1_PER
    BLOCKS = B2_0 + KT

    def xm_block(h, c):
        if isinstance(h, int) and h == 0:
            return c
        return CT + A1_PER * (h - 1) + (0 if c == 0 else 2 + c)

    O0_BLOCK = CT + A1_PER * (AH - 1)

    def qkv_block(h):
        return CT + A1_PER * h + 1

    FT = AI // P
    C_CW, C_CB = 0, TAPS * FT
    C_HN, C_SK = C_CB + FT, C_CB + 2 * FT
    C_AN = C_SK + FT
    C_BN = C_AN + KT
    C_FN = C_BN + KT
    C_QN, C_KN = C_FN + KT, C_FN + KT + 1
    NPAR = C_KN + 1

    with ExitStack() as ctx:
        def sb(name, shape, dt=F32, scope=ctx):
            return scope.enter_context(nc.sbuf_tensor(name, shape, dt))

        def sb_split(name, shape, scope):
            whole = ExitStack()
            raw = sb(name + "_whole", shape, scope=whole)
            whole.close()
            return raw, sb(name + "_low", shape, F32R, scope)

        def sem(name):
            return ctx.enter_context(nc.semaphore(name))

        def dram(name, shape):
            return nc.dram_tensor(name, shape, F32).ap()

        h_d = dram("h_scratch", [P, KT * T])
        qk_d = dram("qk_scratch", [AH, P, 2 * QT * T])
        v_d = dram("v_scratch", [AH, P, NS * DV])
        xc_d = dram("xc_scratch", [P, FT * T])
        y_d = dram("y_scratch", [P, FT * T])
        negm_d = dram("negm_scratch", [AH, T])
        floor_d = dram("floor_scratch", [AH, T])
        negc_d = dram("negc_scratch", [BH, T])

        XH = sb("xh", [P, KT, T], F32R)
        XL = sb("xl", [P, KT, T], F32R)
        w_raw = [sb(f"w_raw{i}", [P, KT * P]) for i in range(2)]
        w_hi = [sb(f"w_hi{i}", [P, KT * P], F32R) for i in range(2)]
        w_lo = [sb(f"w_lo{i}", [P, KT * P], F32R) for i in range(2)]
        ident = sb("ident", [P, P])
        ones = sb("ones", [P, P])
        ones_r = sb("ones_r", [P, P], F32R)
        causal01 = sb("causal01", [P, P])
        par = sb("par", [P, NPAR])
        rstd = sb("rstd", [P, T])
        rtmp = sb("rtmp", [P, T])
        eps_t = sb("eps", [P, 1])
        sel = sb("sel", [2 * NG, NG])
        sq = [sb(f"sq{i}", [P, T]) for i in range(2)]
        causal_add = sb("causal_add", [P, P])
        bf = sb("bf", [BH, 1])

        gacc = rtmp[0:2 * NG, :]
        s0 = ExitStack()
        hT0 = sb("h0", [P, KT, T], scope=s0)
        x_nat = sb("x_nat", [P, NT, D], scope=s0)
        meta_nat = sb("meta_nat", [META, D], scope=s0)
        par_rows = sb("par_rows", [P, 3, P], scope=s0)
        xt0 = [sb(f"xt0{i}", [P, T], scope=s0) for i in range(2)]
        diag0 = sb("diag0", [P, NT + 1, P], scope=s0)
        stat0 = sb("stat0", [P, 3, NT + 1], scope=s0)
        s0.close()
        s1 = ExitStack()
        xmh = sb("xmh", [P, CT, T], F32R, s1)
        xml = sb("xml", [P, CT, T], F32R, s1)
        xch = sb("xch", [P, CT, T], F32R, s1)
        xcl = sb("xcl", [P, CT, T], F32R, s1)
        qkv = sb("qkv", [P, 2 * QT + CT, T], scope=s1)
        vn1 = sb("vn1", [P, NS, DV], scope=s1)
        xm_pad = [sb(f"xm_pad{i}", [P, TAPS - 1 + T], scope=s1) for i in range(2)]
        conv = [sb(f"conv{i}", [P, T], scope=s1) for i in range(2)]
        xc2 = [sb(f"xc2{i}", [P, T], scope=s1) for i in range(2)]
        th1 = sq[0]
        gh, gl = ([sb(f"gate_{n}{i}", [P, T], F32R, s1) for i in range(2)] for n in ("high", "low"))
        wgp = sb("wgp", [P, 2 * QT + CT, 2 * NG], F32R, s1)
        wg = sb("wg", [P, 2 * QT + CT, NG], scope=s1)
        bg = sb("bg", [NG, 1], scope=s1)
        s1.close()
        s2 = ExitStack()
        qkh = sb("qkh", [P, 2 * QT, T], F32R, s2)
        qk2, qkl = sb_split("qk", [P, 2 * QT, T], s2)
        vh = sb("vh", [P, NS, DV], F32R, s2)
        v2, vl = sb_split("v", [P, NS, DV], s2)
        OT = sb("ot", [P, CT, T], scope=s2)
        aT = sb("aT", [P, NS, AH], scope=s2)
        s2g = ExitStack()
        gr = {n: sb(f"gr_{n}", [AH, T], scope=s2g)
              for n in ("ig", "f", "abs", "e", "lf", "B", "a", "M", "negm", "m", "floor", "one")}
        s2g.close()
        EW, EWl = sb_split("w", [P, E_OFF[NS]], s2)
        EWh = sb("ewh", [P, E_OFF[NS]], F32R, s2)
        xcl2 = sb("xc_load", [P, CT, T], scope=s2)
        yb = [sb(f"yb{i}", [P, T], scope=s2) for i in range(2)]
        th2 = [sb(f"th2{i}", [P, T], scope=s2) for i in range(2)]
        negm_b = sb("negm_b", [P, T], scope=s2)
        floor_b = sb("floor_b", [P, T], scope=s2)
        dn = sb("dn", [P, T], scope=s2)
        s2.close()
        s3 = ExitStack()
        y_in = sb("y_in", [P, KT, T], scope=s3)
        hT3 = sb("h3", [P, KT, T], scope=s3)
        xt3 = [sb(f"xt3{i}", [P, T], scope=s3) for i in range(2)]
        s3.close()
        s4 = ExitStack()
        Y = sb("y", [P, BH, SEQ], scope=s4)
        QR = sb("q_raw", [P, SEQ], scope=s4)
        KR = sb("k_raw", [P, T], scope=s4)
        VT = sb("v_t", [P, T], scope=s4)
        Qh, Ql = (sb(f"q_{n}", [P, SEQ], F32R, s4) for n in ("high", "low"))
        Kh, Kl = (sb(f"k_{n}", [P, T], F32R, s4) for n in ("high", "low"))
        Vh, Vl = (sb(f"v4_{n}", [P, NT * BD], F32R, s4) for n in ("high", "low"))
        Vm = sb("vm4", [MROWS, BD], F32R, s4)
        SS = [rtmp, sb("scores1", [P, T], scope=s4)]
        PR = sb("probs", [P, NT, T], scope=s4)
        PTh, PTl = (sb(f"probs_t_{n}", [P, 4 * NT - 3, P], F32R, s4) for n in ("high", "low"))
        PM = sb("probs_t_meta", [MROWS, SEQ], F32R, s4)
        negc_b = sb("negc_b", [P, T], scope=s4)
        s_max, s_neg, s_sum, s_inv, rq_ln, rq = (sb(f"s_{n}", [P, NT], scope=s4) for n in (
            "max", "neg", "sum", "inv", "rq_ln", "rq"))
        s4.close()
        s4g = ExitStack()
        fg = {n: sb(f"fg_{n}", [BH, T], scope=s4g) for n in ("f", "abs", "e", "l1", "lf", "c", "negc", "one")}
        s4g.close()
        s5 = ExitStack()
        sb("y_kept", [P, BH * SEQ], scope=s5)
        hT5 = sb("h5", [P, KT, T], scope=s5)
        hg = [sb(f"hg{i}", [P, SEQ], scope=s5) for i in range(2)]
        stat5 = sb("stat5", [P, 2, NT], scope=s5)
        s5.close()
        o_nat = sb("o_nat", [P, NT, D], scope=s5)
        s5.close()

        mm = [ctx.enter_context(nc.psum_tensor(f"mm{i}", [P, 2 * BANK], F32)) for i in range(2)]
        ax = [ctx.enter_context(nc.psum_tensor(f"ax{i}", [P, 2 * BANK], F32)) for i in range(2)]

        def halves(ps, n=HT, rows=P):
            return ps[0:rows, :].rearrange("p (a n) -> p a n", a=2)[:, :, 0:n]

        def two(ap):
            return ap.rearrange("p (a n) -> p a n", a=2)

        PT_ORDER = (0, 1, 2, NT, 3)

        def transposed_p(i):
            if i == NT:
                return ax[0][0:META, 0:SEQ], PM[M0, :], PM[M1, :]
            base = 0 if i % 2 else BANK
            slots = slice(i, 4 * i + 1, 3)
            return (ax[1][:, base:base + (i + 1) * P].rearrange("p (j n) -> p j n", n=P), PTh[:, slots, :],
                    PTl[:, slots, :])

        X0 = BANK - META
        SCORES_AT = ((ax[0], 0), (ax[1], 0), (ax[1], BANK), (ax[0], 0), (ax[0], BANK))

        w_raw_ready = [sem(f"w_raw_ready{i}") for i in range(2)]
        wk_raw_ready = sem("wk_raw_ready")
        w_hi_ready, w_lo_ready, blk_done = sem("w_hi_ready"), sem("w_lo_ready"), sem("blk_done")
        meta_loaded = sem("meta_loaded")
        x_loaded = [sem(f"x_loaded{i}") for i in range(NT)]
        ones_ready, stat0_ready, diag0_ready, bcast0_done, rstd0_ready = (sem(n) for n in (
            "ones_ready", "stat0_ready", "diag0_ready", "bcast0_done", "rstd0_ready"))
        zeroed, qk_hi, qk_lo, v_hi, v_lo, w2_hi, w2_lo, og_ready, ss2_ready, ss_ready = (sem(n) for n in (
            "zeroed", "qk_hi", "qk_lo", "v_hi", "v_lo", "w2_hi", "w2_lo", "og_ready", "ss2_ready", "ss_ready"))
        (par_loaded, const_ready, ident0, par_tr, par_ready, x_tr, h_copied, h_stored, h_loaded,
         sq_ready, sumsq_done, ln_ready, rstd_ready, xt_ready, xh_ready, xl_ready) = (sem(n) for n in (
            "par_loaded", "const_ready", "ident0", "par_tr", "par_ready", "x_tr", "h_copied",
            "h_stored", "h_loaded", "sq_ready", "sumsq_done", "ln_ready", "rstd_ready", "xt_ready",
            "xh_ready", "xl_ready"))
        (pad_zero, xm_raw, xm_hi, cv_aff, xm_lo, taps, th1_ready, xc2_ready, xc_hi, xc_lo,
         qkv_mm, qkv_ev, qkv_hi, qkv_lo, wg_hi, wg_lo, gate_mm, gacc_ready, wg_loaded, v_tr, vn1_ev, qk_stored, v_stored) = (sem(n) for n in (
            "pad_zero", "xm_raw", "xm_hi", "cv_aff", "xm_lo", "taps", "th1_ready", "xc2_ready", "xc_hi",
            "xc_lo", "qkv_mm", "qkv_ev", "qkv_hi", "qkv_lo", "wg_hi", "wg_lo", "gate_mm",
            "gacc_ready", "wg_loaded", "v_tr", "vn1_ev",
            "qk_stored", "v_stored"))
        xc_stored = [sem(f"xc_stored{i}") for i in range(2)]
        (gb_ready, gsel_done, grow, gexp, a_tr, grow_stored, qk_loaded, v_loaded, negm_loaded,
         floor_loaded, xc_loaded, e_arg, e_ready, e_diag, sc_done, w_ready, ot_ready, pv_done, dn_ready,
         rd_ready, g_ready, sqg_ready, sumg_done, th2_ready, mix_ready, gate2_ready, y_ready) = (
            sem(n) for n in (
            "gb_ready", "gsel_done", "grow", "gexp", "a_tr", "grow_stored", "qk_loaded",
            "v_loaded", "negm_loaded", "floor_loaded", "xc_loaded", "e_arg", "e_ready", "e_diag", "sc_done",
            "w_ready", "ot_ready", "pv_done", "dn_ready", "rd_ready", "g_ready", "sqg_ready", "sumg_done",
            "th2_ready", "mix_ready", "gate2_ready", "y_ready"))
        y_stored = [sem(f"y_stored{i}") for i in range(2)]
        y_loaded, h_acc, h_stored2 = (sem(n) for n in ("y_loaded", "h_acc", "h_stored2"))
        h_loaded2 = [sem(f"h_loaded2_{i}") for i in range(2)]
        (f_row, fexp, negc_stored, negc_loaded, qkv4_ev, sq4_ready, sum4_done, ln4_ready, r4_ready, hat_ready,
         vtr4, v4_hi, v4_lo, rq_scaled, hat_hi, hat_lo, pt_hi, s4_done, sadd, smask, smax, sneg, pexp, sinv,
         pscaled, ptr_done, pt_lo, pv4_done,
         th4_ready, gate4_ready, y4_ready) = (sem(n) for n in (
            "f_row", "fexp", "negc_stored", "negc_loaded", "qkv4_ev", "sq4_ready", "sum4_done", "ln4_ready",
            "r4_ready", "hat_ready", "vtr4", "v4_hi", "v4_lo", "rq_scaled", "hat_hi", "hat_lo", "pt_hi",
            "s4_done", "sadd", "smask", "smax", "sneg", "pexp",
            "sinv", "pscaled", "ptr_done", "pt_lo", "pv4_done", "th4_ready", "gate4_ready", "y4_ready"))
        hg_ready, out_tr, raw_ready, stat5_ready, o_even, o_odd, out_stored = (sem(n) for n in (
            "hg_ready", "out_tr", "raw_ready", "stat5_ready", "o_even", "o_odd", "out_stored"))

        w_in_a = a_w_in[0].rearrange("(k p) m -> p k m", p=P)
        w_in_b = b_w_in[0].rearrange("(k p) m -> p k m", p=P)
        w_out_a = a_w_out[0].rearrange("(f k p) m -> f p k m", p=P, k=KT)
        w_out_b = b_w_out[0].rearrange("(k p) m -> p k m", p=P)
        w_q = a_w_q[0].rearrange("h (k p) m -> p (h k) m", p=P)
        w_k = a_w_k[0].rearrange("h (k p) m -> p (h k) m", p=P)
        w_v = a_w_v[0].rearrange("h (k p) m -> p (h k) m", p=P)
        w_g = a_w_gate[0].rearrange("(r p) g -> p r g", p=P)
        Z_B = 3 * BH * BD + BH

        def wait(eng, semaphore, value):
            if not (isinstance(value, int) and value <= 0):
                eng.wait_ge(semaphore, value)

        def flat(t):
            return t.rearrange("p a b -> p (a b)")

        block = ctx.enter_context(nc.Block())

        @block.sync
        def _(sp):
            def load(b, par_, src, cols=P, tiles=KT, at=0, done=None):
                if not (isinstance(b, int) and b < 2):
                    sp.wait_ge(w_lo_ready, b - 1)
                full = w_raw[par_][:, :].rearrange("p (k m) -> p k m", k=tiles)
                sp.dma_start(full[:, :, at:at + cols], src).then_inc(done or w_raw_ready[par_], 16)

            def load_xm(h, c):
                load(xm_block(h, c), c % 2, w_in_a[:, :, ds(h * DV + c * P, P)])

            def load_qkv(h, par_):
                b = qkv_block(h)
                load(b, par_, w_k[:, ds(h * CT, CT), :], DQK, CT, DQK, wk_raw_ready)
                sp.wait_ge(wk_raw_ready, h * 16 + 16)
                load(b, par_, w_q[:, ds(h * CT, CT), :], DQK, CT)
                load(b + 1, 1 - par_, w_v[:, ds(h * CT, CT), :], DV, CT)
                if not (isinstance(h, int) and h == 0):
                    sp.wait_ge(gate_mm, h * (2 * QT + CT))
                for r, n, at in ((0, QT, 0), (AH * QT, QT, QT), (2 * AH * QT, CT, 2 * QT)):
                    sp.dma_start(wg[:, at:at + n, :], w_g[:, ds(h * n + r, n), :]).then_inc(wg_loaded, 16)

            sp.dma_start(meta_nat[:, :], meta_tokens).then_inc(meta_loaded, 16)
            for i in range(NT):
                if i == NT // 2:
                    load_xm(0, 0)
                sp.dma_start(x_nat[:, i, :], x[0, i * P:(i + 1) * P, :]).then_inc(x_loaded[i], 16)
            for c in range(1, CT):
                load_xm(0, c)
            sp.wait_ge(xl_ready, KT)
            sp.wait_ge(h_stored, 16 * H_PARTS)

            def load_head_a1(h):
                load_xm(h, 0)
                load_qkv(h - 1, 1)
                for c in range(1, CT):
                    load_xm(h, c)

            def load_a2(h, k, b):
                part = (1 + k // CT) * AI + k % CT * P
                load(b, k % 2, w_in_a[:, :, ds(h * DV + part, P)])

            load_head_a1(1)
            with sp.Fori(2, AH) as h:
                load_head_a1(h)
            load_a2(0, 0, O0_BLOCK)
            load_qkv(AH - 1, 1)
            for k in range(1, A2_PER):
                load_a2(0, k, A2_0 + k)
            with sp.Fori(1, AH) as h:
                for k in range(A2_PER):
                    load_a2(h, k, h * A2_PER + (A2_0 + k))
            for f in range(2):
                with sp.Fori(0, KT // 2) as i:
                    for k in range(2):
                        load(i * 2 + (A3_0 + f * KT + k), k, w_out_a[f][:, :, ds(i * (2 * P) + k * P, P)])
            load(B1_0, B1_0 % 2, w_in_b[:, :, 3 * BH * BD:3 * BH * BD + P])
            with sp.Fori(0, BH) as h:
                for k in range(B1_PER):
                    part = (0, BH * BD, 2 * BH * BD, Z_B)[k]
                    load(h * B1_PER + (B1_0 + 1 + k), (B1_0 + 1 + k) % 2, w_in_b[:, :, ds(h * BD + part, P)])
            with sp.Fori(0, KT // 2) as i:
                for k in range(2):
                    load(i * 2 + (B2_0 + k), (B2_0 + k) % 2, w_out_b[:, :, ds(i * (2 * P) + k * P, P)])
            for i in range(NT):
                sp.wait_ge((o_even, o_odd)[i % 2], i // 2 + 1)
                sp.dma_start(out[0, i * P:(i + 1) * P, :], o_nat[:, i, :]).then_inc(out_stored, 16)
            sp.wait_ge(out_stored, 16 * NT)

        @block.gpsimd
        def _(pool):
            pool.memset(ident[:, :], 0.0).then_inc(ident0, 1)
            pool.memset(ones[:, :], 1.0).then_inc(ident0, 1)
            pool.memset(causal01[:, :], 1.0).then_inc(ident0, 1)
            pool.memset(causal_add[:, :], 0.0).then_inc(ident0, 1)
            pool.memset(eps_t[:, :], EPS).then_inc(ident0, 1)
            pool.wait_ge(ident0, 5)
            pool.affine_select(out=ident[:, :], in_=ident[:, :], compare_op=ALU.not_equal, fill=1.0, base=0,
                               pattern=[[-1, P]], channel_multiplier=1).then_inc(const_ready, 1)
            pool.affine_select(out=causal01[:, :], in_=causal01[:, :], compare_op=ALU.is_ge, fill=0.0, base=0,
                               pattern=[[1, P]], channel_multiplier=-1).then_inc(const_ready, 1)
            pool.affine_select(out=causal_add[:, :], in_=causal_add[:, :], compare_op=ALU.is_ge, fill=-1e30,
                               base=0, pattern=[[-1, P]], channel_multiplier=1).then_inc(const_ready, 1)
            for i in range(H_PARTS):
                w = KT // H_PARTS
                pool.wait_ge(h_copied, (i + 1) * w)
                pool.dma_start(h_d[:, i * w * T:(i + 1) * w * T],
                               flat(hT0[:, i * w:(i + 1) * w, :])).then_inc(h_stored, 16)

            def store_xc(h, c):
                pool.wait_ge(xc2_ready, h * CT + (c + 1))
                pool.dma_start(xc_d[:, ds(h * (CT * T) + c * T, T)], xc2[c % 2][:, :]).then_inc(xc_stored[c % 2], 16)

            def store_qkv(h):
                pool.wait_ge(qkv_ev, h * (2 * QT + CT) + 2 * QT)
                pool.dma_start(qk_d[ds(h, 1)].rearrange("a p n -> (a p) n"),
                               flat(qkv[:, 0:2 * QT, :])).then_inc(qk_stored, 16)
                pool.wait_ge(vn1_ev, h * NS + NS)
                dst = v_d[ds(h, 1)].rearrange("a p n -> (a p) n")
                pool.dma_start(dst[0:META, 0:DV], vn1[0:META, 0, :]).then_inc(v_stored, 16)
                pool.dma_start(dst[:, DV:NS * DV], flat(vn1[:, 1:NS, :])).then_inc(v_stored, 16)

            for c in range(CT):
                store_xc(0, c)
            store_qkv(0)
            for c in range(CT):
                store_xc(1, c)
            with pool.Fori(2, AH) as h:
                store_qkv(h - 1)
                for c in range(CT):
                    store_xc(h, c)
            store_qkv(AH - 1)

            def load_negm(h):
                pool.dma_start(negm_b[:, :], negm_d[ds(h, 1), :].broadcast_to([P, T])).then_inc(negm_loaded, 16)

            def load_qk(h):
                pool.dma_start(flat(qk2[:, :, :]),
                               qk_d[ds(h, 1)].rearrange("a p n -> (a p) n")).then_inc(qk_loaded, 16)

            def load_v(h):
                src = v_d[ds(h, 1)].rearrange("a p n -> (a p) n")
                pool.dma_start(v2[0:META, 0, :], src[0:META, 0:DV]).then_inc(v_loaded, 16)
                pool.dma_start(flat(v2[:, 1:NS, :]), src[:, DV:NS * DV]).then_inc(v_loaded, 16)

            def load_floor(h):
                pool.dma_start(floor_b[:, :], floor_d[ds(h, 1), :].broadcast_to([P, T])).then_inc(floor_loaded, 16)

            def load_xc(h):
                pool.dma_start(flat(xcl2[:, :, :]), xc_d[:, ds(h * (CT * T), CT * T)]).then_inc(xc_loaded, 16)

            def sum_squares_a2(h):
                for c in range(1, CT):
                    pool.wait_ge(sqg_ready, h * CT + (c + 1))
                    if c > 1:
                        pool.wait_ge(ss2_ready, h * (CT - 1) + (c - 1))
                    pool.tensor_tensor(rtmp[:, :], sq[0][:, :] if c == 1 else rtmp[:, :], sq[c % 2][:, :],
                                       ALU.add).then_inc(ss2_ready, 1)

            def store_y(h):
                for c in range(CT):
                    pool.wait_ge(y_ready, h * CT + (c + 1))
                    pool.dma_start(y_d[:, ds(h * (CT * T) + c * T, T)], yb[c % 2][:, :]).then_inc(y_stored[c % 2], 16)

            def sum_squares(r, w):
                pool.memset(rtmp[:, 0:w], 0.0).then_inc(ss_ready, 2)
                with pool.Fori(0, KT // 2) as i:
                    for k in range(2):
                        pool.wait_ge(sq_ready, i * 2 + (r * KT + k + 1))
                        pool.wait_ge(ss_ready, i * 2 + (r * (KT + 2) + 2 + k))
                        pool.tensor_tensor(rtmp[:, 0:w], rtmp[:, 0:w], sq[k][:, 0:w], ALU.add).then_inc(ss_ready, 1)

            pool.wait_ge(qk_stored, 16 * AH)
            pool.wait_ge(v_stored, 32 * AH)
            for i in range(2):
                pool.wait_ge(xc_stored[i], 16 * AH * CT // 2)
            pool.wait_ge(gate_mm, AH * (2 * QT + CT))
            load_qk(0)
            load_v(0)
            pool.wait_ge(grow, 12)
            pool.wait_ge(gexp, 3)
            pool.dma_start(negm_d, gr["negm"][:, :]).then_inc(grow_stored, 16)
            pool.dma_start(floor_d, gr["floor"][:, :]).then_inc(grow_stored, 16)
            pool.wait_ge(grow_stored, 32)
            load_negm(0)
            load_floor(0)
            load_xc(0)
            with pool.Fori(0, AH - 1) as h:
                pool.wait_ge(e_arg, h * NS + NS)
                load_negm(h + 1)
                pool.wait_ge(sc_done, h * NS + NS)
                load_qk(h + 1)
                pool.wait_ge(pv_done, h * (1 + CT) + (1 + CT))
                load_v(h + 1)
                load_floor(h + 1)
                sum_squares_a2(h)
                store_y(h)
                load_xc(h + 1)
            for i in range(2):
                pool.wait_ge(y_stored[i], 16 * AH * CT // 4)
            pool.wait_ge(pv_done, (1 + CT) * AH)
            pool.dma_start(flat(y_in[:, :, :]), y_d[:, 0:KT * T]).then_inc(y_loaded, 16)
            sum_squares_a2(AH - 1)
            store_y(AH - 1)
            for i in range(2):
                pool.wait_ge(y_stored[i], 16 * AH * CT // 2)
            pool.dma_start(flat(hT3[:, :, :]), h_d).then_inc(h_loaded, 16)
            pool.wait_ge(xl_ready, 2 * KT)
            pool.dma_start(flat(y_in[:, :, :]), y_d[:, KT * T:2 * KT * T]).then_inc(y_loaded, 16)
            pool.wait_ge(rstd_ready, AH)
            sum_squares(0, T)
            pool.wait_ge(h_acc, 2 * KT)
            pool.dma_start(h_d, flat(hT3[:, :, :])).then_inc(h_stored2, 16)

            pool.wait_ge(f_row, 6)
            pool.dma_start(negc_d, fg["negc"][:, :]).then_inc(negc_stored, 16)
            pool.wait_ge(negc_stored, 16)
            pool.dma_start(negc_b[:, :], negc_d[0:1, :].broadcast_to([P, T])).then_inc(negc_loaded, 16)
            with pool.Fori(1, BH) as h:
                pool.wait_ge(sadd, h * NT)
                pool.dma_start(negc_b[:, :], negc_d[ds(h, 1), :].broadcast_to([P, T])).then_inc(negc_loaded, 16)
            pool.wait_ge(y4_ready, BH)
            for i, (j0, j1) in enumerate(((0, 2), (2, KT))):
                pool.dma_start(flat(hT5[:, j0:j1, :]), h_d[:, j0 * T:j1 * T]).then_inc(h_loaded2[i], 16)
            pool.wait_ge(r4_ready, 2 * BH)
            sum_squares(1, SEQ)

        @block.scalar
        def _(act):
            def round_w(b, par_):
                if isinstance(b, int) and b >= BLOCKS:
                    return
                act.wait_ge(w_raw_ready[par_], b * 8 + (16 - 8 * par_))
                if not (isinstance(b, int) and b < 2):
                    act.wait_ge(blk_done, b - 1)
                act.activation(w_hi[par_][:, :], w_raw[par_][:, :], ACT.Copy).then_inc(w_hi_ready, 1)

            def inv_sqrt(src, dst, scale, tmp, n, view, ln, done):
                act.activation(view(tmp), src, ACT.Ln, bias=eps_t[:, 0:1], scale=scale).then_inc(ln, 1)
                act.wait_ge(ln, n)
                act.activation(dst, tmp, ACT.Exp, scale=-0.5).then_inc(done, 1)

            cw = a_conv_w[0].rearrange("c (j p) -> (c j) p", p=P)
            act.dma_start(par_rows[:, 0, :], cw).then_inc(par_loaded, 16)
            rows = [(a_conv_b[0], FT, 1, 0), (a_head_norm[0], FT, 1, FT), (a_skip[0], FT, 1, 2 * FT),
                    (a_norm[0], KT, 1, 3 * FT), (b_norm[0], KT, 1, 3 * FT + KT), (final_norm, KT, 2, 0),
                    (b_q_norm[0], 1, 2, KT), (b_k_norm[0], 1, 2, KT + 1)]
            for src, n, t, at in rows:
                act.dma_start(par_rows[at:at + n, t, :],
                              src.rearrange("(j p) -> j p", p=P)).then_inc(par_loaded, 16)
            act.dma_start(bf[:, :], b_b_f[0].rearrange("(g a) -> g a", a=1)).then_inc(par_loaded, 16)
            act.wait_ge(ident0, 5)
            act.activation(ones_r[:, :], ones[:, :], ACT.Copy).then_inc(ones_ready, 1)
            act.wait_ge(meta_loaded, 16)
            act.activation(flat(hT0[:, :, :])[0:META, 0:D], meta_nat[:, :], ACT.Square,
                           accum_out=stat0[0:META, 0, NT:NT + 1]).then_inc(stat0_ready, 1)
            act.wait_ge(stat0_ready, 1)
            for i in range(NT):
                if i == NT // 2:
                    round_w(0, 0)
                act.wait_ge(x_loaded[i], 16)
                act.activation(flat(hT0[:, :, :])[:, i * D:(i + 1) * D], x_nat[:, i, :], ACT.Square,
                               accum_out=stat0[:, 0, i:i + 1]).then_inc(stat0_ready, 1)
            act.wait_ge(stat0_ready, NT + 1)
            for r, c0, c1 in ((P, 0, NT), (META, NT, NT + 1)):
                act.activation(stat0[0:r, 1, c0:c1], stat0[0:r, 0, c0:c1], ACT.Ln, bias=eps_t[0:r, 0:1],
                               scale=1.0 / D).then_inc(stat0_ready, 1)
            act.wait_ge(stat0_ready, NT + 3)
            for r, c0, c1 in ((P, 0, NT), (META, NT, NT + 1)):
                act.activation(stat0[0:r, 2, c0:c1], stat0[0:r, 1, c0:c1], ACT.Exp, scale=-0.5).then_inc(stat0_ready, 1)

            def copy_h(j):
                act.wait_ge(x_tr, j + 1)
                act.activation(hT0[:, j, :], ax[j % 2][:, X0:2 * BANK], ACT.Copy).then_inc(h_copied, 1)

            copy_h(0)
            copy_h(1)
            round_w(1, 1)
            for j in range(KT):
                act.wait_ge(xt_ready, j + 1)
                act.activation(XH[:, j, :], xt0[j % 2][:, :], ACT.Copy).then_inc(xh_ready, 1)
                if j + 2 < KT:
                    copy_h(j + 2)

            act.wait_ge(xl_ready, KT)
            act.wait_ge(h_stored, 16 * H_PARTS)
            act.dma_start(bg[:, :], a_b_gate[0].rearrange("(g a) -> g a", a=1)).then_inc(par_loaded, 16)

            def conv_tile(h, c, n, npar):
                b = xm_block(h, c)
                e = h * CT + c
                p = c % 2
                src = halves(mm[p])
                act.wait_ge(blk_done, b + 1)
                if not (isinstance(h, int) and h == 0 and c < 2):
                    act.wait_ge(taps, e * 3 - 3)
                act.activation(two(xm_pad[p][:, TAPS - 1:]), src, ACT.Copy).then_inc(xm_raw, 1)
                act.activation(two(xmh[:, c, :]), src, ACT.Copy).then_inc(xm_hi, 1)
                if not (isinstance(h, int) and h == 0 and c < 2):
                    act.wait_ge(xc2_ready, e - 1)
                act.activation(two(conv[p][:, :]), src, ACT.Identity,
                               bias=par[:, ds(h * CT + (C_CB + c), 1)],
                               scale=par[:, ds(h * CT + (C_CW + (TAPS - 1) * FT + c), 1)]).then_inc(cv_aff, 1)
                round_w(n, npar)
                act.wait_ge(taps, e * 3 + 3)
                act.activation(th1[:, :], conv[p][:, :], ACT.Tanh, scale=0.5).then_inc(th1_ready, 1)
                act.wait_ge(xc2_ready, e + 1)
                act.activation(xch[:, c, :], xc2[p][:, :], ACT.Copy, scale=0.5).then_inc(xc_hi, 1)

            def evacuate_qkv(h, b):
                NJ = 2 * QT + CT
                act.wait_ge(wg_loaded, h * 48 + 48)
                if not (isinstance(h, int) and h == 0):
                    act.wait_ge(gate_mm, h * NJ)
                    act.wait_ge(qk_stored, h * 16)
                act.activation(wgp[:, :, 0:NG], wg[:, :, :], ACT.Copy).then_inc(wg_hi, 1)
                for j in range(2 * QT + CT):
                    if j == 2 * QT and not (isinstance(h, int) and h == 0):
                        act.wait_ge(v_tr, h * NS)
                    act.wait_ge(qkv_mm, h * 8 + (j + 1))
                    act.activation(two(qkv[:, j, :]), halves(ax[j % 2]), ACT.Copy).then_inc(qkv_ev, 1)
                    if j >= 2:
                        act.wait_ge(gate_mm, h * NJ + (j - 1))
                    act.activation(two(gh[j % 2][:, :]), halves(ax[j % 2]), ACT.Copy).then_inc(qkv_hi, 1)
                    if j == 2 * QT - 1:
                        round_w(b + 2, 1)

            for c in range(CT):
                conv_tile(0, c, c + 2, c % 2)
            act.wait_ge(par_loaded, 16 * 11)

            def head_a1(h):
                b0 = xm_block(h, 0)
                round_w(b0 + 2, 0)
                evacuate_qkv(h - 1, b0 + 1)
                for c in range(CT):
                    conv_tile(h, c, b0 + (4 + c), c % 2)

            head_a1(1)
            with act.Fori(2, AH) as h:
                head_a1(h)
            round_w(O0_BLOCK + 2, 0)
            evacuate_qkv(AH - 1, O0_BLOCK + 1)

            act.wait_ge(v_stored, 32 * AH)
            for i in range(2):
                act.wait_ge(xc_stored[i], 16 * AH * CT // 2)

            def gates():
                act.wait_ge(grow, 3)
                act.activation(gr["e"][:, :], gr["abs"][:, :], ACT.Exp, scale=-1.0).then_inc(gexp, 1)
                act.wait_ge(gexp, 1)
                act.activation(gr["e"][:, :], gr["e"][:, :], ACT.Ln, bias=1.0).then_inc(gexp, 1)
                act.wait_ge(grow, 9)
                act.activation(gr["floor"][:, :], gr["m"][:, :], ACT.Exp, scale=-1.0).then_inc(gexp, 1)

            def round_qk(h):
                act.wait_ge(qk_loaded, h * 16 + 16)
                act.activation(flat(qkh[:, :, :]), flat(qk2[:, :, :]), ACT.Copy).then_inc(qk_hi, 1)

            def round_v(h):
                act.wait_ge(v_loaded, h * 32 + 32)
                for m in (M0, M1):
                    act.activation(vh[m, 0, :], v2[M0, 0, :], ACT.Copy).then_inc(v_hi, 1)
                act.activation(flat(vh[:, 1:NS, :]), flat(v2[:, 1:NS, :]), ACT.Copy).then_inc(v_hi, 1)

            def exponentials(h):
                act.wait_ge(e_arg, h * NS + NS)
                for rows, c0, c1 in ((META, 0, T), (P, T, E_OFF[NS])):
                    e = EW[0:rows, c0:c1]
                    act.activation(e, e, ACT.Exp).then_inc(e_ready, 1)

            def round_w2(h, j):
                n = S_TILES[j][1]
                cols = slice(E_OFF[j], E_OFF[j + 1])
                act.wait_ge(w_ready, h * NS + (j + 1))
                act.activation(EWh[0:n, cols], EW[0:n, cols], ACT.Copy).then_inc(w2_hi, 1)
                if j == 0:
                    act.activation(EWh[M2, cols], EW[M0, cols], ACT.Copy).then_inc(w2_hi, 1)

            def o_gate(h, c):
                b = h * A2_PER + A2_0
                act.wait_ge(blk_done, b + (c + 1))
                wait(act, y_ready, h * CT)
                act.activation(two(OT[:, c, :]), halves(mm[c % 2]), ACT.Tanh, scale=0.5).then_inc(ot_ready, 1)
                round_w(b + (c + 2), c % 2)

            def head_a2(h, first=False, last=False):
                b = h * A2_PER + A2_0
                if first:
                    o_gate(h, 0)
                    gates()
                    o_gate(h, 1)
                    round_qk(h)
                    act.activation(vh[0:MROWS, 0, :], rstd[0:MROWS, 0:DV], ACT.Copy, scale=0.0).then_inc(zeroed, 1)
                    act.wait_ge(zeroed, 1)
                    round_v(h)
                    exponentials(h)
                    act.activation(EWh[0:MROWS, 0:T], rstd[0:MROWS, :], ACT.Copy, scale=0.0).then_inc(zeroed, 1)
                    act.wait_ge(zeroed, 2)
                else:
                    round_qk(h)
                    o_gate(h, 0)
                    exponentials(h)
                    round_v(h)
                for j in range(3):
                    round_w2(h, j)
                o_gate(h, 2 if first else 1)
                for j in range(3, NS):
                    round_w2(h, j)
                for c in range(3 if first else 2, CT):
                    o_gate(h, c)
                for c in range(CT):
                    act.wait_ge(g_ready, h * CT + (c + 1))
                    if c >= 2:
                        act.wait_ge(ss2_ready, h * (CT - 1) + (c - 1))
                    act.activation(sq[c % 2][:, :], OT[:, c, :], ACT.Square).then_inc(sqg_ready, 1)
                for c in range(CT):
                    k = CT + c
                    if c == 0:
                        round_w(b + (k + 2), 0)
                        act.wait_ge(sumg_done, h + 1)
                        wait(act, y_ready, h * CT)
                        inv_sqrt(halves(ax[0]), rstd[:, :], 0.25 / DV, rtmp[:, :], h + 1, two, ln_ready, rstd_ready)
                    act.wait_ge(blk_done, b + (k + 1))
                    wait(act, y_ready, h * CT + (c - 1))
                    act.activation(two(th2[c % 2][:, :]), halves(mm[k % 2]), ACT.Tanh, scale=0.5).then_inc(th2_ready, 1)
                    if c > 0 and not (last and c == CT - 1):
                        round_w(b + (k + 2), c % 2)

            head_a2(0, True)
            with act.Fori(1, AH - 1) as h:
                head_a2(h)
            head_a2(AH - 1, last=True)

            def round_x(src, n=T, weights=None):
                for j in range(KT):
                    if j == W_AFTER and weights is not None:
                        round_w(weights, weights % 2)
                    act.activation(XH[:, j, 0:n], src[:, j, :], ACT.Copy).then_inc(xh_ready, 1)

            def tile_a3(f, i, k, weights=True):
                if weights:
                    round_w(i * 2 + (A3_0 + f * KT + 2 + k), k)
                if f:
                    act.wait_ge(h_acc, i * 2 + (KT + k + 1))
                    act.wait_ge(ss_ready, i * 2 + (k + 1))
                    row = hT3[:, ds(i * 2 + k, 1), :].rearrange("p a n -> p (a n)")
                    act.activation(sq[k][:, :], row, ACT.Square).then_inc(sq_ready, 1)

            for f in range(2):
                act.wait_ge(y_loaded, 16 * (f + 1))
                act.wait_ge(blk_done, A3_0 + f * KT)
                round_x(y_in, T, A3_0 + f * KT + 1)
                with act.Fori(0, KT // 2 - 1) as i:
                    for k in range(2):
                        tile_a3(f, i, k)
                for k in range(2):
                    tile_a3(f, KT // 2 - 1, k, k == 0)
            act.wait_ge(sumsq_done, 1)
            inv_sqrt(halves(ax[0]), rstd[:, :], 1.0 / D, rtmp[:, :], AH + 1, two, ln_ready, rstd_ready)
            for j in range(KT):
                if j == W_AFTER:
                    round_w(B1_0 + 1, (B1_0 + 1) % 2)
                act.wait_ge(xt_ready, KT + j + 1)
                act.activation(XH[:, j, :], xt3[j % 2][:, :], ACT.Copy).then_inc(xh_ready, 1)

            act.wait_ge(f_row, 2)
            act.activation(fg["e"][:, :], fg["abs"][:, :], ACT.Exp, scale=-1.0).then_inc(fexp, 1)
            act.wait_ge(fexp, 1)
            act.activation(fg["l1"][:, :], fg["e"][:, :], ACT.Ln, bias=1.0).then_inc(fexp, 1)
            round_w(B1_0 + 2, B1_0 % 2)
            act.wait_ge(h_stored2, 16)
            act.activation(Vm[:, :], rstd[0:MROWS, 0:BD], ACT.Copy, scale=0.0).then_inc(zeroed, 1)
            act.activation(PM[:, :], rstd[0:MROWS, 0:SEQ], ACT.Copy, scale=0.0).then_inc(zeroed, 1)
            act.wait_ge(zeroed, 4)

            def softmax_exp(p_, i):
                act.wait_ge(sneg, p_ * NT + (i + 1))
                w = S_TILES[i + 1][0] + P
                act.activation(PR[:, i, 0:w], SS[i % 2][:, 0:w], ACT.Exp, bias=s_neg[:, i:i + 1],
                               accum_out=s_sum[:, i:i + 1]).then_inc(pexp, 1)

            def high_pt(p_, n):
                act.wait_ge(ptr_done, p_ * (NT + 1) + (n + 1))
                src, high, _ = transposed_p(PT_ORDER[n])
                act.activation(high, src, ACT.Copy).then_inc(pt_hi, 1)
                if PT_ORDER[n] == NT:
                    act.activation(PM[M2, :], src, ACT.Copy).then_inc(pt_hi, 1)

            def head_b1(h, first, attend):
                b = h * B1_PER + (B1_0 + 1)
                q0 = B1_0 + 1
                act.wait_ge(blk_done, b + 1)
                if not first:
                    act.wait_ge(hat_lo, h * 2)
                act.activation(QR[:, :], mm[0][:, 0:SEQ], ACT.Copy).then_inc(qkv4_ev, 1)
                act.activation(sq[0][:, 0:SEQ], mm[0][:, 0:SEQ], ACT.Square).then_inc(sq4_ready, 1)
                round_w(b + 2, q0 % 2)
                if attend:
                    for i in range(3):
                        softmax_exp(h - 1, i)
                act.wait_ge(blk_done, b + 2)
                act.activation(two(KR[:, :]), halves(mm[1]), ACT.Copy).then_inc(qkv4_ev, 1)
                act.activation(two(sq[1][:, :]), halves(mm[1]), ACT.Square).then_inc(sq4_ready, 1)
                round_w(b + 3, (q0 + 1) % 2)
                if attend:
                    softmax_exp(h - 1, 3)
                    high_pt(h - 1, 0)
                act.wait_ge(blk_done, b + 3)
                if not first:
                    act.wait_ge(vtr4, h * 2)
                act.activation(two(VT[:, :]), halves(mm[0]), ACT.Copy).then_inc(qkv4_ev, 1)
                if attend:
                    for n in range(1, NT + 1):
                        high_pt(h - 1, n)
                round_w(b + 4, q0 % 2)
                act.wait_ge(blk_done, b + 4)
                row = Y[:, ds(h, 1), :].rearrange("p a n -> p (a n)")
                act.activation(row, mm[1][:, 0:SEQ], ACT.Tanh, scale=0.5).then_inc(th4_ready, 1)
                act.wait_ge(sum4_done, h * 2 + 1)
                act.activation(two(rtmp[:, :]), halves(mm[0]), ACT.Ln, bias=eps_t[:, 0:1], scale=1.0 / BD).then_inc(ln4_ready, 1)
                act.wait_ge(sum4_done, h * 2 + 2)
                act.activation(rq_ln[:, :], ax[0][:, 0:NT], ACT.Ln, bias=eps_t[:, 0:1], scale=1.0 / BD).then_inc(ln4_ready, 1)
                act.wait_ge(ln4_ready, h * 2 + 2)
                act.activation(rstd[:, :], rtmp[:, :], ACT.Exp, scale=-0.5).then_inc(r4_ready, 1)
                act.activation(rq[:, :], rq_ln[:, :], ACT.Exp, scale=-0.5).then_inc(r4_ready, 1)
                act.wait_ge(vtr4, h * 2 + 2)
                act.activation(Vh[:, :], ax[1][:, 0:NT * BD], ACT.Copy).then_inc(v4_hi, 1)
                for m in (M0, M1):
                    act.activation(Vm[m, :], ax[0][M0, BANK:BANK + BD], ACT.Copy).then_inc(v4_hi, 1)
                act.wait_ge(hat_ready, h + 1)
                act.activation(Kh[:, :], KR[:, :], ACT.Copy).then_inc(hat_hi, 1)
                act.wait_ge(qkv4_ev, h * 3 + 3)
                act.activation(Qh[:, :], QR[:, :], ACT.Copy).then_inc(hat_hi, 1)
                round_w(b + 5, (q0 + 1) % 2)

            head_b1(0, True, False)
            with act.Fori(1, BH) as h:
                head_b1(h, False, True)

            def round_y(tiles):
                for j in tiles:
                    act.activation(XH[:, j, 0:SEQ], Y[:, j, :], ACT.Copy).then_inc(xh_ready, 1)

            act.wait_ge(y4_ready, BH - 1)
            act.wait_ge(blk_done, B2_0)
            round_y(range(0, 5))
            for i in range(3):
                softmax_exp(BH - 1, i)
            round_y(range(5, 8))
            softmax_exp(BH - 1, 3)
            high_pt(BH - 1, 0)
            round_y(range(8, 11))
            for n in range(1, NT + 1):
                high_pt(BH - 1, n)
            round_y(range(11, KT - 1))
            act.wait_ge(y4_ready, BH)
            round_y([KT - 1])

            def tile_b2(i, k, more=True):
                if more:
                    round_w(i * 2 + (B2_0 + 2 + k), (B2_0 + k) % 2)
                act.wait_ge(h_acc, i * 2 + (2 * KT + k + 1))
                act.wait_ge(ss_ready, i * 2 + (KT + 2 + k + 1))
                row = hT5[:, ds(i * 2 + k, 1), META:T].rearrange("p a n -> p (a n)")
                act.activation(sq[k][:, 0:SEQ], row, ACT.Square).then_inc(sq_ready, 1)
                if not (isinstance(i, int) and i == 0):
                    act.wait_ge(out_tr, i * 2 + (k - 1))
                act.activation(hg[k][:, :], row, ACT.Copy, scale=par[:, ds(i * 2 + (C_FN + k), 1)]).then_inc(hg_ready, 1)

            for k in range(2):
                tile_b2(0, k)
            with act.Fori(1, KT // 2 - 1) as i:
                for k in range(2):
                    tile_b2(i, k)
            for k in range(2):
                tile_b2(KT // 2 - 1, k, False)
            act.wait_ge(sumsq_done, 2)
            act.activation(stat5[:, 0, :], ax[0][:, 0:NT], ACT.Ln, bias=eps_t[:, 0:1], scale=1.0 / D).then_inc(stat5_ready, 1)
            act.wait_ge(stat5_ready, 1)
            act.activation(stat5[:, 1, :], stat5[:, 0, :], ACT.Exp, scale=-0.5).then_inc(stat5_ready, 1)
            act.wait_ge(stat5_ready, 2)
            act.wait_ge(raw_ready, KT)
            for i in range(1, NT, 2):
                act.activation(o_nat[:, i, :], o_nat[:, i, :], ACT.Copy, scale=stat5[:, 1, i:i + 1]).then_inc(o_odd, 1)

        @block.vector
        def _(dve):
            def low_w(b, par_):
                if isinstance(b, int) and b >= BLOCKS:
                    return
                dve.wait_ge(w_hi_ready, b + 1)
                dve.tensor_tensor(w_lo[par_][:, :], w_raw[par_][:, :], w_hi[par_][:, :].bitcast(F32),
                                  ALU.subtract).then_inc(w_lo_ready, 1)


            def norm_tile(src, j, gain, xt):
                if j >= 2:
                    dve.wait_ge(xl_ready, xl_base + j - 1)
                dve.scalar_tensor_tensor(out=xt[j % 2][:, :], in0=src, scalar=gain, in1=rstd[:, :],
                                         op0=ALU.mult, op1=ALU.mult).then_inc(xt_ready, 1)

            def low_x(src, j, n=T):
                dve.wait_ge(xh_ready, xl_base + j + 1)
                dve.tensor_tensor(XL[:, j, 0:n], src, XH[:, j, 0:n].bitcast(F32), ALU.subtract).then_inc(xl_ready, 1)

            xl_base = 0
            low_w(0, 0)
            dve.wait_ge(const_ready, 3)
            dve.wait_ge(stat0_ready, NT + 5)
            for i in range(NT):
                dve.tensor_scalar(diag0[:, i, :], ident[:, :], stat0[:, 2, i:i + 1], None, ALU.mult).then_inc(diag0_ready, 1)
            dve.tensor_scalar(diag0[0:META, NT, 0:META], ident[0:META, 0:META], stat0[0:META, 2, NT:NT + 1], None,
                              ALU.mult).then_inc(diag0_ready, 1)
            dve.wait_ge(par_tr, 3)
            dve.tensor_copy(par[:, :], mm[0][:, 0:NPAR]).then_inc(par_ready, 1)
            dve.wait_ge(par_ready, 1)
            dve.tensor_scalar(par[:, C_HN:C_AN], par[:, C_HN:C_AN], 0.25, None, ALU.mult).then_inc(par_ready, 1)
            dve.tensor_tensor(par[:, C_KN:C_KN + 1], par[:, C_KN:C_KN + 1], par[:, C_QN:C_QN + 1], ALU.mult).then_inc(par_ready, 1)
            dve.wait_ge(par_ready, 3)
            dve.wait_ge(bcast0_done, 1)
            dve.tensor_copy(rstd[:, :], mm[1][:, X0:2 * BANK]).then_inc(rstd0_ready, 1)
            dve.wait_ge(rstd0_ready, 1)
            for j in range(KT + 1):
                if j < KT:
                    dve.wait_ge(h_copied, j + 1)
                    norm_tile(hT0[:, j, :], j, par[:, C_AN + j:C_AN + j + 1], xt0)
                if j == 2:
                    low_w(1, 1)
                if j > 0:
                    low_x(xt0[(j - 1) % 2][:, :], j - 1)

            dve.wait_ge(xl_ready, KT)
            dve.wait_ge(h_stored, 16 * H_PARTS)
            for i in range(2):
                dve.memset(xm_pad[i][:, 0:TAPS - 1], 0.0).then_inc(pad_zero, 1)
            dve.memset(gacc[:, :], 0.0).then_inc(gacc_ready, 1)
            dve.wait_ge(pad_zero, 2)

            def conv_tile(h, c, n, npar):
                e = h * CT + c
                p = c % 2
                dve.wait_ge(xm_hi, e + 1)
                dve.tensor_tensor(xml[:, c, :], xm_pad[p][:, TAPS - 1:], xmh[:, c, :].bitcast(F32),
                                  ALU.subtract).then_inc(xm_lo, 1)
                dve.wait_ge(cv_aff, e + 1)
                for k in range(TAPS - 1):
                    tap = TAPS - 2 - k
                    if k:
                        dve.wait_ge(taps, e * 3 + k)
                    dve.scalar_tensor_tensor(out=conv[p][:, :], in0=xm_pad[p][:, tap:tap + T],
                                             scalar=par[:, ds(h * CT + (C_CW + tap * FT + c), 1)],
                                             in1=conv[p][:, :], op0=ALU.mult, op1=ALU.add).then_inc(taps, 1)
                low_w(n, npar)
                dve.wait_ge(th1_ready, e + 1)
                if not (isinstance(h, int) and h == 0 and c < 2):
                    dve.wait_ge(xc_stored[p], h * (8 * CT) + (c // 2) * 16)
                    dve.wait_ge(xc_lo, e - 1)
                dve.scalar_tensor_tensor(out=xc2[p][:, :], in0=th1[:, :], scalar=1.0, in1=conv[p][:, :],
                                         op0=ALU.add, op1=ALU.mult).then_inc(xc2_ready, 1)
                dve.wait_ge(xc_hi, e + 1)
                dve.scalar_tensor_tensor(out=xcl[:, c, :], in0=xc2[p][:, :], scalar=0.5,
                                         in1=xch[:, c, :].bitcast(F32), op0=ALU.mult,
                                         op1=ALU.subtract).then_inc(xc_lo, 1)

            def low_gate_weights(h):
                dve.wait_ge(wg_hi, h + 1)
                dve.tensor_tensor(wgp[:, :, NG:], wg[:, :, :], wgp[:, :, 0:NG].bitcast(F32), ALU.subtract).then_inc(wg_lo, 1)

            def low_qkv(h, tiles):
                NJ = 2 * QT + CT
                for j in tiles:
                    dve.wait_ge(qkv_hi, h * NJ + (j + 1))
                    if j >= 2:
                        dve.wait_ge(gate_mm, h * NJ + (j - 1))
                    dve.tensor_tensor(gl[j % 2][:, :], qkv[:, j, :], gh[j % 2][:, :].bitcast(F32),
                                      ALU.subtract).then_inc(qkv_lo, 1)

            def finish_qkv(h):
                if not (isinstance(h, int) and h == 0):
                    dve.wait_ge(v_stored, h * 32)
                for i, (_, n) in enumerate(S_TILES):
                    if i == 2:
                        dve.wait_ge(gate_mm, h * (2 * QT + CT) + (2 * QT + CT))
                        dve.wait_ge(gacc_ready, h + 1)
                        dve.tensor_tensor(two(gacc[:, :]), two(gacc[:, :]), halves(mm[1], HT, 2 * NG),
                                          ALU.add).then_inc(gacc_ready, 1)
                    dve.wait_ge(v_tr, h * NS + (i + 1))
                    dve.tensor_copy(vn1[0:n, i, :], ax[i % 2][0:n, 0:BANK]).then_inc(vn1_ev, 1)

            for c in range(CT):
                conv_tile(0, c, c + 2, c % 2)

            def head_a1(h):
                b0 = xm_block(h, 0)
                low_w(b0 + 2, 0)
                low_gate_weights(h - 1)
                low_qkv(h - 1, range(2 * QT))
                low_w(b0 + 3, 1)
                low_qkv(h - 1, range(2 * QT, 2 * QT + CT))
                finish_qkv(h - 1)
                for c in range(CT):
                    conv_tile(h, c, b0 + (4 + c), c % 2)

            head_a1(1)
            with dve.Fori(2, AH) as h:
                head_a1(h)
            low_w(O0_BLOCK + 2, 0)
            low_gate_weights(AH - 1)
            low_qkv(AH - 1, range(2 * QT))
            low_w(O0_BLOCK + 3, 1)
            low_qkv(AH - 1, range(2 * QT, 2 * QT + CT))
            finish_qkv(AH - 1)

            dve.wait_ge(gacc_ready, AH + 1)
            dve.wait_ge(par_loaded, 16 * 11)
            dve.tensor_scalar(gacc[0:NG, :], gacc[0:NG, :], bg[:, 0:1], None, ALU.add).then_inc(gb_ready, 1)
            dve.tensor_tensor(sel[:, :], ident[0:2 * NG, 0:NG], ident[0:2 * NG, NG:2 * NG], ALU.add).then_inc(gb_ready, 1)
            dve.wait_ge(gsel_done, 2)
            dve.wait_ge(qk_stored, 16 * AH)
            dve.wait_ge(v_stored, 32 * AH)
            for i in range(2):
                dve.wait_ge(xc_stored[i], 16 * AH * CT // 2)
            dve.tensor_copy(two(gr["ig"][:, :]), halves(ax[0], HT, AH)).then_inc(grow, 1)
            dve.tensor_copy(two(gr["f"][:, :]), halves(ax[1], HT, AH)).then_inc(grow, 1)
            dve.wait_ge(grow, 2)
            dve.scalar_tensor_tensor(out=gr["abs"][:, :], in0=gr["f"][:, :], scalar=-1.0, in1=gr["f"][:, :],
                                     op0=ALU.mult, op1=ALU.max).then_inc(grow, 1)
            dve.memset(gr["one"][:, :], 1.0).then_inc(grow, 1)
            low_w(A2_0 + 2, 0)
            dve.wait_ge(gexp, 2)
            dve.scalar_tensor_tensor(out=gr["lf"][:, :], in0=gr["f"][:, :], scalar=0.0, in1=gr["e"][:, :],
                                     op0=ALU.min, op1=ALU.subtract).then_inc(grow, 1)
            dve.wait_ge(grow, 5)
            dve.tensor_tensor_scan(gr["B"][:, :], gr["one"][:, :], gr["lf"][:, :], 0.0, ALU.mult, ALU.add).then_inc(grow, 1)
            dve.wait_ge(grow, 6)
            dve.tensor_tensor(gr["a"][:, :], gr["ig"][:, :], gr["B"][:, :], ALU.subtract).then_inc(grow, 1)
            dve.wait_ge(grow, 7)
            dve.tensor_tensor_scan(gr["M"][:, :], gr["one"][:, :], gr["a"][:, :], 0.0, ALU.mult, ALU.max).then_inc(grow, 1)
            dve.wait_ge(grow, 8)
            dve.tensor_tensor(gr["m"][:, :], gr["B"][:, :], gr["M"][:, :], ALU.add).then_inc(grow, 1)
            dve.tensor_scalar(gr["negm"][:, :], gr["M"][:, :], -1.0, None, ALU.mult).then_inc(grow, 1)
            dve.wait_ge(a_tr, 1)
            dve.tensor_copy(aT[0:META, 0, :], ax[0][0:META, 0:AH]).then_inc(grow, 1)
            dve.tensor_copy(flat(aT[:, 1:NS, :]), ax[0][:, AH:NS * AH]).then_inc(grow, 1)
            dve.wait_ge(grow, 12)

            def low_qk(h):
                dve.wait_ge(qk_hi, h + 1)
                dve.tensor_tensor(flat(qkl[:, :, :]), flat(qk2[:, :, :]), flat(qkh[:, :, :]).bitcast(F32), ALU.subtract).then_inc(qk_lo, 1)

            def low_v(h):
                dve.wait_ge(v_hi, h * 3 + 3)
                dve.tensor_tensor(vh[M2, 0, :], v2[M0, 0, :], vh[M0, 0, :].bitcast(F32),
                                  ALU.subtract).then_inc(v_lo, 1)
                dve.tensor_tensor(flat(vl[:, 1:NS, :]), flat(v2[:, 1:NS, :]), flat(vh[:, 1:NS, :]).bitcast(F32),
                                  ALU.subtract).then_inc(v_lo, 1)

            def exponents(h):
                dve.wait_ge(negm_loaded, h * 16 + 16)
                wait(dve, pv_done, h * (1 + CT))
                for j, (s, n) in enumerate(S_TILES):
                    dve.tensor_scalar(EW[0:n, E_OFF[j]:E_OFF[j + 1]], negm_b[0:n, s:T],
                                      aT[0:n, j, ds(h, 1)], 0.0, ALU.add, ALU.min).then_inc(e_arg, 1)

            def causal_w(h):
                dve.wait_ge(e_ready, h * 2 + 2)
                for j, (s, n) in enumerate(S_TILES):
                    dg = EW[0:n, E_OFF[j]:E_OFF[j] + n]
                    dve.tensor_tensor(dg, dg, causal01[0:n, 0:n], ALU.mult).then_inc(e_diag, 1)
                dve.wait_ge(e_diag, h * NS + NS)

            def w_rows(h, tiles):
                for j in tiles:
                    s, n = S_TILES[j]
                    dve.wait_ge(sc_done, h * NS + (j + 1))
                    ps, at = SCORES_AT[j]
                    row = EW[0:n, E_OFF[j]:E_OFF[j + 1]]
                    src = ps[0:n, at:at + T - s]
                    if j == 0:
                        row, src = two(row), halves(ps, HT, n)
                    dve.scalar_tensor_tensor(out=row, in0=src, scalar=float(DQK) ** -0.5, in1=row,
                                             op0=ALU.mult, op1=ALU.mult).then_inc(w_ready, 1)
                for j in tiles:
                    n = S_TILES[j][1]
                    cols = slice(E_OFF[j], E_OFF[j + 1])
                    dve.wait_ge(w2_hi, h * (NS + 1) + (j + 2))
                    dve.tensor_tensor(EWh[M1, cols] if j == 0 else EWl[0:n, cols], EW[0:n, cols], EWh[0:n, cols].bitcast(F32),
                                      ALU.subtract).then_inc(w2_lo, 1)

            def head_a2(h, first=False, last=False):
                b = h * A2_PER + A2_0
                if first:
                    low_w(b + 3, 1)
                low_qk(h)
                exponents(h)
                if not first:
                    low_w(b + 2, 0)
                causal_w(h)
                w_rows(h, range(3))
                if not first:
                    low_w(b + 3, 1)
                low_v(h)
                w_rows(h, range(3, NS))
                low_w(b + 4, 0)
                dve.wait_ge(floor_loaded, h * 16 + 16)
                dve.wait_ge(pv_done, h * (1 + CT) + 1)
                dve.scalar_tensor_tensor(out=two(dn[:, :]), in0=halves(ax[1]), scalar=-1.0, in1=two(floor_b[:, :]),
                                         op0=ALU.mult, op1=ALU.max).then_inc(dn_ready, 1)
                dve.wait_ge(dn_ready, h * 2 + 1)
                dve.tensor_tensor(two(dn[:, :]), halves(ax[1]), two(dn[:, :]), ALU.max).then_inc(dn_ready, 1)
                dve.wait_ge(dn_ready, h * 2 + 2)
                dve.reciprocal(dn[:, :], dn[:, :]).then_inc(rd_ready, 1)
                dve.wait_ge(rd_ready, h + 1)
                for c in range(CT):
                    dve.wait_ge(ot_ready, h * CT + (c + 1))
                    dve.scalar_tensor_tensor(out=OT[:, c, :], in0=OT[:, c, :], scalar=1.0, in1=dn[:, :],
                                             op0=ALU.add, op1=ALU.mult).then_inc(og_ready, 1)
                low_w(b + 5, 1)
                for c in range(CT):
                    dve.wait_ge(pv_done, h * (1 + CT) + (c + 2))
                    dve.wait_ge(og_ready, h * CT + (c + 1))
                    dve.tensor_tensor(two(OT[:, c, :]), halves(ax[c % 2]), two(OT[:, c, :]), ALU.mult).then_inc(g_ready, 1)
                low_w(b + 6, 0)
                dve.wait_ge(rstd_ready, h + 1)
                dve.wait_ge(xc_loaded, h * 16 + 16)
                for c in range(CT):
                    k = CT + c
                    y = yb[c % 2]
                    wait(dve, y_stored[c % 2], h * 32 + (c // 2) * 16)
                    dve.scalar_tensor_tensor(out=y[:, :], in0=OT[:, c, :],
                                             scalar=par[:, ds(h * CT + (C_HN + c), 1)], in1=rstd[:, :],
                                             op0=ALU.mult, op1=ALU.mult).then_inc(mix_ready, 1)
                    dve.wait_ge(mix_ready, h * (2 * CT) + (2 * c + 1))
                    dve.scalar_tensor_tensor(out=y[:, :], in0=xcl2[:, c, :],
                                             scalar=par[:, ds(h * CT + (C_SK + c), 1)], in1=y[:, :],
                                             op0=ALU.mult, op1=ALU.add).then_inc(mix_ready, 1)
                    dve.wait_ge(th2_ready, h * CT + (c + 1))
                    dve.scalar_tensor_tensor(out=two(th2[c % 2][:, :]), in0=two(th2[c % 2][:, :]), scalar=1.0,
                                             in1=halves(mm[k % 2]), op0=ALU.add, op1=ALU.mult).then_inc(gate2_ready, 1)
                    dve.wait_ge(gate2_ready, h * CT + (c + 1))
                    dve.wait_ge(mix_ready, h * (2 * CT) + (2 * c + 2))
                    dve.tensor_tensor(y[:, :], y[:, :], th2[c % 2][:, :], ALU.mult).then_inc(y_ready, 1)
                    if c < CT - 1 - last:
                        low_w(b + (k + 3), (k + 3) % 2)

            head_a2(0, True)
            with dve.Fori(1, AH - 1) as h:
                head_a2(h)
            head_a2(AH - 1, last=True)

            for f in range(2):
                xl_base = KT * (1 + f)
                dve.wait_ge(y_loaded, 16 * (f + 1))
                for j in range(KT):
                    if j == W_AFTER:
                        low_w(A3_0 + f * KT + 1, 1)
                    low_x(y_in[:, j, :], j)
                dve.wait_ge(h_loaded, 16)

                def add_a3(i, k, weights=True):
                    b = i * 2 + (A3_0 + f * KT + k)
                    dve.wait_ge(blk_done, b + 1)
                    if f:
                        dve.wait_ge(h_acc, i * 2 + (k + 1))
                    row = hT3[:, ds(i * 2 + k, 1), :].rearrange("p a (b n) -> p (a b) n", b=2)
                    dve.tensor_tensor(row, row, halves(mm[k]), ALU.add).then_inc(h_acc, 1)
                    if weights:
                        low_w(b + 2, k)

                with dve.Fori(0, KT // 2 - 1) as i:
                    for k in range(2):
                        add_a3(i, k)
                for k in range(2):
                    add_a3(KT // 2 - 1, k, k == 0)
            xl_base = 3 * KT
            dve.wait_ge(rstd_ready, AH + 1)
            for j in range(KT + 1):
                if j == W_AFTER + 1:
                    low_w(B1_0 + 1, (B1_0 + 1) % 2)
                if j < KT:
                    norm_tile(hT3[:, j, :], j, par[:, C_BN + j:C_BN + j + 1], xt3)
                if j > 0:
                    dve.wait_ge(xt_ready, KT + j)
                    low_x(xt3[(j - 1) % 2][:, :], j - 1)

            dve.wait_ge(h_stored2, 16)
            dve.wait_ge(xl_ready, 4 * KT)
            dve.wait_ge(blk_done, B1_0 + 1)
            dve.tensor_scalar(two(fg["f"][:, :]), halves(mm[1], HT, BH), bf[:, 0:1], None, ALU.add).then_inc(f_row, 1)
            dve.wait_ge(f_row, 1)
            dve.scalar_tensor_tensor(out=fg["abs"][:, :], in0=fg["f"][:, :], scalar=-1.0, in1=fg["f"][:, :],
                                     op0=ALU.mult, op1=ALU.max).then_inc(f_row, 1)
            dve.memset(fg["one"][:, :], 1.0).then_inc(f_row, 1)
            dve.wait_ge(fexp, 2)
            dve.scalar_tensor_tensor(out=fg["lf"][:, :], in0=fg["f"][:, :], scalar=0.0, in1=fg["l1"][:, :],
                                     op0=ALU.min, op1=ALU.subtract).then_inc(f_row, 1)
            dve.wait_ge(f_row, 4)
            dve.tensor_tensor_scan(fg["c"][:, :], fg["one"][:, :], fg["lf"][:, :], 0.0, ALU.mult, ALU.add).then_inc(f_row, 1)
            dve.wait_ge(f_row, 5)
            dve.tensor_scalar(fg["negc"][:, :], fg["c"][:, :], -1.0, None, ALU.mult).then_inc(f_row, 1)
            low_w(B1_0 + 2, B1_0 % 2)
            dve.wait_ge(negc_stored, 16)

            def softmax_in(p_, i):
                w = S_TILES[i + 1][0] + P
                s_ = SS[i % 2]
                out_, neg = s_[:, 0:w], negc_b[:, 0:w]
                if i < NT - 1:
                    ps, at = ((ax[0], 0), (ax[0], BANK), (ax[1], 0))[i]
                    src = ps[:, at:at + w]
                else:
                    out_, neg, src = two(out_), two(neg), halves(ax[0])
                dve.wait_ge(s4_done, p_ * NT + (i + 1))
                if i == 0:
                    dve.wait_ge(negc_loaded, p_ * 16 + 16)
                    dve.wait_ge(rq_scaled, p_ + 1)
                if i >= 2:
                    dve.wait_ge(pexp, p_ * NT + (i - 1))
                dve.scalar_tensor_tensor(out=out_, in0=src, scalar=rq[:, i:i + 1], in1=neg,
                                         op0=ALU.mult, op1=ALU.add).then_inc(sadd, 1)
                dve.wait_ge(sadd, p_ * NT + (i + 1))
                dve.tensor_tensor(s_[:, w - P:w], s_[:, w - P:w], causal_add[:, :], ALU.add).then_inc(smask, 1)
                dve.wait_ge(smask, p_ * NT + (i + 1))
                dve.reduce_max(s_max[:, i:i + 1], s_[:, 0:w], AX_X).then_inc(smax, 1)
                dve.wait_ge(smax, p_ * NT + (i + 1))
                dve.tensor_scalar(s_neg[:, i:i + 1], s_max[:, i:i + 1], -1.0, None, ALU.mult).then_inc(sneg, 1)

            def softmax_out(p_, i):
                w = S_TILES[i + 1][0] + P
                dve.wait_ge(pexp, p_ * NT + (i + 1))
                dve.reciprocal(s_inv[:, i:i + 1], s_sum[:, i:i + 1]).then_inc(sinv, 1)
                dve.wait_ge(sinv, p_ * NT + (i + 1))
                dve.tensor_scalar(PR[:, i, 0:w], PR[:, i, 0:w], s_inv[:, i:i + 1], None, ALU.mult).then_inc(pscaled, 1)

            def gate_y(p_):
                dve.wait_ge(pv4_done, p_ + 1)
                row = Y[:, ds(p_, 1), :].rearrange("p a n -> p (a n)")
                dve.scalar_tensor_tensor(out=row, in0=ax[1][:, BANK:BANK + SEQ], scalar=0.5, in1=row,
                                         op0=ALU.mult, op1=ALU.mult).then_inc(y4_ready, 1)

            def low_pt(p_, n):
                src, high, low = transposed_p(PT_ORDER[n])
                dve.wait_ge(pt_hi, p_ * (NT + 2) + (n + 1 + (n >= PT_ORDER.index(NT))))
                dve.tensor_tensor(low, src, high.bitcast(F32), ALU.subtract).then_inc(pt_lo, 1)

            def head_b1(h, proj, attend, p_):
                b = h * B1_PER + (B1_0 + 1)
                q0 = B1_0 + 1
                if attend:
                    for i in range(3):
                        softmax_in(p_, i)
                if proj:
                    low_w(b + 2, q0 % 2)
                if attend:
                    for i in range(3):
                        softmax_out(p_, i)
                    softmax_in(p_, 3)
                if proj:
                    low_w(b + 3, (q0 + 1) % 2)
                if attend:
                    softmax_out(p_, 3)
                    for n in range(NT + 1):
                        low_pt(p_, n)
                if proj:
                    low_w(b + 4, q0 % 2)
                if attend:
                    gate_y(p_)
                if proj:
                    dve.wait_ge(th4_ready, h + 1)
                    row = Y[:, ds(h, 1), :].rearrange("p a n -> p (a n)")
                    dve.scalar_tensor_tensor(out=row, in0=row, scalar=1.0, in1=mm[1][:, 0:SEQ],
                                             op0=ALU.add, op1=ALU.mult).then_inc(gate4_ready, 1)
                    dve.wait_ge(r4_ready, h * 2 + 1)
                    dve.scalar_tensor_tensor(out=KR[:, :], in0=KR[:, :], scalar=par[:, C_KN:C_KN + 1], in1=rstd[:, :],
                                             op0=ALU.mult, op1=ALU.mult).then_inc(hat_ready, 1)
                    dve.wait_ge(v4_hi, h * 3 + 3)
                    dve.tensor_tensor(Vl[:, :], ax[1][:, 0:NT * BD], Vh[:, :].bitcast(F32), ALU.subtract).then_inc(v4_lo, 1)
                    dve.tensor_tensor(Vm[M2, :], ax[0][M0, BANK:BANK + BD], Vm[M0, :].bitcast(F32),
                                      ALU.subtract).then_inc(v4_lo, 1)
                    dve.wait_ge(r4_ready, h * 2 + 2)
                    dve.tensor_scalar(rq[:, :], rq[:, :], float(BD) ** -0.5, None, ALU.mult).then_inc(rq_scaled, 1)
                    dve.wait_ge(hat_hi, h * 2 + 1)
                    dve.tensor_tensor(Kl[:, :], KR[:, :], Kh[:, :].bitcast(F32), ALU.subtract).then_inc(hat_lo, 1)
                    dve.wait_ge(hat_hi, h * 2 + 2)
                    dve.tensor_tensor(Ql[:, :], QR[:, :], Qh[:, :].bitcast(F32), ALU.subtract).then_inc(hat_lo, 1)
                    low_w(b + 5, (q0 + 1) % 2)

            head_b1(0, True, False, 0)
            with dve.Fori(1, BH) as h:
                head_b1(h, True, True, h - 1)

            xl_base = 4 * KT

            def low_y(tiles):
                for j in tiles:
                    low_x(Y[:, j, :], j, SEQ)

            low_y(range(0, 5))
            for i in range(3):
                softmax_in(BH - 1, i)
            for i in range(3):
                softmax_out(BH - 1, i)
            softmax_in(BH - 1, 3)
            low_y(range(5, 8))
            softmax_out(BH - 1, 3)
            low_pt(BH - 1, 0)
            low_y(range(8, 11))
            for n in range(1, NT + 1):
                low_pt(BH - 1, n)
            low_y(range(11, KT - 1))
            gate_y(BH - 1)
            low_y([KT - 1])
            dve.wait_ge(h_loaded2[0], 16)

            def add_b2(i, k, more=True):
                b = i * 2 + (B2_0 + k)
                dve.wait_ge(blk_done, b + 1)
                row = hT5[:, ds(i * 2 + k, 1), META:T].rearrange("p a n -> p (a n)")
                dve.tensor_tensor(row, row, mm[k][:, 0:SEQ], ALU.add).then_inc(h_acc, 1)
                if more:
                    low_w(b + 2, (B2_0 + k) % 2)

            def take_raw(i, k):
                dve.wait_ge(out_tr, i * 2 + (k + 1))
                dve.tensor_copy(o_nat[:, :, ds(i * (2 * P) + k * P, P)],
                                ax[1][:, k * BANK:(k + 1) * BANK].rearrange("p (a n) -> p a n", a=NT)).then_inc(raw_ready, 1)

            add_b2(0, 0)
            add_b2(0, 1)
            dve.wait_ge(h_loaded2[1], 16)
            with dve.Fori(1, KT // 2 - 1) as i:
                for k in range(2):
                    add_b2(i, k)
                    take_raw(i - 1, k)
            for k in range(2):
                add_b2(KT // 2 - 1, k, False)
                take_raw(KT // 2 - 2, k)
            for k in range(2):
                take_raw(KT // 2 - 1, k)
            dve.wait_ge(raw_ready, KT)
            dve.wait_ge(stat5_ready, 2)
            for i in range(0, NT, 2):
                dve.tensor_scalar(o_nat[:, i, :], o_nat[:, i, :], stat5[:, 1, i:i + 1], None, ALU.mult).then_inc(o_even, 1)

        @block.tensor
        def _(pe):
            ALL = ((0, 0, HT), (BANK, HT, HT))
            REAL = ((0, META, SEQ),)
            PACKED = ((0, 0, SEQ),)

            def three(ps, wh, wl, xh, xl, spans, first, last):
                for k, (w, v) in enumerate(((wh, xh), (wh, xl), (wl, xh))):
                    for at, t0, n in spans:
                        i = pe.matmul(ps[:, at:at + n], w, v[:, t0:t0 + n],
                                      start=first and k == 0, stop=last and k == 2)
                return i

            def block_tile(par_, ps, spans, k, fresh):
                if fresh is not None:
                    pe.wait_ge(xl_ready, fresh + k + 1)
                i = three(ps, w_hi[par_][:, k * P:(k + 1) * P], w_lo[par_][:, k * P:(k + 1) * P],
                          XH[:, k, :], XL[:, k, :], spans, k == 0, k == KT - 1)
                if k == KT - 1:
                    i.then_inc(blk_done, 1)

            BEHIND = 8

            def two_blocks(b, par_, ps, spans, fresh):
                for k in range(KT + BEHIND):
                    for a, j in enumerate((k, k - BEHIND)):
                        if j == 0:
                            pe.wait_ge(w_lo_ready, b + a + 1)
                        if 0 <= j < KT:
                            block_tile((par_ + a) % 2, ps[a], spans[a], j, fresh)

            def blockmm(b, par_, ps, spans=ALL, fresh=None):
                pe.wait_ge(w_lo_ready, b + 1)
                for k in range(KT):
                    block_tile(par_, ps, spans, k, fresh)

            def full_sum(ps, src, n, first=True, last=True):
                for a in range(2):
                    i = pe.matmul(ps[:, a * BANK:a * BANK + n], ones[:, :], src[:, a * n:(a + 1) * n],
                                  start=first, stop=last)
                return i

            pe.wait_ge(const_ready, 3)
            pe.wait_ge(meta_loaded, 16)
            for i in range(NT):
                pe.wait_ge(x_loaded[i], 16)
            LAG = 3
            for j in range(KT + LAG + BEHIND):
                if j == 2:
                    pe.wait_ge(par_loaded, 16 * 10)
                    for t, n in enumerate((P, P, NPAR - 2 * P)):
                        pe.transpose(mm[0][:, t * P:t * P + n], par_rows[0:n, t, :], ident[0:n, 0:n]).then_inc(par_tr, 1)
                    pe.wait_ge(diag0_ready, NT + 1)
                    pe.matmul(mm[1][:, X0:BANK], ones[0:META, :], diag0[0:META, NT, 0:META], start=True, stop=True)
                    pe.matmul(mm[1][:, BANK:2 * BANK], ones[:, :], flat(diag0[:, 0:NT, :]), start=True,
                              stop=True).then_inc(bcast0_done, 1)
                if j < KT:
                    if j >= 2:
                        pe.wait_ge(h_copied, j - 1)
                    ps = ax[j % 2]
                    pe.transpose(ps[:, X0:BANK], meta_nat[:, j * P:(j + 1) * P], ident[0:META, 0:META])
                    for i in range(NT):
                        t = pe.transpose(ps[:, BANK + i * P:BANK + (i + 1) * P], x_nat[:, i, j * P:(j + 1) * P], ident[:, :])
                    t.then_inc(x_tr, 1)
                if j >= LAG:
                    if j == LAG:
                        pe.wait_ge(par_ready, 1)
                        pe.wait_ge(rstd0_ready, 1)
                        pe.wait_ge(w_lo_ready, 1)
                    if j < KT + LAG:
                        block_tile(0, mm[0], ALL, j - LAG, 0)
                    if j == LAG + BEHIND:
                        pe.wait_ge(w_lo_ready, 2)
                    if j >= LAG + BEHIND:
                        block_tile(1, mm[1], ALL, j - LAG - BEHIND, 0)

            def xm_tile(h, c, par_):
                if isinstance(h, int) and h == 0:
                    pe.wait_ge(cv_aff, c - 1)
                else:
                    pe.wait_ge(cv_aff, h * CT + (c - 1))
                    if c == 1:
                        pe.wait_ge(gacc_ready, h + 1)
                blockmm(xm_block(h, c), par_, mm[c % 2])

            def qkv_tiles(h, par_):
                b = qkv_block(h)
                pe.wait_ge(w_lo_ready, b + 1)
                pe.wait_ge(xc_lo, h * CT + CT)
                first = isinstance(h, int) and h == 0
                NJ = 2 * QT + CT

                def gate(j):
                    pe.wait_ge(qkv_lo, h * NJ + (j + 1))
                    for a in range(2):
                        for k, g in enumerate((gh, gl)):
                            i = pe.matmul(mm[1][0:2 * NG, a * BANK:a * BANK + HT], wgp[:, j, :],
                                          g[j % 2][:, a * HT:(a + 1) * HT], start=j == 0 and k == 0, stop=j == NJ - 1 and k == 1)
                    i.then_inc(gate_mm, 1)

                for j in range(NJ):
                    if j == 2 * QT:
                        pe.wait_ge(w_lo_ready, b + 2)
                    if j < 2:
                        if not first:
                            pe.wait_ge(vn1_ev, h * NS)
                    else:
                        pe.wait_ge(qkv_hi, h * NJ + (j - 1))
                    p_ = par_ if j < 2 * QT else 1 - par_
                    col = j % (2 * QT) * P
                    xh, xl = (xch, xcl) if j < 2 * QT else (xmh, xml)
                    for k in range(CT):
                        at = k * CT * P + col
                        i = three(ax[j % 2], w_hi[p_][:, at:at + P], w_lo[p_][:, at:at + P],
                                  xh[:, k, :], xl[:, k, :], ALL, k == 0, k == CT - 1)
                    if j % (2 * QT) == 2 * QT - 1:
                        i.then_inc(qkv_mm, 1)
                        pe.wait_ge(qkv_mm, h * NJ + (j + 1))
                        pe.sem_inc(blk_done, 1)
                    else:
                        i.then_inc(qkv_mm, 1)
                    if j == 1:
                        pe.wait_ge(wg_lo, h + 1)
                    if j >= 1:
                        gate(j - 1)
                pe.wait_ge(qkv_hi, h * NJ + NJ)
                for i, (s, n) in enumerate(S_TILES):
                    if i == 2:
                        gate(NJ - 1)
                    if i >= 2:
                        pe.wait_ge(vn1_ev, h * NS + (i - 1))
                    for c in range(CT):
                        t = pe.transpose(ax[i % 2][0:n, c * P:(c + 1) * P], qkv[:, 2 * QT + c, s:s + n], ident[:, :])
                    t.then_inc(v_tr, 1)

            for c in range(2, CT):
                xm_tile(0, c, c % 2)

            def head_a1(h):
                xm_tile(h, 0, 0)
                qkv_tiles(h - 1, 1)
                for c in range(1, CT):
                    xm_tile(h, c, c % 2)

            head_a1(1)
            with pe.Fori(2, AH) as h:
                head_a1(h)
            pe.wait_ge(cv_aff, AH * CT - 1)
            blockmm(O0_BLOCK, 0, mm[0])
            qkv_tiles(AH - 1, 1)

            def three_f32r(ps, xh, xl, yh, yl, first, last):
                for k, (x_, y_) in enumerate(((xh, yh), (xh, yl), (xl, yh))):
                    i = pe.matmul(ps, x_, y_, start=first and k == 0, stop=last and k == 2)
                return i

            def gates():
                pe.wait_ge(gb_ready, 2)
                pe.wait_ge(vn1_ev, AH * NS)
                for g in range(2):
                    for a in range(2):
                        i = pe.matmul(ax[g][0:AH, a * BANK:a * BANK + HT], sel[:, g * AH:(g + 1) * AH],
                                      gacc[:, a * HT:(a + 1) * HT], start=True, stop=True)
                    i.then_inc(gsel_done, 1)

            def a_columns():
                pe.wait_ge(grow, 7)
                for i, (s, n) in enumerate(S_TILES):
                    t = pe.transpose(ax[0][0:n, i * AH:(i + 1) * AH], gr["a"][:, s:s + n], ident[0:AH, 0:AH])
                t.then_inc(a_tr, 1)

            def scores_a2(h, j):
                s, n = S_TILES[j]
                ps, at0 = SCORES_AT[j]
                if j == 0:
                    pe.wait_ge(qk_lo, h + 1)
                    wait(pe, rstd_ready, h)
                    wait(pe, g_ready, h * CT)
                if j == 3:
                    pe.wait_ge(w_ready, h * NS + 1)
                for at, t0, w in (ALL if j == 0 else ((at0, s, T - s),)):
                    for k in range(QT):
                        i = three_f32r(ps[0:n, at:at + w], qkh[:, QT + k, s:s + n], qkl[:, QT + k, s:s + n],
                                       qkh[:, k, t0:t0 + w], qkl[:, k, t0:t0 + w], k == 0, k == QT - 1)
                i.then_inc(sc_done, 1)

            def over_s(ps, meta, high, low):
                for j, (s, n) in enumerate(S_TILES):
                    for a in range(2):
                        lo, hi = max(s, a * HT), (a + 1) * HT
                        if lo >= hi:
                            continue
                        last = not any(max(s2, a * HT) < hi for s2, _ in S_TILES[j + 1:])
                        cols = slice(E_OFF[j] + lo - s, E_OFF[j] + hi - s)
                        if j == 0:
                            passes = [(meta, EWh[0:meta.shape[0], cols])]
                        else:
                            passes = [(high(j), EWh[:, cols]), (high(j), EWl[:, cols])]
                            if low:
                                passes.append((low(j), EWh[:, cols]))
                        for k, (v, w) in enumerate(passes):
                            i = pe.matmul(ps[:, a * BANK + lo - a * HT:a * BANK + HT], v, w,
                                          start=j == 0 and k == 0, stop=last and k == len(passes) - 1)
                i.then_inc(pv_done, 1)

            def head_a2(h, first=False):
                b = h * A2_PER + A2_0
                for c in range(CT):
                    if c < 2:
                        if first:
                            pe.wait_ge(gacc_ready, AH + 1)
                        else:
                            pe.wait_ge(gate2_ready, h * CT + (c - 1))
                    else:
                        pe.wait_ge(ot_ready, h * CT + (c - 1))
                    if not (first and c == 0):
                        blockmm(b + c, c % 2, mm[c % 2])
                    if first and c == 0:
                        gates()
                    if first and c == 1:
                        a_columns()
                    if c == (2 if first else 0):
                        if first:
                            pe.wait_ge(grow, 12)
                        for j in range(3):
                            scores_a2(h, j)
                    if c == (3 if first else 1):
                        for j in range(3, NS):
                            scores_a2(h, j)
                    if c == (3 if first else 2):
                        pe.wait_ge(w2_lo, h * NS + NS)
                        over_s(ax[1], ones_r[0:32 + META, :], lambda j: ones_r[:, :], None)
                pe.wait_ge(v_lo, h * 2 + 2)
                for c in range(CT):
                    if c == 1:
                        pe.wait_ge(dn_ready, h * 2 + 2)
                    if c > 1:
                        pe.wait_ge(g_ready, h * CT + (c - 1))
                    cols = slice(c * P, (c + 1) * P)
                    over_s(ax[c % 2], vh[0:MROWS, 0, cols], lambda j: vh[:, j, cols], lambda j: vl[:, j, cols])
                for c in range(CT):
                    k = CT + c
                    if c < 2:
                        pe.wait_ge(ot_ready, h * CT + (c + 3))
                    else:
                        pe.wait_ge(gate2_ready, h * CT + (c - 1))
                    blockmm(b + k, k % 2, mm[k % 2])
                    if c == 0:
                        pe.wait_ge(g_ready, h * CT + CT)
                        pe.wait_ge(ss2_ready, h * (CT - 1) + (CT - 1))
                        full_sum(ax[0], rtmp, HT).then_inc(sumg_done, 1)

            head_a2(0, True)
            with pe.Fori(1, AH) as h:
                head_a2(h)

            def out_blocks(b0, acc0, spans, fresh, mm1_free):
                for k in range(2):
                    if k:
                        pe.wait_ge(*mm1_free)
                    blockmm(b0 + k, (b0 + k) % 2, mm[k], spans, fresh if k == 0 else None)
                with pe.Fori(1, KT // 2) as i:
                    for k in range(2):
                        pe.wait_ge(h_acc, i * 2 + (acc0 + k - 1))
                        blockmm(i * 2 + (b0 + k), (b0 + k) % 2, mm[k], spans)

            pe.wait_ge(gate2_ready, AH * CT - 1)
            out_blocks(A3_0, 0, ALL, KT, (gate2_ready, AH * CT))
            pe.wait_ge(h_acc, KT - 1)
            out_blocks(A3_0 + KT, KT, ALL, 2 * KT, (h_acc, KT))
            pe.wait_ge(ss_ready, KT + 2)
            full_sum(ax[0], rtmp, HT).then_inc(sumsq_done, 1)

            pe.wait_ge(h_acc, 2 * KT)
            two_blocks(B1_0, B1_0 % 2, (mm[1], mm[0]), (ALL, REAL), 3 * KT)

            def scores(p_, i):
                w = S_TILES[i + 1][0] + P
                q, ql = Qh[:, i * P:(i + 1) * P], Ql[:, i * P:(i + 1) * P]
                if i < 3:
                    at = (ax[0][:, 0:w], ax[0][:, BANK:BANK + w], ax[1][:, 0:w])[i]
                    m = three_f32r(at, q, ql, Kh[:, 0:w], Kl[:, 0:w], True, True)
                else:
                    for at, t0, n in ALL:
                        m = three_f32r(ax[0][:, at:at + n], q, ql, Kh[:, t0:t0 + n], Kl[:, t0:t0 + n], True, True)
                m.then_inc(s4_done, 1)

            def transpose_p(p_, n):
                i = PT_ORDER[n]
                if n == NT:
                    pe.wait_ge(pt_lo, p_ * (NT + 1) + 2)
                pe.wait_ge(pscaled, p_ * NT + (min(i, NT - 1) + 1))
                at = ax[0][0:META, :] if i == NT else ax[1][:, 0 if i % 2 else BANK:]
                for j in range(NT if i == NT else i + 1):
                    if i == NT:
                        src = PR[:, j, 0:META]
                    else:
                        s = S_TILES[j + 1][0]
                        src = PR[:, i, s:s + P]
                    t = pe.transpose(at[:, j * P:(j + 1) * P], src, ident[:, :])
                t.then_inc(ptr_done, 1)

            def probs_v(p_):
                pe.wait_ge(pt_lo, p_ * (NT + 1) + (NT + 1))
                o = ax[1][:, BANK:BANK + SEQ]
                pe.matmul(o, Vm[:, :], PM[:, :], start=True, stop=False)
                for j in range(NT):
                    v = slice(j * BD, (j + 1) * BD)
                    ph, pl = (flat(t[:, 4 * j:3 * j + NT, :]) for t in (PTh, PTl))
                    m = three_f32r(o[:, j * P:], Vh[:, v], Vl[:, v], ph, pl, False, j == NT - 1)
                m.then_inc(pv4_done, 1)

            def head_b1(h, proj, attend, p_, first=False):
                b = h * B1_PER + (B1_0 + 1)
                q0 = B1_0 + 1
                if proj and not first:
                    pe.wait_ge(ln4_ready, h * 2 - 1)
                    blockmm(b, q0 % 2, mm[0], REAL)
                if attend:
                    pe.wait_ge(hat_lo, p_ * 2 + 2)
                    pe.wait_ge(v4_lo, p_ * 2 + 2)
                    pe.wait_ge(ln4_ready, p_ * 2 + 2)
                    for i in range(3):
                        scores(p_, i)
                if proj:
                    if first:
                        pe.wait_ge(f_row, 1)
                    else:
                        pe.wait_ge(gate4_ready, h)
                    blockmm(b + 1, (q0 + 1) % 2, mm[1])
                if attend:
                    pe.wait_ge(sadd, p_ * NT + 2)
                    scores(p_, 3)
                    transpose_p(p_, 0)
                if proj:
                    pe.wait_ge(sq4_ready, h * 2 + 1)
                    blockmm(b + 2, q0 % 2, mm[0])
                if attend:
                    pe.wait_ge(sadd, p_ * NT + 4)
                    transpose_p(p_, 1)
                    pe.wait_ge(pt_lo, p_ * (NT + 1) + 1)
                    for n in range(2, NT + 1):
                        transpose_p(p_, n)
                if proj:
                    pe.wait_ge(sq4_ready, h * 2 + 2)
                    blockmm(b + 3, (q0 + 1) % 2, mm[1], REAL)
                    pe.wait_ge(qkv4_ev, h * 3 + 3)
                    full_sum(mm[0], sq[1], HT).then_inc(sum4_done, 1)
                    if attend:
                        pe.wait_ge(pt_lo, p_ * (NT + 1) + (NT + 1))
                    for a in range(NT):
                        m = pe.matmul(ax[0][:, a:a + 1], sq[0][:, a * P:(a + 1) * P], ones[:, 0:1], start=True, stop=True)
                    m.then_inc(sum4_done, 1)
                if attend:
                    probs_v(p_)
                if proj:
                    for j in range(NT):
                        s = S_TILES[j + 1][0]
                        t = pe.transpose(ax[1][:, j * P:(j + 1) * P], VT[:, s:s + P], ident[:, :])
                    t.then_inc(vtr4, 1)
                    pe.transpose(ax[0][0:META, BANK:BANK + P], VT[:, 0:META], ident[:, :]).then_inc(vtr4, 1)

            head_b1(0, True, False, 0, True)
            with pe.Fori(1, BH) as h:
                head_b1(h, True, True, h - 1)

            def last_head_and_y(p_):
                def y_tiles(k, tiles):
                    for j in tiles:
                        block_tile((B2_0 + k) % 2, mm[k], PACKED, j, 4 * KT)

                pe.wait_ge(hat_lo, p_ * 2 + 2)
                pe.wait_ge(v4_lo, p_ * 2 + 2)
                pe.wait_ge(ln4_ready, p_ * 2 + 2)
                for i in range(3):
                    scores(p_, i)
                pe.wait_ge(w_lo_ready, B2_0 + 2)
                pe.wait_ge(gate4_ready, BH)
                for k in range(2):
                    y_tiles(k, range(0, 5))
                pe.wait_ge(sadd, p_ * NT + 2)
                scores(p_, 3)
                transpose_p(p_, 0)
                y_tiles(0, range(5, 10))
                y_tiles(1, range(5, 8))
                pe.wait_ge(sadd, p_ * NT + 4)
                transpose_p(p_, 1)
                pe.wait_ge(pt_lo, p_ * (NT + 1) + 1)
                for n in range(2, NT + 1):
                    transpose_p(p_, n)
                y_tiles(1, range(8, 11))
                probs_v(p_)
                y_tiles(0, range(10, KT))
                y_tiles(1, range(11, KT))

            last_head_and_y(BH - 1)

            def transpose_h(i, k):
                pe.wait_ge(hg_ready, i * 2 + (k + 1))
                if not (isinstance(i, int) and i == 0):
                    pe.wait_ge(raw_ready, i * 2 + (k - 1))
                for a in range(NT):
                    t = pe.transpose(ax[1][:, k * BANK + a * P:k * BANK + (a + 1) * P], hg[k][:, a * P:(a + 1) * P], ident[:, :])
                t.then_inc(out_tr, 1)

            pe.wait_ge(h_acc, 2 * KT + 1)
            blockmm(B2_0 + 2, B2_0 % 2, mm[0], PACKED)
            for k in range(2):
                transpose_h(0, k)
            pe.wait_ge(h_acc, 2 * KT + 2)
            blockmm(B2_0 + 3, (B2_0 + 1) % 2, mm[1], PACKED)
            with pe.Fori(2, KT // 2) as i:
                for k in range(2):
                    pe.wait_ge(h_acc, i * 2 + (2 * KT + k - 1))
                    blockmm(i * 2 + (B2_0 + k), (B2_0 + k) % 2, mm[k], PACKED)
                    transpose_h(i - 1, k)
            for k in range(2):
                transpose_h(KT // 2 - 1, k)
            pe.wait_ge(ss_ready, 2 * (KT + 2))
            for a in range(NT):
                i = pe.matmul(ax[0][:, a:a + 1], rtmp[:, a * P:(a + 1) * P], ones[:, 0:1], start=True, stop=True)
            i.then_inc(sumsq_done, 1)


_INS = ['x', 'meta_tokens', 'a_norm', 'a_w_in', 'a_conv_w', 'a_conv_b', 'a_w_q', 'a_w_k', 'a_w_v', 'a_w_gate',
        'a_b_gate', 'a_head_norm', 'a_skip', 'a_w_out', 'b_norm', 'b_w_in', 'b_b_f', 'b_q_norm', 'b_k_norm',
        'b_w_out', 'final_norm']


def kernel(**inputs):
    import numpy as _np
    import concourse.bacc as _bacc
    from concourse import mybir as _mybir
    from concourse.bass_utils import run_bass_kernel_spmd as _run

    nc = _bacc.Bacc("TRN2", target_bir_lowering=False, num_devices=1)
    arrays, args = {}, []
    for name in _INS:
        a = _np.ascontiguousarray(inputs[name])
        arrays[f"in_{name}_dram"] = a
        args.append(nc.dram_tensor(f"in_{name}_dram", a.shape, _mybir.dt.from_np(a.dtype), kind="ExternalInput").ap())
    shape = tuple(inputs["x"].shape)
    args.append(nc.dram_tensor("out_0_dram", shape, _mybir.dt.from_np(_np.dtype("float32")), kind="ExternalOutput").ap())
    hybrid_trunk(nc, *args)
    r = _run(nc, [arrays], core_ids=[0])
    return r.results[0]["out_0_dram"]
```
